# Optimizing a Trainium2 kernel written in Bass

```python
import math
import jax, jax.numpy as jnp
from jax import lax
import numpy as np

D_MODEL = 1024
BATCH = 1
SEQ = 1024
DEPTH = 1

N_MEM = 256
D_MIX = D_MODEL
POOL_WIDTH = D_MIX // 4
POOL_WINDOWS = (2, 4, 8, 16)
POOL_GROUP = POOL_WIDTH // 4
CONV_WIDTH = D_MIX // 4
CONV_KSIZE = 31
NSA_WIDTH = D_MIX - POOL_WIDTH - CONV_WIDTH
HEAD_DIM = 64
N_HEADS = NSA_WIDTH // HEAD_DIM
N_KV = 2
Q_PER_KV = N_HEADS // N_KV
KV_WIDTH = N_KV * HEAD_DIM
CMP_LEN = 32
CMP_STRIDE = 16
CMP_HIDDEN = 256
SEL_BLOCK = 64
N_SELECT = 16
WINDOW = 512
Q_BLOCK = 128
N_BRANCH = 3
N_BUCKETS = 32
MAX_EXACT = 16
MAX_DISTANCE = 128
XA_HEADS = 4
XA_HEAD_DIM = D_MODEL // XA_HEADS
D_FF = 4 * D_MODEL
EPS = 1e-6
NEG_INF = -1e30
FORCE = 1e30
IN_SPLITS = (POOL_WIDTH, 2 * CONV_WIDTH, NSA_WIDTH, 6 * KV_WIDTH, N_HEADS * N_BRANCH)
D_IN = POOL_WIDTH + 2 * CONV_WIDTH + NSA_WIDTH + 6 * KV_WIDTH + N_HEADS * N_BRANCH

kernel_name = 'hybrid_pool_conformer_nsa_decoder'

def rms_norm(x, g):
    xf = x.astype(jnp.float32)
    y = xf * lax.rsqrt(jnp.mean(xf * xf, axis=-1, keepdims=True) + EPS)
    return (y * g.astype(jnp.float32)).astype(x.dtype)

def layer_norm(x, g, b):
    xf = x.astype(jnp.float32)
    mu = jnp.mean(xf, axis=-1, keepdims=True)
    var = jnp.mean(jnp.square(xf - mu), axis=-1, keepdims=True)
    y = (xf - mu) * lax.rsqrt(var + EPS) * g.astype(jnp.float32) + b.astype(jnp.float32)
    return y.astype(x.dtype)

def masked_softmax(logits, mask):
    p = jax.nn.softmax(jnp.where(mask, logits, NEG_INF), axis=-1)
    return jnp.where(mask, p, 0.0)

def rel_bucket(dist):
    n = jnp.maximum(dist, 0)
    nf = jnp.maximum(n, 1).astype(jnp.float32)
    large = MAX_EXACT + (jnp.log(nf / MAX_EXACT) / math.log(MAX_DISTANCE / MAX_EXACT)
                         * (N_BUCKETS - MAX_EXACT)).astype(jnp.int32)
    return jnp.where(n < MAX_EXACT, n, jnp.minimum(large, N_BUCKETS - 1))

def pool_mixer(u, w, scale):
    S = u.shape[1]
    uf = u.astype(jnp.float32)
    csum = jnp.cumsum(uf, axis=1)
    t1 = jnp.arange(1, S + 1, dtype=jnp.float32)
    outs = []
    for g, win in enumerate(POOL_WINDOWS):
        sl = slice(g * POOL_GROUP, (g + 1) * POOL_GROUP)
        cg = csum[..., sl]
        prev = jnp.pad(cg, ((0, 0), (win, 0), (0, 0)))[:, :S]
        mean = (cg - prev) / jnp.minimum(t1, win)[None, :, None]
        outs.append((mean - uf[..., sl]).astype(u.dtype) @ w[g])
    return jnp.concatenate(outs, axis=-1) * scale

def conv_mixer(u, conv_w, conv_b, ln_g, ln_b, pw):
    a, gate = jnp.split(u, 2, axis=-1)
    h = a * jax.nn.sigmoid(gate)
    h = lax.conv_general_dilated(
        h, conv_w[:, None, :], window_strides=(1,), padding=[(CONV_KSIZE - 1, 0)],
        dimension_numbers=('NWC', 'WIO', 'NWC'), feature_group_count=CONV_WIDTH) + conv_b
    h = jax.nn.silu(layer_norm(h, ln_g, ln_b))
    return h @ pw

def compress(kv, pos, w1, w2):
    B, S = kv.shape[0], kv.shape[1]
    nc = (S - CMP_LEN) // CMP_STRIDE + 1
    idx = jnp.arange(nc)[:, None] * CMP_STRIDE + jnp.arange(CMP_LEN)[None, :]
    blocks = kv[:, idx] + pos[None, None, :, None, :]
    flat = blocks.transpose(0, 1, 3, 2, 4).reshape(B, nc, N_KV, CMP_LEN * HEAD_DIM)
    return jax.nn.gelu(flat @ w1) @ w2

def nsa_mixer(q, k_c, v_c, k_s, v_s, k_w, v_w, gates, rel_bias,
              ck_pos, ck_w1, ck_w2, cv_pos, cv_w1, cv_w2):
    B, S = q.shape[0], q.shape[1]
    q = q.reshape(B, S, N_KV, Q_PER_KV, HEAD_DIM) * HEAD_DIM ** -0.5
    gates = gates.reshape(B, S, N_KV, Q_PER_KV, N_BRANCH)
    kc = compress(k_c, ck_pos, ck_w1, ck_w2)
    vc = compress(v_c, cv_pos, cv_w1, cv_w2)
    nc = kc.shape[1]
    n_sel = S // SEL_BLOCK
    top = min(N_SELECT, n_sel)
    ks_blocks = k_s.reshape(B, n_sel, SEL_BLOCK, N_KV, HEAD_DIM).transpose(0, 3, 1, 2, 4)
    vs_blocks = v_s.reshape(B, n_sel, SEL_BLOCK, N_KV, HEAD_DIM).transpose(0, 3, 1, 2, 4)
    kw_pad = jnp.pad(k_w, ((0, 0), (WINDOW, 0), (0, 0), (0, 0)))
    vw_pad = jnp.pad(v_w, ((0, 0), (WINDOW, 0), (0, 0), (0, 0)))
    c_start = jnp.arange(nc) * CMP_STRIDE
    c_end = c_start + CMP_LEN - 1
    s_idx = jnp.arange(n_sel)
    s_start = s_idx * SEL_BLOCK
    overlap = ((c_start[:, None] < s_start[None, :] + SEL_BLOCK)
               & (c_start[:, None] + CMP_LEN > s_start[None, :])).astype(jnp.float32)
    bias_tab = rel_bias.astype(jnp.float32).reshape(N_BUCKETS, N_KV, Q_PER_KV)
    b_ix = jnp.arange(B)[:, None, None, None]
    g_ix = jnp.arange(N_KV)[None, None, :, None]

    def block(i):
        s0 = i * Q_BLOCK
        t = s0 + jnp.arange(Q_BLOCK)
        qb = lax.dynamic_slice_in_dim(q, s0, Q_BLOCK, axis=1)
        gb = lax.dynamic_slice_in_dim(gates, s0, Q_BLOCK, axis=1)
        dist_c = t[:, None] - c_end[None, :]
        lc = (jnp.einsum('bqgrd,bcgd->bqgrc', qb, kc).astype(jnp.float32)
              + bias_tab[rel_bucket(dist_c)].transpose(0, 2, 3, 1)[None])
        pc = masked_softmax(lc, (dist_c >= 0)[:, None, None, :])
        oc = jnp.einsum('bqgrc,bcgd->bqgrd', pc.astype(vc.dtype), vc)
        imp = jnp.einsum('bqgrc,cj->bqgj', pc, overlap)
        cur = t // SEL_BLOCK
        forced = ((s_idx[None, :] == 0) | (s_idx[None, :] == cur[:, None])
                  | (s_idx[None, :] == cur[:, None] - 1))
        causal_s = s_start[None, :] <= t[:, None]
        score = jnp.where(forced[None, :, None, :], FORCE,
                          jnp.where(causal_s[None, :, None, :], imp, NEG_INF))
        _, idx = lax.top_k(score, top)
        ks_g = ks_blocks[b_ix, g_ix, idx].reshape(B, Q_BLOCK, N_KV, top * SEL_BLOCK, HEAD_DIM)
        vs_g = vs_blocks[b_ix, g_ix, idx].reshape(B, Q_BLOCK, N_KV, top * SEL_BLOCK, HEAD_DIM)
        pos_s = (idx[..., None] * SEL_BLOCK + jnp.arange(SEL_BLOCK)).reshape(
            B, Q_BLOCK, N_KV, top * SEL_BLOCK)
        dist_s = t[None, :, None, None] - pos_s
        bias_s = bias_tab[rel_bucket(dist_s), g_ix].transpose(0, 1, 2, 4, 3)
        ls = jnp.einsum('bqgrd,bqgld->bqgrl', qb, ks_g).astype(jnp.float32) + bias_s
        ps = masked_softmax(ls, (dist_s >= 0)[:, :, :, None, :])
        osl = jnp.einsum('bqgrl,bqgld->bqgrd', ps.astype(vs_g.dtype), vs_g)
        kwb = lax.dynamic_slice_in_dim(kw_pad, s0, WINDOW + Q_BLOCK, axis=1)
        vwb = lax.dynamic_slice_in_dim(vw_pad, s0, WINDOW + Q_BLOCK, axis=1)
        pos_w = s0 - WINDOW + jnp.arange(WINDOW + Q_BLOCK)
        dist_w = t[:, None] - pos_w[None, :]
        mask_w = (dist_w >= 0) & (dist_w < WINDOW) & (pos_w[None, :] >= 0)
        lw = (jnp.einsum('bqgrd,bkgd->bqgrk', qb, kwb).astype(jnp.float32)
              + bias_tab[rel_bucket(dist_w)].transpose(0, 2, 3, 1)[None])
        pw = masked_softmax(lw, mask_w[:, None, None, :])
        ow = jnp.einsum('bqgrk,bkgd->bqgrd', pw.astype(vwb.dtype), vwb)
        return gb[..., 0:1] * oc + gb[..., 1:2] * osl + gb[..., 2:3] * ow

    out = lax.map(block, jnp.arange(S // Q_BLOCK))
    return out.transpose(1, 0, 2, 3, 4, 5).reshape(B, S, NSA_WIDTH)

def setup_inputs(seed: int = 0) -> dict:
    key = jax.random.key(seed)
    ks = jax.random.split(key, 40)
    f32 = jnp.float32
    L = DEPTH

    def nrm(k, shape, fan_in):
        return jax.random.normal(k, shape, f32) * fan_in ** -0.5

    def gain(k, shape):
        return 1.0 + 0.05 * jax.random.normal(k, shape, f32)

    def small(k, shape):
        return 0.02 * jax.random.normal(k, shape, f32)

    return {
        'x': jax.random.normal(ks[0], (BATCH, SEQ, D_MODEL), f32),
        'mem': jax.random.normal(ks[1], (BATCH, N_MEM, D_MODEL), f32),
        'rel_bias': 0.5 * jax.random.normal(ks[2], (N_BUCKETS, N_HEADS), f32),
        'mix_pre_g': gain(ks[3], (L, D_MODEL)),
        'mix_post_g': gain(ks[4], (L, D_MODEL)),
        'w_in': nrm(ks[5], (L, D_MODEL, D_IN), D_MODEL),
        'pool_w': nrm(ks[6], (L, len(POOL_WINDOWS), POOL_GROUP, POOL_GROUP), POOL_GROUP),
        'pool_scale': gain(ks[7], (L, POOL_WIDTH)),
        'conv_w': nrm(ks[8], (L, CONV_KSIZE, CONV_WIDTH), CONV_KSIZE),
        'conv_b': small(ks[9], (L, CONV_WIDTH)),
        'conv_ln_g': gain(ks[10], (L, CONV_WIDTH)),
        'conv_ln_b': small(ks[11], (L, CONV_WIDTH)),
        'conv_pw': nrm(ks[12], (L, CONV_WIDTH, CONV_WIDTH), CONV_WIDTH),
        'cmp_k_pos': small(ks[13], (L, CMP_LEN, HEAD_DIM)),
        'cmp_k_w1': nrm(ks[14], (L, CMP_LEN * HEAD_DIM, CMP_HIDDEN), CMP_LEN * HEAD_DIM),
        'cmp_k_w2': nrm(ks[15], (L, CMP_HIDDEN, HEAD_DIM), CMP_HIDDEN),
        'cmp_v_pos': small(ks[16], (L, CMP_LEN, HEAD_DIM)),
        'cmp_v_w1': nrm(ks[17], (L, CMP_LEN * HEAD_DIM, CMP_HIDDEN), CMP_LEN * HEAD_DIM),
        'cmp_v_w2': nrm(ks[18], (L, CMP_HIDDEN, HEAD_DIM), CMP_HIDDEN),
        'w_out': nrm(ks[19], (L, D_MIX, D_MODEL), D_MIX),
        'xa_pre_g': gain(ks[20], (L, D_MODEL)),
        'xa_post_g': gain(ks[21], (L, D_MODEL)),
        'mem_g': gain(ks[22], (L, D_MODEL)),
        'xa_wq': nrm(ks[23], (L, D_MODEL, D_MODEL), D_MODEL),
        'xa_wk': nrm(ks[24], (L, D_MODEL, D_MODEL), D_MODEL),
        'xa_wv': nrm(ks[25], (L, D_MODEL, D_MODEL), D_MODEL),
        'xa_wo': nrm(ks[26], (L, D_MODEL, D_MODEL), D_MODEL),
        'mlp_pre_g': gain(ks[27], (L, D_MODEL)),
        'mlp_post_g': gain(ks[28], (L, D_MODEL)),
        'mlp_w1': nrm(ks[29], (L, D_MODEL, D_FF), D_MODEL),
        'mlp_w2': nrm(ks[30], (L, D_FF, D_MODEL), D_FF),
    }

def reference(x, mem, rel_bias, mix_pre_g, mix_post_g, w_in, pool_w, pool_scale,
              conv_w, conv_b, conv_ln_g, conv_ln_b, conv_pw,
              cmp_k_pos, cmp_k_w1, cmp_k_w2, cmp_v_pos, cmp_v_w1, cmp_v_w2, w_out,
              xa_pre_g, xa_post_g, mem_g, xa_wq, xa_wk, xa_wv, xa_wo,
              mlp_pre_g, mlp_post_g, mlp_w1, mlp_w2):
    B, S = x.shape[0], x.shape[1]
    M = mem.shape[1]
    offsets = [int(o) for o in np.cumsum(IN_SPLITS)[:-1]]
    for l in range(DEPTH):
        h = rms_norm(x, mix_pre_g[l])
        proj = h @ w_in[l]
        u_pool, u_conv, q, kv, gate_logits = jnp.split(proj, offsets, axis=-1)
        k_c, v_c, k_s, v_s, k_w, v_w = [a.reshape(B, S, N_KV, HEAD_DIM)
                                        for a in jnp.split(kv, 6, axis=-1)]
        y_pool = pool_mixer(u_pool, pool_w[l], pool_scale[l])
        y_conv = conv_mixer(u_conv, conv_w[l], conv_b[l], conv_ln_g[l],
                            conv_ln_b[l], conv_pw[l])
        y_nsa = nsa_mixer(q, k_c, v_c, k_s, v_s, k_w, v_w, jax.nn.sigmoid(gate_logits), rel_bias,
                          cmp_k_pos[l], cmp_k_w1[l], cmp_k_w2[l],
                          cmp_v_pos[l], cmp_v_w1[l], cmp_v_w2[l])
        mix = jnp.concatenate([y_pool, y_conv, y_nsa], axis=-1) @ w_out[l]
        x = x + rms_norm(mix, mix_post_g[l])
        h = rms_norm(x, xa_pre_g[l])
        m = rms_norm(mem, mem_g[l])
        qx = (h @ xa_wq[l]).reshape(B, S, XA_HEADS, XA_HEAD_DIM) * XA_HEAD_DIM ** -0.5
        km = (m @ xa_wk[l]).reshape(B, M, XA_HEADS, XA_HEAD_DIM)
        vm = (m @ xa_wv[l]).reshape(B, M, XA_HEADS, XA_HEAD_DIM)
        p = jax.nn.softmax(jnp.einsum('bshd,bmhd->bhsm', qx, km).astype(jnp.float32), axis=-1)
        o = jnp.einsum('bhsm,bmhd->bshd', p.astype(vm.dtype), vm).reshape(B, S, D_MODEL)
        x = x + rms_norm(o @ xa_wo[l], xa_post_g[l])
        h = rms_norm(x, mlp_pre_g[l])
        y = jnp.square(jax.nn.relu(h @ mlp_w1[l])) @ mlp_w2[l]
        x = x + rms_norm(y, mlp_post_g[l])
    return x


_drawn_inputs = setup_inputs


def setup_inputs(seed=0):
    import zlib

    import numpy as np

    out = dict(_drawn_inputs(seed))
    spreads = {}
    factors = {'conv_b': 3.48, 'conv_ln_b': 6.754, 'cmp_k_pos': 64.0, 'cmp_v_pos': 8.0}
    for name, (base, spread) in spreads.items():
        noise = np.random.default_rng([zlib.crc32(name.encode()), seed]).standard_normal(out[name].shape)
        drawn = base * np.exp(spread * noise) if base else spread * noise
        out[name] = __import__('jax').numpy.asarray(drawn.astype(out[name].dtype))
    for name, factor in factors.items():
        out[name] = (out[name] * factor).astype(out[name].dtype)
    return out
```

```python
import math
import numpy as np
import concourse.bass as bass
from concourse import mybir

F32 = mybir.dt.float32
F32R = mybir.dt.float32r
BF16 = mybir.dt.bfloat16
ALU = mybir.AluOpType
ACT = mybir.ActivationFunctionType
AX = mybir.AxisListType

P = 128
SEQ, D = 1024, 1024
NT, KC = SEQ // P, D // P
MEM = 256
MT = MEM // P
HALF = 512
HD = 64
NH, NKV, QPK = 8, 2, 4
NCMP, CMP_STRIDE, CMP_LEN = 63, 16, 32
CPAD = 64
WIN_TILES = 512 // P
NEAR = 2 * P
TAPS = 31
CMP_HID = 256
XH = 4
FF = 4096
GROUP = 4
NGROUP = FF // P // GROUP
NBUCKET, MAX_EXACT, MAX_DIST = 32, 16, 128
NEG = -1e30
EPS = 1e-6
DMIN = -(CMP_STRIDE * (CPAD - 1) + CMP_LEN - 1)
ND = 992 - DMIN + 1
ZC = 120
OHR = 97

SM = {}
_at = 0
for _n, _w in (("conv_w", 2 * TAPS), ("conv_b", 2), ("ln_g", 2), ("ln_b", 2), ("pool_scale", 2),
               ("pos_k", 16), ("pos_v", 16), ("inv_win", 2), ("inv16", 32), ("valid", 1), ("eps", 1)):
    SM[_n] = (_at, _at + _w)
    _at += _w
SMW = _at

T_MEM = [("wk", m) for m in range(8)] + [("wv", m) for m in range(8)]
T_IN = [("in", m) for m in (13, 15, 0, 1, 2, 4, 3, 5, 10, 11, 12, 14, 6, 7, 8, 9)]
T_Q = [("wq", m) for m in range(8)]
PIECES = T_MEM + T_IN + [("wout", k) for k in range(8)] + T_Q + [("wo", k) for k in range(8)]
N_IN = len(T_MEM)
N_OUT = N_IN + len(T_IN)
N_Q = N_OUT + 8
N_O = N_Q + 8
N_MLP = N_O + 8
J_Q = len(T_MEM) + len(T_IN)
J_MLP = J_Q + 8


POOL_STEPS = 24


def hybrid_layer(nc, a):
    def at(name, shape, dt, kb):
        return nc.alloc_sbuf_tensor_at(name, shape, dt, offset=BASE + int(kb * 1024))

    BASE = -(-nc.sbuf_base // 32) * 32
    hT_h = at("hT_h", [P, KC, SEQ], F32R, 0)
    hT_l = at("hT_l", [P, KC, SEQ], F32R, 32)
    cw1 = [at("cw1_k", [P, 16, CMP_HID], F32, 16), at("cw1_v", [P, 16, CMP_HID], F32, 48)]
    x_in = [at(f"x_in{s}", [P, D], F32, 64 + 4 * s) for s in range(2)]
    hn0 = [at(f"hn0{s}", [P, D], F32, 72 + 4 * s) for s in range(2)]
    gain_x = at("gain_x", [P, D], F32, 80)
    gain_m = at("gain_m", [P, D], F32, 84)
    mT_h = at("mT_h", [P, KC, MEM], F32R, 88)
    mT_l = at("mT_l", [P, KC, MEM], F32R, 96)
    km0 = at("km0", [P, KC, MEM], F32, 104)
    vm0 = at("vm0", [P, MT, D], F32, 112)
    junk0 = at("junk0", [P, D], F32, 120)
    pool_a = at("pool_a", [P, SEQ], F32, 64)
    pool_b = at("pool_b", [P, SEQ], F32, 68)
    sig = at("sig", [P, SEQ], F32, 72)
    q_st = at("q_st", [P, NH, SEQ], F32R, 64)
    k_h = at("k_h", [P, 2, NKV, SEQ], F32R, 96)
    k_l = at("k_l", [P, 2, NKV, SEQ], F32R, 112)
    v_sw = at("v_sw", [P, NT, 2, P], F32, 128)
    c_st = [at("kc_st", [P, NKV, SEQ], F32, 136), at("vc_st", [P, NKV, SEQ], F32, 144)]
    pu = at("pu", [P, 2, SEQ], F32, 152)
    ch = at("ch", [P, 2, SEQ], F32, 160)
    ca = at("ca", [P, 2, SEQ], F32, 168)
    cm = [at("cm_k", [P, 16, NKV, NCMP], F32, 184), at("cm_v", [P, 16, NKV, NCMP], F32, 192)]
    ctmp = at("ctmp", [P, SEQ], F32, 176)
    cln = at("cln", [P, SEQ], F32, 180)
    tn = at("tn", [P, NH, NEAR], F32, 136)
    tc = at("tc", [P, NH, ZC], F32, 144)
    wm = at("wm", [P, 3 * P], F32, 190)
    p_sel = at("p_sel", [P, QPK, SEQ], F32, 148)
    p_win = at("p_win", [P, QPK, 5 * P + CPAD], F32, 164)
    pt = at("pt", [P, 2, HALF], F32, 184)
    wb_h = at("wb_h", [P, KC, D], F32R, 64)
    wb_l = at("wb_l", [P, KC, D], F32R, 96)
    upd = [at(f"upd{s}", [P, D], F32, 128 + 4 * s) for s in range(2)]
    res = [at(f"res{s}", [P, D], F32, 136 + 4 * s) for s in range(2)]
    hn = [at(f"hn{s}", [P, D], F32, 144 + 4 * s) for s in range(2)]
    gain_post = at("gain_post", [P, D], F32, 152)
    gain_pre = at("gain_pre", [P, D], F32, 156)
    junk = at("junk", [P, D], F32, 160)
    xq = at("xq", [P, KC, SEQ], F32, 128)
    km = at("km", [P, KC, MEM], F32, 160)
    vm = at("vm", [P, MT, D], F32, 168)
    xp = [at(f"xp{s}", [P, XH, MEM], F32, 184 + 4 * s) for s in range(2)]
    xpt = [at(f"xpt{s}", [P, MT, XH, P], F32, 192 + 4 * s) for s in range(2)]
    acc = at("acc", [P, NT, D], F32, 64)
    hid_h = at("hid_h", [P, GROUP, SEQ], F32R, 96)
    hid_l = at("hid_l", [P, GROUP, SEQ], F32R, 112)
    w2_h = at("w2_h", [P, GROUP, D], F32R, 128)
    w2_l = at("w2_l", [P, GROUP, D], F32R, 144)
    rl = [at(f"rl{s}", [P, SEQ], F32, 160 + 4 * s) for s in range(2)]
    gain_f = at("gain_f", [P, D], F32, 168)
    junk_f = at("junk_f", [P, D], F32, 172)
    res_f = [at(f"res_f{s}", [P, D], F32, 128 + 4 * s) for s in range(2)]
    upd_f = [at(f"upd_f{s}", [P, D], F32, 136 + 4 * s) for s in range(2)]
    wraw = [at(f"wraw{s}", [P, D], F32, 176 + 4 * s) for s in range(2)]
    tw_h = [at(f"tw_h{s}", [P, KC, P], F32R, 184 + 8 * s) for s in range(2)]
    tw_l = [at(f"tw_l{s}", [P, KC, P], F32R, 188 + 8 * s) for s in range(2)]
    ident = at("ident", [P, P], F32, 200)
    ones = at("ones", [P, P], F32, 200.5)
    sm = at("sm", [P, SMW], F32, 201)
    gates = at("gates", [P, NT, 24], F32, 202)
    cw2k = at("cw2k", [P, 2, 2, HD], F32, 202.75)
    hid_c = at("hid_c", [P, 2, NKV * NCMP], F32, 203.75)
    kc_h = at("kc_h", [P, NKV, CPAD], F32R, 204.75)
    kc_l = at("kc_l", [P, NKV, CPAD], F32R, 205.25)
    vc = at("vc", [P, NKV, HD], F32, 205.75)
    cw2v = at("cw2v", [P, 2, HD], F32, 206.25)
    half_neg = at("half_neg", [P, 16], F32, 206.75)
    ss = at("ss", [P, 10], F32, 206.875)
    rstd = at("rstd", [P, 10], F32, 206.9375)
    mx = at("mx", [P, 3], F32, 207)
    nmx = at("nmx", [P, 2, 2], F32, 207.0625)
    mpos = at("mpos", [P, 2, 2], F32, 207.125)
    sums = at("sums", [P, QPK, 3], F32, 207.1875)
    rsum = at("rsum", [P, QPK, 3], F32, 207.25)
    xs = at("xs", [P, 3, XH], F32, 207.3125)
    t16 = at("t16", [P, 16], F32, 207.375)
    ssb = at("ssb", [P, 2, 2], F32, 207.5)
    rsb = at("rsb", [P, 2, 2], F32, 207.5625)
    wg_raw = at("wg_raw", [P, KC, 24], F32, 124)
    wg_h = at("wg_h", [P, KC, 24], F32R, 124.75)
    wg_l = at("wg_l", [P, KC, 24], F32R, 125.5)
    pw = at("pw", [P, 2, P], F32, 203.75)
    cpw = at("cpw", [P, 2, CMP_HID], F32, 44)
    oh = at("oh", [OHR, ND], BF16, 12)
    rb = at("rb", [3 * NBUCKET, NH], F32, 207.625)
    rb1 = at("rb1", [3 * NBUCKET, NH], F32, 207.65625)
    rb2 = at("rb2", [3 * NBUCKET, NH], F32, 207.6875)
    rhm = at("rhm", [3 * NBUCKET, 2, NH], BF16, 207.71875)
    relb = at("relb", [OHR, NH], BF16, 207.75)

    from contextlib import ExitStack
    ctx = ExitStack()
    with ctx:
        ps = ctx.enter_context(nc.psum_tensor("ps", [P, 8, HALF], F32))

        def sem(name):
            return ctx.enter_context(nc.semaphore(name))

        def pair(j):
            return ps[:, 2 * j:2 * j + 2, :].rearrange("p a b -> p (a b)")

        def smc(name, j=0, rows=slice(0, P)):
            return sm[rows, SM[name][0] + j:SM[name][0] + j + 1]

        raw_in = [sem("raw_in0"), sem("raw_in1")]
        wh_done, wl_done = sem("wh_done"), sem("wl_done")
        const_in, x_ld, store0 = sem("const_in"), [sem("x_ld0"), sem("x_ld1")], sem("store0")
        gates_in, ph_in, oh_in, wm_in, kv_in = sem("gates_in"), sem("ph_in"), sem("oh_in"), sem("wm_in"), sem("kv_in")
        ss_n, rs_n, hn_n, tr_n, hh_n, hl_n, msq = (sem(n) for n in ("ss_n", "rs_n", "hn_n", "tr_n", "hh_n", "hl_n", "msq"))
        consts_set = sem("consts_set")
        gh, gl = sem("gates_hi"), sem("gates_lo")
        gemm, ev_act, ev_dve = sem("gemm"), sem("ev_act"), sem("ev_dve")
        sig_e, sig_step, gate_e, gates_ok, pool_step, conv_step = (
            sem(n) for n in ("sig_e", "sig_step", "gate_e", "gates_ok", "pool_step", "conv_step"))
        end = {n: sem("end_" + n) for n in ("pe", "act", "dve", "pool")}
        fb = {n: sem("fb_" + n) for n in (
            "rb", "relb", "tab", "tab_ev", "pool", "pool_h", "pool_l", "cm", "hid", "gelu", "kc", "kc_h", "kc_l",
            "vc", "vc_ev", "mean", "dev", "sq", "var", "sd", "z", "ez", "silu", "pw", "pw_h", "pw_l", "chain")}
        at_ = {n: sem("at_" + n) for n in (
            "qk", "chain", "max", "exp", "pn", "tr", "pt", "pv", "o", "o_h", "o_l")}
        bo = [{n: sem(f"bo{s}_" + n) for n in (
            "mm", "ss", "rs", "up", "x", "ss2", "rs2", "hn", "tr", "hh", "hl", "res0", "res1", "gain", "st0", "st1",
            "sq", "psq")}
            for s in range(2)]
        xa = {n: sem("xa_" + n) for n in ("q_ev", "s", "max", "exp", "pn", "tr", "pt", "pv", "oh", "ol", "chain")}
        ml = {n: sem("ml_" + n) for n in ("up", "relu", "sq", "hh", "hl", "dn", "acc", "ss", "rs", "y", "gain", "res0",
                                          "res1", "st0", "st1", "fin", "psq")}

        x_t = a["x"].rearrange("(t p) d -> t p d", p=P)
        x1_t = a["x1"].rearrange("(t p) d -> t p d", p=P)
        x2_t = a["x2"].rearrange("(t p) d -> t p d", p=P)
        out_t = a["out"].rearrange("(t p) d -> t p d", p=P)
        mem_t = a["mem"].rearrange("(t p) d -> t p d", p=P)

        def w_dram(name, c):
            if name in ("wout", "wo"):
                return a[name][c * P:(c + 1) * P, :]
            return a[name][c].rearrange("p k n -> p (k n)")

        def t_index(n):
            if n < N_OUT:
                return n
            return J_Q + n - N_Q if N_Q <= n < N_O else None

        def w_dest(n):
            j = t_index(n)
            if j is None:
                k = PIECES[n][1]
                return wb_h[:, k, :], wb_l[:, k, :]
            return (tw_h[j % 2][:, :, :].rearrange("p k n -> p (k n)"),
                    tw_l[j % 2][:, :, :].rearrange("p k n -> p (k n)"))

        def name_of(j):
            return PIECES[j] if j < N_OUT else ("gate", 0)

        READS = [name_of(j)[0] == "in" and name_of(j)[1] in (10, 11, 12, 14, 6, 7, 8, 9) for j in range(N_OUT)]

        def dve_reads(j):
            return sum(READS[:j + 1])

        GATE_AT = N_IN + 2

        block = ctx.enter_context(nc.Block())

        @block.sync
        def _(sp):
            for n in range(N_MLP):
                if n == N_OUT:
                    sp.wait_ge(end["dve"], 2)
                    sp.wait_ge(end["act"], 2)
                    sp.wait_ge(end["pe"], 2)
                if n >= 2:
                    sp.wait_ge(wl_done, n - 1)
                sp.dma_start(wraw[n % 2][:, :], w_dram(*PIECES[n])).then_inc(raw_in[n % 2], 16)

            def mlp_piece(g, c, w):
                n = N_MLP + c
                sp.wait_ge(wl_done, g * 8 + (n - 1))
                sp.dma_start(wraw[n % 2][:, :], w).then_inc(raw_in[n % 2], 16)

            with sp.Fori(0, NGROUP) as g:
                for c in range(GROUP):
                    mlp_piece(g, c, a["w1"][bass.ds(g * GROUP + c, 1)].rearrange("a p k n -> p (a k n)"))
                for c in range(GROUP):
                    mlp_piece(g, GROUP + c, a["w2"][bass.ds(g * GROUP + c, 1)].rearrange("a p n -> p (a n)"))

        @block.gpsimd
        def _(pool):
            pool.dma_start(x_in[0][:, :], mem_t[0]).then_inc(x_ld[0], 16)
            pool.dma_start(x_in[1][:, :], mem_t[1]).then_inc(x_ld[1], 16)
            pool.dma_start(gain_m[:, :], a["mem_g"].partition_broadcast(P)).then_inc(const_in, 16)
            pool.dma_start(gain_x[:, :], a["mix_pre_g"].partition_broadcast(P)).then_inc(const_in, 16)
            pool.dma_start(ident[:, :], a["ident"]).then_inc(const_in, 16)
            pool.dma_start(sm[:, :], a["small"]).then_inc(const_in, 16)
            pool.dma_start(pw[:, :, :], a["pool_w"]).then_inc(const_in, 16)
            pool.dma_start(wg_raw[:, :, :], a["w_gate"]).then_inc(gates_in, 16)
            for s in range(2):
                pool.dma_start(cw2k[:, :, s, :], a["cmp_k_w2"].rearrange("(t p) n -> p t n", p=P)).then_inc(const_in, 16)
            pool.dma_start(cw2v[:, :, :], a["cmp_v_w2"].rearrange("(t p) n -> p t n", p=P)).then_inc(const_in, 16)
            for s in range(3):
                pool.dma_start(rb[32 * s:32 * s + 32, :], a["rel_bias"]).then_inc(const_in, 16)
            pool.memset(half_neg[:, :], -0.5).then_inc(consts_set, 1)
            pool.memset(ones[:, :], 1.0 / 256).then_inc(consts_set, 1)
            pool.wait_ge(consts_set, 2)

            def inv_rms(src, dst, ready, chain, n, done):
                pool.wait_ge(ready[0], ready[1])
                pool.tensor_scalar(src, src, 1.0 / D, EPS, ALU.mult, ALU.add).then_inc(chain, 1)
                pool.wait_ge(chain, n)
                pool.tensor_tensor(dst, src, half_neg[:, 0:1], ALU.pow).then_inc(done, 1)

            for u in range(MT + NT):
                inv_rms(ss[:, u:u + 1], rstd[:, u:u + 1], (ss_n, u + 1), msq, u + 1, rs_n)
                if u + 2 < MT + NT:
                    pool.wait_ge(hn_n, u + 1)
                    pool.dma_start(x_in[u % 2][:, :], x_t[u + 2 - MT]).then_inc(x_ld[u % 2], 16)
            pool.wait_ge(ev_act, len(T_MEM))
            pool.dma_start(a["kmd"], km0[:, :, :]).then_inc(store0, 16)
            pool.dma_start(a["vmd"], vm0[:, :, :]).then_inc(store0, 16)
            pool.wait_ge(store0, 32)

            pool.wait_ge(end["pe"], 1)
            pool.dma_start(oh[:, :], a["onehot"]).then_inc(oh_in, 16)
            pool.dma_start(cw1[0][:, :, :], a["cmp_k_w1"].rearrange("(j p) n -> p j n", p=P)).then_inc(ph_in, 16)
            pool.dma_start(cw1[1][:, :, :], a["cmp_v_w1"].rearrange("(j p) n -> p j n", p=P)).then_inc(ph_in, 16)
            pool.dma_start(cpw[:, :, :], a["conv_pw"].rearrange("(t p) n -> p t n", p=P)).then_inc(ph_in, 16)
            for n in ("pe", "act", "dve"):
                pool.wait_ge(end[n], 2)
            pool.dma_start(wm[:, :], a["winmask"]).then_inc(wm_in, 16)

            def block_out(s, src, dst, last_phase):
                b = bo[s]
                for n in ("pe", "act", "dve"):
                    pool.wait_ge(end[n], last_phase)
                pool.dma_start(gain_post[:, :], a[("mix_post_g", "xa_post_g")[s]].partition_broadcast(P)).then_inc(b["gain"], 16)
                pool.dma_start(gain_pre[:, :], a[("xa_pre_g", "mlp_pre_g")[s]].partition_broadcast(P)).then_inc(b["gain"], 16)
                for t in range(2):
                    pool.dma_start(res[t][:, :], src[t]).then_inc(b[f"res{t}"], 16)
                for t in range(NT):
                    inv_rms(ssb[:, 0, t % 2:t % 2 + 1], rsb[:, 0, t % 2:t % 2 + 1], (b["ss"], t + 1), b["sq"], 2 * t + 1, b["rs"])
                    inv_rms(ssb[:, 1, t % 2:t % 2 + 1], rsb[:, 1, t % 2:t % 2 + 1], (b["ss2"], t + 1), b["sq"], 2 * t + 2, b["rs2"])
                    pool.dma_start(dst[t], upd[t % 2][:, :]).then_inc(b[f"st{t % 2}"], 16)
                    if t + 2 < NT:
                        pool.dma_start(res[t % 2][:, :], src[t + 2]).then_inc(b[f"res{t % 2}"], 16)
                for t in range(2):
                    pool.wait_ge(b[f"st{t}"], 16 * (NT // 2))

            block_out(0, x_t, x1_t, 3)
            for n in ("pe", "act", "dve"):
                pool.wait_ge(end[n], 4)
            pool.dma_start(km[:, :, :], a["kmd"]).then_inc(kv_in, 16)
            pool.dma_start(vm[:, :, :], a["vmd"]).then_inc(kv_in, 16)
            block_out(1, x1_t, x2_t, 6)

            for n in ("pe", "act", "dve"):
                pool.wait_ge(end[n], 7)
            pool.dma_start(gain_f[:, :], a["mlp_post_g"].partition_broadcast(P)).then_inc(ml["gain"], 16)
            pool.wait_ge(ml["dn"], 2 * NT * NGROUP + 1)
            for t in range(2):
                pool.dma_start(res_f[t][:, :], x2_t[t]).then_inc(ml[f"res{t}"], 16)
            for t in range(NT):
                inv_rms(ssb[:, 0, t % 2:t % 2 + 1], rsb[:, 0, t % 2:t % 2 + 1], (ml["ss"], t + 1), ml["psq"], t + 1, ml["rs"])
                pool.wait_ge(ml["fin"], t + 1)
                pool.dma_start(out_t[t], upd_f[t % 2][:, :]).then_inc(ml[f"st{t % 2}"], 16)
                if t + 2 < NT:
                    pool.dma_start(res_f[t % 2][:, :], x2_t[t + 2]).then_inc(ml[f"res{t % 2}"], 16)
            for t in range(2):
                pool.wait_ge(ml[f"st{t}"], 16 * (NT // 2))

        def three_pass(pe, out, lh, ll, rh, rl_, first, last):
            nc.tensor.matmul(out, lh, rh, start=first, stop=False)
            nc.tensor.matmul(out, lh, rl_, start=False, stop=False)
            return nc.tensor.matmul(out, ll, rh, start=False, stop=last)

        def t_product(pe, j, rh, rl_, out, cols):
            for c0 in range(0, cols, HALF):
                w = min(HALF, cols - c0)
                for k in range(KC):
                    last = three_pass(pe, out[:, c0:c0 + w], tw_h[j % 2][:, k, :], tw_l[j % 2][:, k, :],
                                      rh[:, k, c0:c0 + w], rl_[:, k, c0:c0 + w], k == 0, k == KC - 1)
            return last

        def n_product(pe, lh, ll, rh, rl_, out):
            for k in range(KC):
                last = three_pass(pe, out, lh[:, k], ll[:, k], rh[:, k], rl_[:, k], k == 0, k == KC - 1)
            return last

        SUB = [(i, g, kind) for i in range(NT) for g in range(NKV) for kind in (0, 1)]

        def tiles_of(s):
            i, _, kind = SUB[s]
            return i + 1 if kind == 0 else min(WIN_TILES + 1, i + 1) + 1

        def events(s):
            n = tiles_of(s) if s >= 0 else 0
            rows = QPK if s + 1 < len(SUB) else 0
            out, t = [], 0
            for r in range(rows):
                out.append(("row", r))
                if r >= 1 and t < n:
                    out.append(("tile", t))
                    t += 1
            return out + [("tile", k) for k in range(t, n)]

        TILE0 = [sum(tiles_of(s) for s in range(k)) for k in range(len(SUB) + 1)]

        def width(i, kind):
            return P * (i + 1) if kind == 0 else P * min(WIN_TILES + 1, i + 1)

        @block.tensor
        def _(pe):
            pe.wait_ge(const_in, 16 * 11)

            def transposes(u, src, ready, need, done, free):
                pe.wait_ge(ready, need)
                if free is not None:
                    pe.wait_ge(*free)
                for k in range(KC):
                    last = nc.tensor.transpose(pair(2 + u % 2)[:, k * P:(k + 1) * P], src[:, k * P:(k + 1) * P], ident[:, :])
                last.then_inc(done, 1)

            def before(j):
                pe.wait_ge(wl_done, j + 1)
                if j >= 2:
                    pe.wait_ge(ev_act, j - 1)
                    if dve_reads(j - 2):
                        pe.wait_ge(ev_dve, dve_reads(j - 2))

            def mem_chunk(j):
                before(j)
                if j < 8:
                    last = t_product(pe, j, mT_h, mT_l, pair(j % 2), MEM)
                else:
                    for i in range(MT):
                        ts = slice(i * P, (i + 1) * P)
                        last = n_product(pe, mT_h[:, :, ts], mT_l[:, :, ts], tw_h[j % 2], tw_l[j % 2],
                                         pair(j % 2)[:, ts])
                last.then_inc(gemm, 1)

            for u in range(MT + NT):
                transposes(u, hn0[u % 2], hn_n, u + 1, tr_n, (hl_n, u - 1) if u >= 2 else None)
                if u >= MT:
                    if u == MT:
                        pe.wait_ge(hl_n, MT)
                    for j in (2 * (u - MT), 2 * (u - MT) + 1):
                        mem_chunk(j)
            pe.wait_ge(hl_n, MT + NT)
            for j in range(N_IN, N_OUT):
                if j == GATE_AT:
                    pe.wait_ge(gl, 1)
                    for t in range(NT):
                        ts = slice(t * P, (t + 1) * P)
                        last = n_product(pe, hT_h[:, :, ts], hT_l[:, :, ts], wg_h, wg_l, pair(2)[:, 24 * t:24 * t + 24])
                    last.then_inc(gemm, 1)
                before(j)
                if PIECES[j][1] in (13, 15):
                    for t in range(NT):
                        ts = slice(t * P, (t + 1) * P)
                        last = n_product(pe, hT_h[:, :, ts], hT_l[:, :, ts], tw_h[j % 2], tw_l[j % 2], pair(j % 2)[:, ts])
                else:
                    last = t_product(pe, j, hT_h, hT_l, pair(j % 2), SEQ)
                last.then_inc(gemm, 1)
            pe.drain().then_inc(end["pe"], 1)
            for n in ("act", "dve"):
                pe.wait_ge(end[n], 1)

            pe.wait_ge(consts_set, 2)
            pe.wait_ge(oh_in, 16)
            pe.wait_ge(fb["relb"], 1)
            for xcol in range(NEAR):
                o = P - xcol - DMIN
                last = nc.tensor.matmul(ps[:, xcol // 64, (xcol % 64) * 8:(xcol % 64) * 8 + 8], oh[:, o:o + P], relb[:, :],
                                        start=True, stop=True)
            last.then_inc(fb["tab"], 1)
            for z in range(ZC):
                o = -CMP_STRIDE * (z - 56) - (CMP_LEN - 1) - DMIN
                last = nc.tensor.matmul(ps[:, 4 + z // 64, (z % 64) * 8:(z % 64) * 8 + 8], oh[:, o:o + P], relb[:, :],
                                        start=True, stop=True)
            last.then_inc(fb["tab"], 1)
            for c in range(2):
                if c == 1:
                    pe.wait_ge(fb["tab_ev"], 2)
                for hf in range(2):
                    last = nc.tensor.matmul(ps[:, 6 - 2 * c + hf, :], pw[:, c, :], pu[:, c, hf * HALF:(hf + 1) * HALF],
                                            start=True, stop=True)
                last.then_inc(fb["pool"], 1)
            pe.wait_ge(fb["tab_ev"], 1)
            for hf in range(2):
                for c in range(2):
                    last = nc.tensor.matmul(ps[:, hf, :], ones[:, :], ca[:, c, hf * HALF:(hf + 1) * HALF],
                                            start=c == 0, stop=c == 1)
            last.then_inc(fb["mean"], 1)
            pe.wait_ge(ph_in, 48)
            for kv in range(2):
                pe.wait_ge(fb["cm"], kv + 1)
                for ht in range(2):
                    for j in range(16):
                        last = nc.tensor.matmul(ps[:, 2 + kv, 126 * ht:126 * ht + 126], cw1[kv][:, j, ht * P:(ht + 1) * P],
                                                cm[kv][:, j, :, :], start=j == 0, stop=j == 15)
                last.then_inc(fb["hid"], 1)
            pe.wait_ge(fb["sq"], 2)
            pe.wait_ge(fb["pool_l"], 2)
            pe.wait_ge(fb["dev"], 2)
            for hf in range(2):
                for c in range(2):
                    last = nc.tensor.matmul(ps[:, hf, :], ones[:, :], ch[:, c, hf * HALF:(hf + 1) * HALF],
                                            start=c == 0, stop=c == 1)
            last.then_inc(fb["var"], 1)
            for kv in range(2):
                pe.wait_ge(fb["gelu"], kv + 1)
                if kv == 0:
                    for ht in range(2):
                        last = nc.tensor.matmul(ps[:, 4, 0:126], cw2k[:, ht, :, :], hid_c[:, ht, :], start=ht == 0, stop=ht == 1)
                    last.then_inc(fb["kc"], 1)
                else:
                    for g in range(NKV):
                        for ht in range(2):
                            last = nc.tensor.matmul(ps[0:NCMP, 5, HD * g:HD * g + HD], hid_c[:, ht, g * NCMP:(g + 1) * NCMP],
                                                    cw2v[:, ht, :], start=ht == 0, stop=ht == 1)
                    last.then_inc(fb["vc"], 1)
            pe.wait_ge(fb["silu"], 2)
            for m in range(2):
                for hf in range(2):
                    for c in range(2):
                        last = nc.tensor.matmul(ps[:, 6 - 4 * m + hf, :], cpw[:, c, m * P:(m + 1) * P],
                                                ca[:, c, hf * HALF:(hf + 1) * HALF], start=c == 0, stop=c == 1)
                last.then_inc(fb["pw"], 1)
            pe.drain().then_inc(end["pe"], 1)
            for n in ("act", "dve"):
                pe.wait_ge(end[n], 2)

            def score_row(s, r):
                i, g, kind = SUB[s]
                n = s * QPK + r
                h = QPK * g + r
                if n >= 2:
                    pe.wait_ge(at_["exp"], n - 1)
                sc = pair(n % 2)
                qs = q_st[:, h, i * P:(i + 1) * P]
                w = width(i, kind)
                k0 = (i + 1) * P - w
                for c0 in range(0, w, HALF):
                    c1 = min(c0 + HALF, w)
                    nc.tensor.matmul(sc[:, c0:c1], qs, k_h[:, kind, g, k0 + c0:k0 + c1], start=True, stop=False)
                    last = nc.tensor.matmul(sc[:, c0:c1], qs, k_l[:, kind, g, k0 + c0:k0 + c1], start=False, stop=True)
                if kind == 1:
                    cc = sc[:, 5 * P:5 * P + CPAD]
                    nc.tensor.matmul(cc, qs, kc_h[:, g, :], start=True, stop=False)
                    last = nc.tensor.matmul(cc, qs, kc_l[:, g, :], start=False, stop=True)
                last.then_inc(at_["qk"], 1)

            def key_tile_transposed(s, t):
                i, g, kind = SUB[s]
                n = TILE0[s] + t
                if t == 0:
                    pe.wait_ge(at_["pn"], QPK * (s + 1))
                if n >= 2:
                    pe.wait_ge(at_["pt"], n - 1)
                cmp_tile = kind == 1 and t == tiles_of(s) - 1
                for r in range(QPK):
                    src = p_sel[:, r, t * P:(t + 1) * P] if kind == 0 else (
                        p_win[:, r, 5 * P:5 * P + NCMP] if cmp_tile else p_win[:, r, t * P:(t + 1) * P])
                    rows = NCMP if cmp_tile else P
                    last = nc.tensor.transpose(ps[0:rows, 4 + n % 2, r * P:(r + 1) * P], src, ident[:, :])
                last.then_inc(at_["tr"], 1)

            def key_tile_product(s, t):
                i, g, kind = SUB[s]
                n = TILE0[s] + t
                unit = s // 2
                first = kind == 0 and t == 0
                end_of_unit = kind == 1 and t == tiles_of(s) - 1
                pe.wait_ge(at_["pt"], n + 1)
                if first and unit >= 2:
                    pe.wait_ge(at_["o_l"], unit - 1)
                o = ps[0:HD, 6 + unit % 2, :]
                if end_of_unit:
                    last = nc.tensor.matmul(o, vc[0:NCMP, g, :], pt[0:NCMP, n % 2, :], start=False, stop=True)
                else:
                    kt = t if kind == 0 else max(0, i - WIN_TILES) + t
                    last = nc.tensor.matmul(o, v_sw[:, kt, kind, g * HD:(g + 1) * HD], pt[:, n % 2, :], start=first, stop=False)
                last.then_inc(at_["pv"], 1)

            pending = None
            for s in range(-1, len(SUB)):
                for what, k in events(s):
                    if what == "row":
                        score_row(s + 1, k)
                    else:
                        key_tile_transposed(s, k)
                        if pending:
                            key_tile_product(*pending)
                        pending = (s, k)
            key_tile_product(*pending)
            pe.drain().then_inc(end["pe"], 1)

            def block_product(s, n0):
                b = bo[s]

                def tile_t(t):
                    if t == 0:
                        pe.wait_ge(wl_done, n0 + KC)
                    if t >= 2:
                        pe.wait_ge(b["up"], t - 1)
                    ts = slice(t * P, (t + 1) * P)
                    for hf in range(2):
                        c = slice(hf * HALF, (hf + 1) * HALF)
                        last = n_product(pe, hT_h[:, :, ts], hT_l[:, :, ts], wb_h[:, :, c], wb_l[:, :, c], pair(t % 2)[:, c])
                    last.then_inc(b["mm"], 1)

                tile_t(0)
                for t in range(1, NT):
                    tile_t(t)
                    transposes(t - 1, hn[(t - 1) % 2], b["hn"], t, b["tr"], (b["hl"], t - 2) if t >= 3 else None)
                transposes(NT - 1, hn[(NT - 1) % 2], b["hn"], NT, b["tr"], (b["hl"], NT - 2))

            for n in ("act", "dve"):
                pe.wait_ge(end[n], 3)
            block_product(0, N_OUT)
            pe.drain().then_inc(end["pe"], 1)
            for n in ("act", "dve"):
                pe.wait_ge(end[n], 4)
            for m in range(8):
                pe.wait_ge(wl_done, N_Q + m + 1)
                if m >= 2:
                    pe.wait_ge(xa["q_ev"], m - 1)
                t_product(pe, J_Q + m, hT_h, hT_l, pair(m % 2), SEQ).then_inc(gemm, 1)
            pe.drain().then_inc(end["pe"], 1)
            for n in ("act", "dve"):
                pe.wait_ge(end[n], 5)
            pe.wait_ge(kv_in, 32)

            def x_scores(t):
                if t >= 2:
                    pe.wait_ge(xa["exp"], XH * (t - 1))
                for h in range(XH):
                    for c in range(2):
                        last = nc.tensor.matmul(pair(t % 2)[:, h * MEM:(h + 1) * MEM], xq[:, 2 * h + c, t * P:(t + 1) * P],
                                                km[:, 2 * h + c, :], start=c == 0, stop=c == 1)
                last.then_inc(xa["s"], 1)

            def x_transposes(t):
                pe.wait_ge(xa["pn"], t + 1)
                if t >= 1:
                    pe.wait_ge(xa["pt"], t)
                for m in range(MT):
                    for h in range(XH):
                        last = nc.tensor.transpose(pair(2)[:, (m * XH + h) * P:(m * XH + h + 1) * P],
                                                   xp[t % 2][:, h, m * P:(m + 1) * P], ident[:, :])
                last.then_inc(xa["tr"], 1)

            def x_values(t):
                pe.wait_ge(xa["pt"], t + 1)
                if t >= 1:
                    pe.wait_ge(xa["ol"], t)
                for c in range(KC):
                    for m in range(MT):
                        last = nc.tensor.matmul(pair(3)[:, c * P:(c + 1) * P], vm[:, m, c * P:(c + 1) * P],
                                                xpt[t % 2][:, m, c // 2, :], start=m == 0, stop=m == MT - 1)
                last.then_inc(xa["pv"], 1)

            x_scores(0)
            for t in range(NT):
                if t + 1 < NT:
                    x_scores(t + 1)
                x_transposes(t)
                if t >= 1:
                    x_values(t - 1)
            x_values(NT - 1)
            pe.drain().then_inc(end["pe"], 1)
            for n in ("act", "dve"):
                pe.wait_ge(end[n], 6)
            block_product(1, N_O)
            pe.drain().then_inc(end["pe"], 1)
            for n in ("act", "dve"):
                pe.wait_ge(end[n], 7)

            with pe.Fori(0, NGROUP) as g:
                for c in range(GROUP):
                    pe.wait_ge(wl_done, g * 8 + (N_MLP + c + 1))
                    pe.wait_ge(ml["relu"], g * GROUP + (c + 1))
                    t_product(pe, J_MLP + c, hT_h, hT_l, pair(c % 2), SEQ).then_inc(ml["up"], 1)
                for idx in range(2 * NT):
                    t, hf = idx // 2, idx % 2
                    ts, cs = slice(t * P, (t + 1) * P), slice(hf * HALF, (hf + 1) * HALF)
                    pe.wait_ge(ml["acc"], g * (2 * NT) + (idx + 1))
                    for c in range(GROUP):
                        if idx == 0:
                            pe.wait_ge(wl_done, g * 8 + (N_MLP + GROUP + c + 1))
                            pe.wait_ge(ml["hl"], g * GROUP + (c + 3))
                        last = three_pass(pe, ps[:, 4 + idx % 4, :], hid_h[:, c, ts], hid_l[:, c, ts],
                                          w2_h[:, c, cs], w2_l[:, c, cs], c == 0, c == GROUP - 1)
                    last.then_inc(ml["dn"], 1)

        @block.scalar
        def _(act):
            def w_hi(n):
                act.wait_ge(raw_in[n % 2], 16 * (n // 2 + 1))
                j = t_index(n)
                if j is not None and j >= 2:
                    act.wait_ge(gemm, j - 1 + (j - 2 >= GATE_AT))
                nc.scalar.activation(w_dest(n)[0], wraw[n % 2][:, :], ACT.Copy).then_inc(wh_done, 1)

            def sum_squares(src, out, scratch, done):
                nc.scalar.activation(scratch, src, ACT.Square, accum_out=out).then_inc(done, 1)

            act.wait_ge(const_in, 16 * 11)
            act.wait_ge(gates_in, 16)
            act.activation(wg_h[:, :, :], wg_raw[:, :, :], ACT.Copy).then_inc(gh, 1)
            w_hi(0)
            w_hi(1)

            def mem_evac(j):
                act.wait_ge(gemm, j + 1)
                if j < 8:
                    act.activation(km0[:, j, :], pair(j % 2)[:, 0:MEM], ACT.Copy).then_inc(ev_act, 1)
                else:
                    act.activation(vm0[:, :, (j - 8) * P:(j - 7) * P],
                                   pair(j % 2)[:, 0:MEM].rearrange("p (t c) -> p t c", t=MT), ACT.Copy).then_inc(ev_act, 1)

            for u in range(MT + NT + 1):
                if u < MT + NT:
                    act.wait_ge(x_ld[u % 2], 16 * (u // 2 + 1))
                    if u >= 1:
                        act.wait_ge(ss_n, u)
                    sum_squares(x_in[u % 2][:, :], ss[:, u:u + 1], junk0[:, :], ss_n)
                if u >= 1:
                    v = u - 1
                    act.wait_ge(tr_n, v + 1)
                    dst = mT_h[:, :, v * P:(v + 1) * P] if v < MT else hT_h[:, :, (v - MT) * P:(v - MT + 1) * P]
                    act.activation(dst, pair(2 + v % 2).rearrange("p (k c) -> p k c", k=KC), ACT.Copy).then_inc(hh_n, 1)
                    if v >= MT:
                        for j in (2 * (v - MT), 2 * (v - MT) + 1):
                            mem_evac(j)
                            w_hi(j + 2)

            def in_wait(j):
                act.wait_ge(gemm, j + 1 + (j >= GATE_AT))

            for j in range(N_IN, N_OUT):
                if j == GATE_AT:
                    act.wait_ge(gemm, GATE_AT + 1)
                    act.activation(gates[:, :, :], pair(2)[:, 0:24 * NT].rearrange("p (t c) -> p t c", t=NT), ACT.Exp,
                                   scale=-1.0).then_inc(gate_e, 1)
                in_wait(j)
                pp = pair(j % 2)
                m = PIECES[j][1]
                if m in (13, 15):
                    act.activation(v_sw[:, :, (m - 13) // 2, :], pp.rearrange("p (t c) -> p t c", t=NT), ACT.Copy).then_inc(ev_act, 1)
                elif m in (0, 1):
                    act.activation(pu[:, m, :], pp, ACT.Copy).then_inc(ev_act, 1)
                elif m in (2, 3):
                    act.activation(ch[:, m - 2, :], pp, ACT.Copy).then_inc(ev_act, 1)
                elif m in (4, 5):
                    if m == 5:
                        act.wait_ge(sig_step, 3)
                    act.activation(sig[:, :], pp, ACT.Exp, scale=-1.0).then_inc(ev_act, 1)
                elif m in (10, 11):
                    st = c_st[m - 10]
                    act.activation(st[0:HD, 0, :], pp[0:HD, :], ACT.Copy)
                    act.activation(st[0:HD, 1, :], pp[HD:P, :], ACT.Copy).then_inc(ev_act, 1)
                elif m in (12, 14):
                    kd = (m - 12) // 2
                    if m == 12:
                        act.wait_ge(store0, 32)
                    act.activation(k_h[0:HD, kd, 0, :], pp[0:HD, :], ACT.Copy)
                    act.activation(k_h[HD:P, kd, 0, :], pp[0:HD, :], ACT.Copy)
                    act.activation(k_h[0:HD, kd, 1, :], pp[HD:P, :], ACT.Copy)
                    act.activation(k_h[HD:P, kd, 1, :], pp[HD:P, :], ACT.Copy).then_inc(ev_act, 1)
                else:
                    if m == 6:
                        act.wait_ge(sig_step, 6)
                        act.wait_ge(pool_step, POOL_STEPS)
                    h = 2 * (m - 6)
                    act.activation(q_st[0:HD, h, :], pp[0:HD, :], ACT.Copy, scale=HD ** -0.5)
                    act.activation(q_st[HD:P, h + 1, :], pp[HD:P, :], ACT.Copy, scale=HD ** -0.5).then_inc(ev_act, 1)
                if j + 2 < N_OUT:
                    w_hi(j + 2)
            act.drain().then_inc(end["act"], 1)
            for n in ("pe", "dve"):
                act.wait_ge(end[n], 1)

            act.wait_ge(fb["tab"], 1)
            act.wait_ge(fb["cm"], 2)
            act.activation(tn[:, :, :].rearrange("p h x -> p x h"), ps[:, 0:4, :].rearrange("p a (b h) -> p (a b) h", h=NH),
                           ACT.Copy).then_inc(fb["tab_ev"], 1)
            act.wait_ge(fb["tab"], 2)
            act.activation(tc[:, :, :].rearrange("p h x -> p x h"),
                           pair(2)[:, 0:NH * ZC].rearrange("p (z h) -> p z h", h=NH), ACT.Copy).then_inc(fb["tab_ev"], 1)
            for c in range(2):
                act.wait_ge(fb["pool"], c + 1)
                act.activation(hT_h[:, c, :], pair(3 - c), ACT.Copy, scale=smc("pool_scale", c)).then_inc(fb["pool_h"], 1)
            for c in range(2):
                act.wait_ge(fb["dev"], c + 1)
                act.activation(ch[:, c, :], ca[:, c, :], ACT.Square).then_inc(fb["sq"], 1)
            for kv in range(2):
                act.wait_ge(fb["hid"], kv + 1)
                if kv == 1:
                    act.wait_ge(fb["kc"], 1)
                act.activation(hid_c[:, :, :], ps[:, 2 + kv, 0:252].rearrange("p (t c) -> p t c", t=2),
                               ACT.Gelu_apprx_tanh).then_inc(fb["gelu"], 1)
                if kv == 0:
                    act.wait_ge(fb["kc"], 1)
                    act.wait_ge(fb["chain"], 2)
                    act.activation(kc_h[:, :, 0:NCMP], ps[:, 4, 0:126].rearrange("p (g c) -> p g c", g=NKV),
                                   ACT.Copy).then_inc(fb["kc_h"], 1)
            act.wait_ge(fb["vc"], 1)
            act.activation(vc[0:NCMP, :, :], ps[0:NCMP, 5, 0:P].rearrange("p (g c) -> p g c", g=NKV), ACT.Copy).then_inc(fb["vc_ev"], 1)
            act.wait_ge(fb["var"], 1)
            act.activation(cln[:, :], pair(0), ACT.Sqrt, bias=smc("eps")).then_inc(fb["sd"], 1)
            for c in range(2):
                act.wait_ge(fb["z"], c + 1)
                act.activation(ctmp[:, :] if c == 0 else cln[:, :], ca[:, c, :], ACT.Exp, scale=-1.0).then_inc(fb["ez"], 1)
            for m in range(2):
                act.wait_ge(fb["pw"], m + 1)
                act.activation(hT_h[:, 2 + m, :], pair(3 - 2 * m), ACT.Copy).then_inc(fb["pw_h"], 1)
            act.drain().then_inc(end["act"], 1)
            for n in ("pe", "dve"):
                act.wait_ge(end[n], 2)

            def exp_row(s, r):
                i, g, kind = SUB[s]
                n = s * QPK + r
                act.wait_ge(at_["max"], n + 1)
                if s >= 2 and r == 0:
                    act.wait_ge(at_["tr"], TILE0[s - 1])
                w = width(i, kind)
                nb = nmx[:, n % 2, :]
                if kind == 0:
                    act.activation(p_sel[:, r, 0:w], pair(n % 2)[:, 0:w], ACT.Exp, bias=nb[:, 0:1],
                                   accum_out=sums[:, r, 1:2]).then_inc(at_["exp"], 1)
                else:
                    act.activation(p_win[:, r, 0:w], pair(n % 2)[:, 0:w], ACT.Exp, bias=nb[:, 0:1],
                                   accum_out=sums[:, r, 2:3])
                    act.activation(p_win[:, r, 5 * P:5 * P + CPAD], pair(n % 2)[:, 5 * P:5 * P + CPAD], ACT.Exp,
                                   bias=nb[:, 1:2], accum_out=sums[:, r, 0:1]).then_inc(at_["exp"], 1)

            def copy_tile(s, t):
                n = TILE0[s] + t
                rows = NCMP if (SUB[s][2] == 1 and t == tiles_of(s) - 1) else P
                act.wait_ge(at_["tr"], n + 1)
                if n >= 2:
                    act.wait_ge(at_["pv"], n - 1)
                act.activation(pt[0:rows, n % 2, :], ps[0:rows, 4 + n % 2, :], ACT.Copy).then_inc(at_["pt"], 1)

            def take_output(unit):
                i, g = unit // NKV, unit % NKV
                act.wait_ge(at_["pv"], TILE0[2 * unit + 2])
                o = ps[0:HD, 6 + unit % 2, :].rearrange("p (c e q) -> p c e q", e=2, q=P)
                for e in range(2):
                    last = act.activation(hT_h[HD * e:HD * e + HD, 4 + 2 * g:6 + 2 * g, i * P:(i + 1) * P], o[:, :, e, :], ACT.Copy)
                last.then_inc(at_["o_h"], 1)

            for s in range(-1, len(SUB)):
                for what, k in events(s):
                    if what == "row":
                        exp_row(s + 1, k)
                    else:
                        copy_tile(s, k)
                    if (what, k) == ("tile", 1) and s >= 2 and s % 2 == 0:
                        take_output(s // 2 - 1)
                if s >= 2 and s % 2 == 0 and tiles_of(s) < 2:
                    take_output(s // 2 - 1)
            take_output(len(SUB) // 2 - 1)
            act.drain().then_inc(end["act"], 1)
            for n in ("pe", "dve"):
                act.wait_ge(end[n], 3)

            def block_out(s, split_next):
                b = bo[s]
                act.wait_ge(b["gain"], 32)
                for t in range(NT + 1):
                    if t < NT:
                        act.wait_ge(b["mm"], t + 1)
                        if t >= 2:
                            act.wait_ge(b["up"], t - 1)
                        if t >= 1:
                            act.wait_ge(b["ss2"], t)
                        sum_squares(pair(t % 2), ssb[:, 0, t % 2:t % 2 + 1], junk[:, :], b["ss"])
                    if t >= 1:
                        act.wait_ge(b["tr"], t)
                        ts = slice((t - 1) * P, t * P)
                        act.activation(hT_h[:, :, ts], pair(2 + (t - 1) % 2).rearrange("p (k c) -> p k c", k=KC),
                                       ACT.Copy).then_inc(b["hh"], 1)
                    if t < NT:
                        act.wait_ge(b["x"], t + 1)
                        act.wait_ge(b["ss"], t + 1)
                        sum_squares(upd[t % 2][:, :], ssb[:, 1, t % 2:t % 2 + 1], junk[:, :], b["ss2"])
                        if split_next and t == NT - 1:
                            w_hi(N_Q)
                            w_hi(N_Q + 1)

            for k in range(KC):
                w_hi(N_OUT + k)
            block_out(0, True)
            act.drain().then_inc(end["act"], 1)
            for n in ("pe", "dve"):
                act.wait_ge(end[n], 4)
            for m in range(8):
                act.wait_ge(gemm, J_Q + m + 2)
                if m == 0:
                    for t in range(2):
                        act.wait_ge(bo[0][f"st{t}"], 16 * (NT // 2))
                act.activation(xq[:, m, :], pair(m % 2), ACT.Copy, scale=(D // XH) ** -0.5).then_inc(xa["q_ev"], 1)
                if m + 2 < 8:
                    w_hi(N_Q + m + 2)
            act.drain().then_inc(end["act"], 1)
            for n in ("pe", "dve"):
                act.wait_ge(end[n], 5)

            for t in range(NT + 2):
                if t < NT:
                    act.wait_ge(xa["max"], t + 1)
                    if t >= 2:
                        act.wait_ge(xa["tr"], t - 1)
                    for h in range(XH):
                        act.activation(xp[t % 2][:, h, :], pair(t % 2)[:, h * MEM:(h + 1) * MEM], ACT.Exp,
                                       bias=xs[:, 0, h:h + 1], accum_out=xs[:, 1, h:h + 1]).then_inc(xa["exp"], 1)
                if 1 <= t <= NT:
                    act.wait_ge(xa["tr"], t)
                    if t >= 3:
                        act.wait_ge(xa["pv"], t - 2)
                    act.activation(xpt[(t - 1) % 2][:, :, :, :].rearrange("p m h c -> p (m h c)"), pair(2), ACT.Copy).then_inc(xa["pt"], 1)
                if t >= 2:
                    act.wait_ge(xa["pv"], t - 1)
                    ts = slice((t - 2) * P, (t - 1) * P)
                    act.activation(hT_h[:, :, ts], pair(3).rearrange("p (k c) -> p k c", k=KC), ACT.Copy).then_inc(xa["oh"], 1)
                if t < NT:
                    w_hi(N_O + t)
            act.drain().then_inc(end["act"], 1)
            for n in ("pe", "dve"):
                act.wait_ge(end[n], 6)

            def w_hi_mlp(g, c):
                n = N_MLP + c
                act.wait_ge(raw_in[n % 2], g * (16 * 4) + 16 * (n // 2 + 1))
                if c < GROUP:
                    j = J_MLP + c
                    act.wait_ge(ml["up"], g * GROUP + (c + 1))
                    dst = tw_h[j % 2][:, :, :].rearrange("p k n -> p (k n)")
                else:
                    act.wait_ge(ml["dn"], g * (2 * NT) + 1)
                    dst = w2_h[:, c - GROUP, :]
                act.activation(dst, wraw[n % 2][:, :], ACT.Copy).then_inc(wh_done, 1)

            block_out(1, False)
            act.drain().then_inc(end["act"], 1)
            for n in ("pe", "dve"):
                act.wait_ge(end[n], 7)
            for t in range(2):
                act.wait_ge(bo[1][f"st{t}"], 16 * (NT // 2))
            act.sem_inc(ml["relu"], 2)
            act.sem_inc(ml["up"], 2)
            act.sem_inc(ml["dn"], 1)

            def hidden(g, c):
                act.wait_ge(ml["up"], g * GROUP + (c + 3))
                act.wait_ge(ml["hl"], g * GROUP + (c + 1))
                act.activation(rl[c % 2][:, :], pair(c % 2), ACT.Relu).then_inc(ml["relu"], 1)
                act.wait_ge(ml["relu"], g * GROUP + (c + 3))
                act.activation(rl[c % 2][:, :], rl[c % 2][:, :], ACT.Square).then_inc(ml["sq"], 1)
                act.wait_ge(ml["sq"], g * GROUP + (c + 1))
                act.wait_ge(ml["dn"], g * (2 * NT) + 1)
                act.activation(hid_h[:, c, :], rl[c % 2][:, :], ACT.Copy).then_inc(ml["hh"], 1)

            with act.Fori(0, NGROUP) as g:
                w_hi_mlp(g, 0)
                w_hi_mlp(g, 1)
                hidden(g, 0)
                w_hi_mlp(g, 2)
                hidden(g, 1)
                w_hi_mlp(g, 3)
                hidden(g, 2)
                w_hi_mlp(g, 4)
                w_hi_mlp(g, 5)
                hidden(g, 3)
                w_hi_mlp(g, 6)
                w_hi_mlp(g, 7)
            for t in range(NT):
                act.wait_ge(ml["acc"], 2 * NT * (NGROUP - 1) + 4 + 2 * (t + 1))
                if t >= 2:
                    act.wait_ge(ml["y"], t - 1)
                if t >= 1:
                    act.wait_ge(ml["ss"], t)
                sum_squares(acc[:, t, :], ssb[:, 0, t % 2:t % 2 + 1], junk_f[:, :], ml["ss"])

        @block.vector
        def _(dve):
            V = nc.vector

            def w_lo(n):
                dve.wait_ge(wh_done, n + 1)
                dst, hi = w_dest(n)[1], w_dest(n)[0]
                V.tensor_tensor(dst, wraw[n % 2][:, :], hi.bitcast(F32), ALU.subtract).then_inc(wl_done, 1)

            dve.wait_ge(const_in, 16 * 11)
            dve.wait_ge(gh, 1)
            V.tensor_tensor(wg_l[:, :, :], wg_raw[:, :, :], wg_h[:, :, :].bitcast(F32), ALU.subtract).then_inc(gl, 1)
            w_lo(0)
            w_lo(1)
            for u in range(MT + NT + 1):
                if u < MT + NT:
                    dve.wait_ge(rs_n, u + 1)
                    if u >= 2:
                        dve.wait_ge(tr_n, u - 1)
                    V.scalar_tensor_tensor(hn0[u % 2][:, :], x_in[u % 2][:, :], rstd[:, u:u + 1],
                                           (gain_m if u < MT else gain_x)[:, :], ALU.mult, ALU.mult).then_inc(hn_n, 1)
                if u >= 1:
                    v = u - 1
                    dve.wait_ge(hh_n, v + 1)
                    hi, lo = (mT_h, mT_l) if v < MT else (hT_h, hT_l)
                    v0 = v if v < MT else v - MT
                    cs = slice(v0 * P, (v0 + 1) * P)
                    V.tensor_tensor(lo[:, :, cs], pair(2 + v % 2).rearrange("p (k c) -> p k c", k=KC),
                                    hi[:, :, cs].bitcast(F32), ALU.subtract).then_inc(hl_n, 1)
                    if v >= MT:
                        for j in (2 * (v - MT), 2 * (v - MT) + 1):
                            w_lo(j + 2)

            pstep = [0]

            def pooled(ins):
                pstep[0] += 1
                ins.then_inc(pool_step, 1)
                dve.wait_ge(pool_step, pstep[0])

            def window_sum(dst, src, d, rows):
                pooled(V.tensor_tensor(dst[rows, d:], src[rows, d:], src[rows, 0:SEQ - d], ALU.add))
                pooled(V.tensor_copy(dst[rows, 0:d], src[rows, 0:d]))

            def mean_minus(c, src, rows):
                u = pu[:, c, :]
                pooled(V.tensor_tensor(t16[rows, :], src[rows, 0:16], sm[rows, SM["inv16"][0] + 16 * c:SM["inv16"][0] + 16 * c + 16], ALU.mult))
                pooled(V.tensor_tensor(u[rows, 0:16], t16[rows, :], u[rows, 0:16], ALU.subtract))
                pooled(V.scalar_tensor_tensor(u[rows, 16:], src[rows, 16:], smc("inv_win", c, rows), u[rows, 16:], ALU.mult, ALU.subtract))

            lo_rows, hi_rows, all_rows = slice(0, HD), slice(HD, P), slice(0, P)

            def pool_tile(c):
                a_, b_ = pool_a, pool_b
                window_sum(a_, pu[:, c, :], 1, all_rows)
                if c == 0:
                    window_sum(b_, a_, 2, hi_rows)
                    mean_minus(0, a_, lo_rows)
                    mean_minus(0, b_, hi_rows)
                else:
                    window_sum(b_, a_, 2, all_rows)
                    window_sum(a_, b_, 4, all_rows)
                    window_sum(b_, a_, 8, hi_rows)
                    mean_minus(1, a_, lo_rows)
                    mean_minus(1, b_, hi_rows)

            cstep = [0]

            def conv_taps(c, d0, d1):
                for d in range(d0, d1):
                    w = smc("conv_w", c * TAPS + TAPS - 1 - d)
                    if d == 0:
                        ins = V.tensor_scalar(ca[:, c, :], ch[:, c, :], w, smc("conv_b", c), ALU.mult, ALU.add)
                    else:
                        ins = V.scalar_tensor_tensor(ca[:, c, d:], ch[:, c, 0:SEQ - d], w, ca[:, c, d:], ALU.mult, ALU.add)
                    cstep[0] += 1
                    ins.then_inc(conv_step, 1)
                    dve.wait_ge(conv_step, cstep[0])

            def glu(c):
                dve.wait_ge(ev_act, N_IN + 6 + 2 * c)
                for k, op in enumerate((
                        lambda: V.tensor_scalar(sig[:, :], sig[:, :], 1.0, None, ALU.add),
                        lambda: V.reciprocal(sig[:, :], sig[:, :]),
                        lambda: V.tensor_tensor(ch[:, c, :], ch[:, c, :], sig[:, :], ALU.mult))):
                    op().then_inc(sig_step, 1)
                    dve.wait_ge(sig_step, 3 * c + k + 1)

            for j in range(N_IN, N_OUT):
                m = PIECES[j][1]
                if READS[j]:
                    dve.wait_ge(gemm, j + 2)
                pp = pair(j % 2)
                if j == GATE_AT:
                    dve.wait_ge(gate_e, 1)
                    V.tensor_scalar(gates[:, :, :], gates[:, :, :], 1.0, None, ALU.add).then_inc(gates_ok, 1)
                    dve.wait_ge(gates_ok, 1)
                    V.reciprocal(gates[:, :, :], gates[:, :, :]).then_inc(gates_ok, 1)
                    dve.wait_ge(gates_ok, 2)
                    V.tensor_scalar(gates[:, 0, 0:24:3], gates[:, 0, 0:24:3], smc("valid"), None, ALU.mult).then_inc(gates_ok, 1)
                if m in (0, 1):
                    dve.wait_ge(ev_act, j + 1)
                    pool_tile(m)
                elif m in (4, 5):
                    glu(m - 4)
                elif m in (10, 11):
                    st = c_st[m - 10]
                    dve.wait_ge(ev_act, j + 1)
                    V.tensor_copy(st[HD:P, 0, 0:SEQ - 1], pp[0:HD, 1:SEQ])
                    V.tensor_copy(st[HD:P, 1, 0:SEQ - 1], pp[HD:P, 1:SEQ]).then_inc(ev_dve, 1)
                    conv_taps(0, 8 * (m - 10), 8 * (m - 9))
                elif m in (12, 14):
                    kd = (m - 12) // 2
                    dve.wait_ge(ev_act, j + 1)
                    for g in range(NKV):
                        rows = slice(HD * g, HD * g + HD)
                        for e in range(2):
                            last = V.tensor_tensor(k_l[HD * e:HD * e + HD, kd, g, :], pp[rows, :],
                                                   k_h[rows, kd, g, :].bitcast(F32), ALU.subtract)
                    last.then_inc(ev_dve, 1)
                    conv_taps(0, 16 + 8 * kd, min(TAPS, 24 + 8 * kd))
                elif m in (6, 7, 8, 9):
                    h = 2 * (m - 6)
                    dve.wait_ge(ev_act, j + 1)
                    V.scalar_tensor_tensor(q_st[HD:P, h, :], pp[0:HD, :], HD ** -0.5, q_st[0:HD, h, :].bitcast(F32),
                                           ALU.mult, ALU.subtract)
                    V.scalar_tensor_tensor(q_st[0:HD, h + 1, :], pp[HD:P, :], HD ** -0.5, q_st[HD:P, h + 1, :].bitcast(F32),
                                           ALU.mult, ALU.subtract).then_inc(ev_dve, 1)
                    conv_taps(1, 8 * (m - 6), min(TAPS, 8 * (m - 5)))
                if j + 2 < N_OUT:
                    w_lo(j + 2)
            dve.drain().then_inc(end["dve"], 1)
            for n in ("pe", "act"):
                dve.wait_ge(end[n], 1)

            fbc = [0]

            def chained(ins, s=fb["rb"]):
                fbc[0] += 1
                ins.then_inc(s, 1)
                dve.wait_ge(s, fbc[0])

            R = slice(0, 3 * NBUCKET)
            chained(V.memset(relb[96:97, :], NEG))
            chained(V.tensor_copy(rhm[R, 0, :], rb[R, :]))
            chained(V.tensor_tensor(rb1[R, :], rb[R, :], rhm[R, 0, :], ALU.subtract))
            chained(V.tensor_copy(rhm[R, 1, :], rb1[R, :]))
            chained(V.tensor_tensor(rb2[R, :], rb1[R, :], rhm[R, 1, :], ALU.subtract))
            chained(V.tensor_copy(relb[0:32, :], rhm[0:32, 0, :]))
            chained(V.tensor_copy(relb[32:64, :], rhm[32:64, 1, :]))
            V.tensor_copy(relb[64:96, :], rb2[64:96, :]).then_inc(fb["relb"], 1)
            for kv in range(2):
                for j in range(16):
                    last = V.tensor_scalar(cm[kv][:, j, :, :], c_st[kv][:, :, 2 * j:2 * j + CMP_STRIDE * (NCMP - 1) + 1:CMP_STRIDE],
                                           smc(("pos_k", "pos_v")[kv], j), None, ALU.add)
                last.then_inc(fb["cm"], 1)
            V.memset(kc_h[:, :, NCMP:CPAD].bitcast(F32), 0.0).then_inc(fb["chain"], 1)
            V.memset(kc_l[:, :, NCMP:CPAD].bitcast(F32), 0.0).then_inc(fb["chain"], 1)
            for c in range(2):
                dve.wait_ge(fb["pool_h"], c + 1)
                V.scalar_tensor_tensor(hT_l[:, c, :], pair(3 - c), smc("pool_scale", c), hT_h[:, c, :].bitcast(F32),
                                       ALU.mult, ALU.subtract).then_inc(fb["pool_l"], 1)
            dve.wait_ge(fb["mean"], 1)
            for c in range(2):
                V.tensor_tensor(ca[:, c, :], ca[:, c, :], pair(0), ALU.subtract).then_inc(fb["dev"], 1)
            dve.wait_ge(fb["kc_h"], 1)
            V.tensor_tensor(kc_l[:, :, 0:NCMP], ps[:, 4, 0:126].rearrange("p (g c) -> p g c", g=NKV),
                            kc_h[:, :, 0:NCMP].bitcast(F32), ALU.subtract).then_inc(fb["kc_l"], 1)
            dve.wait_ge(fb["sd"], 1)
            V.reciprocal(ctmp[:, :], cln[:, :]).then_inc(fb["chain"], 1)
            dve.wait_ge(fb["chain"], 3)
            for c in range(2):
                V.tensor_tensor(ca[:, c, :], ca[:, c, :], ctmp[:, :], ALU.mult).then_inc(fb["chain"], 1)
                dve.wait_ge(fb["chain"], 4 + c)
            for c in range(2):
                V.tensor_scalar(ca[:, c, :], ca[:, c, :], smc("ln_g", c), smc("ln_b", c), ALU.mult, ALU.add).then_inc(fb["z"], 1)
            for c in range(2):
                e = ctmp if c == 0 else cln
                dve.wait_ge(fb["ez"], c + 1)
                V.tensor_scalar(e[:, :], e[:, :], 1.0, None, ALU.add).then_inc(fb["chain"], 1)
                dve.wait_ge(fb["chain"], 6 + 2 * c)
                V.reciprocal(e[:, :], e[:, :]).then_inc(fb["chain"], 1)
                dve.wait_ge(fb["chain"], 7 + 2 * c)
                V.tensor_tensor(ca[:, c, :], ca[:, c, :], e[:, :], ALU.mult).then_inc(fb["silu"], 1)
            for m in range(2):
                dve.wait_ge(fb["pw_h"], m + 1)
                V.tensor_tensor(hT_l[:, 2 + m, :], pair(3 - 2 * m), hT_h[:, 2 + m, :].bitcast(F32),
                                ALU.subtract).then_inc(fb["pw_l"], 1)
            dve.drain().then_inc(end["dve"], 1)
            for n in ("pe", "act"):
                dve.wait_ge(end[n], 2)

            step = [0]

            def link(ins):
                step[0] += 1
                ins.then_inc(at_["chain"], 1)
                dve.wait_ge(at_["chain"], step[0])

            def row_max(s, r):
                i, g, kind = SUB[s]
                n = s * QPK + r
                h = QPK * g + r
                sc = pair(n % 2)
                w = width(i, kind)
                near = min(w, NEAR)
                far = w - near
                dve.wait_ge(at_["qk"], n + 1)
                if n >= 2:
                    dve.wait_ge(at_["exp"], n - 1)
                init = -3.0e38
                if kind == 1 and w == 5 * P:
                    link(V.tensor_tensor_reduce(sc[:, 0:3 * P], sc[:, 0:3 * P], wm[:, :], 1.0, -3.0e38, ALU.add, ALU.max, mx[:, n % 2:n % 2 + 1]))
                    init = mx[:, n % 2:n % 2 + 1]
                elif far:
                    link(V.tensor_reduce(mx[:, n % 2:n % 2 + 1], sc[:, 0:far], AX.X, ALU.max))
                    init = mx[:, n % 2:n % 2 + 1]
                ins = V.tensor_tensor_reduce(sc[:, far:w], sc[:, far:w], tn[:, h, NEAR - near:NEAR], 1.0, init, ALU.add, ALU.max, mpos[:, n % 2, 0:1])
                if kind == 1:
                    cc = sc[:, 5 * P:5 * P + CPAD]
                    z0 = 56 - 8 * i
                    ins = V.tensor_tensor_reduce(cc, cc, tc[:, h, z0:z0 + CPAD], 1.0, -3.0e38, ALU.add, ALU.max, mpos[:, n % 2, 1:2])
                link(ins)
                nk = 1 + kind
                V.tensor_scalar(nmx[:, n % 2, 0:nk], mpos[:, n % 2, 0:nk], -1.0, None, ALU.mult).then_inc(at_["max"], 1)

            def scale_row(s, r):
                i, g, kind = SUB[s]
                h = QPK * g + r
                dve.wait_ge(at_["exp"], s * QPK + r + 1)
                w = width(i, kind)
                if kind == 0:
                    link(V.reciprocal(rsum[:, r, 1:2], sums[:, r, 1:2]))
                    V.tensor_scalar(p_sel[:, r, 0:w], p_sel[:, r, 0:w], rsum[:, r, 1:2], gates[:, i, 3 * h + 1:3 * h + 2],
                                    ALU.mult, ALU.mult).then_inc(at_["pn"], 1)
                else:
                    link(V.reciprocal(rsum[:, r, 0:3], sums[:, r, 0:3]))
                    V.tensor_scalar(p_win[:, r, 0:w], p_win[:, r, 0:w], rsum[:, r, 2:3], gates[:, i, 3 * h + 2:3 * h + 3],
                                    ALU.mult, ALU.mult)
                    cc = p_win[:, r, 5 * P:5 * P + CPAD]
                    V.tensor_scalar(cc, cc, rsum[:, r, 0:1], gates[:, i, 3 * h:3 * h + 1], ALU.mult, ALU.mult).then_inc(at_["pn"], 1)

            def output_lo(unit):
                i, g = unit // NKV, unit % NKV
                dve.wait_ge(at_["o_h"], unit + 1)
                o = ps[0:HD, 6 + unit % 2, :].rearrange("p (c e q) -> p c e q", e=2, q=P)
                for e in range(2):
                    dst = (slice(HD * e, HD * e + HD), slice(4 + 2 * g, 6 + 2 * g), slice(i * P, (i + 1) * P))
                    last = V.tensor_tensor(hT_l[dst], o[:, :, e, :], hT_h[dst].bitcast(F32), ALU.subtract)
                last.then_inc(at_["o_l"], 1)

            dve.wait_ge(wm_in, 16)
            for s in range(-1, len(SUB)):
                rows = QPK if s + 1 < len(SUB) else 0
                for r in range(rows):
                    row_max(s + 1, r)
                    if r >= 1:
                        scale_row(s + 1, r - 1)
                if rows:
                    scale_row(s + 1, QPK - 1)
                if s >= 2 and s % 2 == 0:
                    output_lo(s // 2 - 1)
            output_lo(len(SUB) // 2 - 1)
            dve.drain().then_inc(end["dve"], 1)
            for n in ("pe", "act"):
                dve.wait_ge(end[n], 3)

            def block_out(s, split_next):
                b = bo[s]
                dve.wait_ge(b["gain"], 32)
                for t in range(NT + 1):
                    if t < NT:
                        u = upd[t % 2][:, :]
                        dve.wait_ge(b["rs"], t + 1)
                        if t >= 2:
                            dve.wait_ge(b[f"st{t % 2}"], 16 * (t // 2))
                        V.scalar_tensor_tensor(u, pair(t % 2), rsb[:, 0, t % 2:t % 2 + 1], gain_post[:, :],
                                               ALU.mult, ALU.mult).then_inc(b["up"], 1)
                        dve.wait_ge(b["up"], t + 1)
                        dve.wait_ge(b[f"res{t % 2}"], 16 * (t // 2 + 1))
                        V.tensor_tensor(u, u, res[t % 2][:, :], ALU.add).then_inc(b["x"], 1)
                    if t >= 1:
                        dve.wait_ge(b["hh"], t)
                        ts = slice((t - 1) * P, t * P)
                        V.tensor_tensor(hT_l[:, :, ts], pair(2 + (t - 1) % 2).rearrange("p (k c) -> p k c", k=KC),
                                        hT_h[:, :, ts].bitcast(F32), ALU.subtract).then_inc(b["hl"], 1)
                    if t < NT:
                        dve.wait_ge(b["rs2"], t + 1)
                        if t >= 2:
                            dve.wait_ge(b["tr"], t - 1)
                        V.scalar_tensor_tensor(hn[t % 2][:, :], upd[t % 2][:, :], rsb[:, 1, t % 2:t % 2 + 1], gain_pre[:, :],
                                               ALU.mult, ALU.mult).then_inc(b["hn"], 1)
                        if split_next and t == NT - 1:
                            w_lo(N_Q)
                            w_lo(N_Q + 1)

            for k in range(KC):
                w_lo(N_OUT + k)
            block_out(0, True)
            dve.drain().then_inc(end["dve"], 1)
            for n in ("pe", "act"):
                dve.wait_ge(end[n], 4)
            for m in range(2, 8):
                w_lo(N_Q + m)
            dve.drain().then_inc(end["dve"], 1)
            for n in ("pe", "act"):
                dve.wait_ge(end[n], 5)

            xstep = [0]

            def x_link(ins):
                xstep[0] += 1
                ins.then_inc(xa["chain"], 1)
                dve.wait_ge(xa["chain"], xstep[0])

            for t in range(NT + 2):
                if t < NT:
                    dve.wait_ge(xa["s"], t + 1)
                    V.tensor_reduce(xs[:, 0, :], pair(t % 2).rearrange("p (h m) -> p h m", h=XH), AX.X, ALU.max,
                                    negate=True).then_inc(xa["max"], 1)
                    dve.wait_ge(xa["exp"], XH * (t + 1))
                    x_link(V.reciprocal(xs[:, 2, :], xs[:, 1, :]))
                    for h in range(XH):
                        last = V.tensor_scalar(xp[t % 2][:, h, :], xp[t % 2][:, h, :], xs[:, 2, h:h + 1], None, ALU.mult)
                    last.then_inc(xa["pn"], 1)
                if t >= 2:
                    dve.wait_ge(xa["oh"], t - 1)
                    ts = slice((t - 2) * P, (t - 1) * P)
                    V.tensor_tensor(hT_l[:, :, ts], pair(3).rearrange("p (k c) -> p k c", k=KC), hT_h[:, :, ts].bitcast(F32),
                                    ALU.subtract).then_inc(xa["ol"], 1)
                if t < NT:
                    w_lo(N_O + t)
            dve.drain().then_inc(end["dve"], 1)
            for n in ("pe", "act"):
                dve.wait_ge(end[n], 6)
            block_out(1, False)
            dve.drain().then_inc(end["dve"], 1)
            for n in ("pe", "act"):
                dve.wait_ge(end[n], 7)

            for q in range(4):
                V.memset(acc[:, 2 * q:2 * q + 2, :], 0.0).then_inc(ml["acc"], 1)
            dve.wait_ge(ml["acc"], 4)
            dve.sem_inc(ml["hl"], 2)

            def w_lo_mlp(g, c):
                n = N_MLP + c
                dve.wait_ge(wh_done, g * 8 + (n + 1))
                if c < GROUP:
                    j = J_MLP + c
                    hi, lo = (w[j % 2][:, :, :].rearrange("p k n -> p (k n)") for w in (tw_h, tw_l))
                else:
                    hi, lo = w2_h[:, c - GROUP, :], w2_l[:, c - GROUP, :]
                V.tensor_tensor(lo, wraw[n % 2][:, :], hi.bitcast(F32), ALU.subtract).then_inc(wl_done, 1)

            def hidden_lo(g, c):
                dve.wait_ge(ml["hh"], g * GROUP + (c + 1))
                V.tensor_tensor(hid_l[:, c, :], rl[c % 2][:, :], hid_h[:, c, :].bitcast(F32), ALU.subtract).then_inc(ml["hl"], 1)

            with dve.Fori(0, NGROUP) as g:
                w_lo_mlp(g, 0)
                w_lo_mlp(g, 1)
                hidden_lo(g, 0)
                w_lo_mlp(g, 2)
                hidden_lo(g, 1)
                w_lo_mlp(g, 3)
                hidden_lo(g, 2)
                w_lo_mlp(g, 4)
                w_lo_mlp(g, 5)
                hidden_lo(g, 3)
                w_lo_mlp(g, 6)
                w_lo_mlp(g, 7)
                for idx in range(2 * NT):
                    t, hf = idx // 2, idx % 2
                    o = acc[:, t, hf * HALF:(hf + 1) * HALF]
                    dve.wait_ge(ml["dn"], g * (2 * NT) + (idx + 2))
                    V.tensor_tensor(o, o, ps[:, 4 + idx % 4, :], ALU.add).then_inc(ml["acc"], 1)
            dve.wait_ge(ml["gain"], 16)
            for t in range(NT):
                u = upd_f[t % 2][:, :]
                dve.wait_ge(ml["rs"], t + 1)
                if t >= 2:
                    dve.wait_ge(ml[f"st{t % 2}"], 16 * (t // 2))
                V.scalar_tensor_tensor(u, acc[:, t, :], rsb[:, 0, t % 2:t % 2 + 1], gain_f[:, :], ALU.mult,
                                       ALU.mult).then_inc(ml["y"], 1)
                dve.wait_ge(ml["y"], t + 1)
                dve.wait_ge(ml[f"res{t % 2}"], 16 * (t // 2 + 1))
                V.tensor_tensor(u, u, res_f[t % 2][:, :], ALU.add).then_inc(ml["fin"], 1)


def kernel(**inputs):
    import concourse.bacc as _bacc
    from concourse.bass_utils import run_bass_kernel_spmd as _run

    c = np.ascontiguousarray
    v = {n: np.asarray(x) for n, x in inputs.items()}

    def chunks(w):
        return c(w.reshape(KC, P, -1, P).transpose(2, 1, 0, 3))

    def cols(w):
        return w.reshape(2, P).T

    w_in = v["w_in"][0]
    small = np.zeros((P, SMW), np.float32)

    def put(name, x):
        small[:, SM[name][0]:SM[name][1]] = x

    put("conv_w", v["conv_w"][0].T.reshape(2, P, TAPS).transpose(1, 0, 2).reshape(P, 2 * TAPS))
    put("conv_b", cols(v["conv_b"][0]))
    put("ln_g", cols(v["conv_ln_g"][0]))
    put("ln_b", cols(v["conv_ln_b"][0]))
    put("pool_scale", cols(v["pool_scale"][0]))
    put("pos_k", v["cmp_k_pos"][0].reshape(16, P).T)
    put("pos_v", v["cmp_v_pos"][0].reshape(16, P).T)
    win = np.repeat(np.array([[2, 8], [4, 16]], np.float32), HD, axis=0)
    put("inv_win", 1 / win)
    put("inv16", (1 / np.minimum(np.arange(1, 17, dtype=np.float32), win[:, :, None])).reshape(P, 32))
    put("valid", (np.arange(P)[:, None] >= CMP_LEN - 1).astype(np.float32))
    put("eps", EPS)
    pool_w = np.zeros((P, 2, P), np.float32)
    for g in range(4):
        r = slice(HD * (g % 2), HD * (g % 2) + HD)
        pool_w[r, g // 2, r] = v["pool_w"][0, g]
    d = np.arange(ND) + DMIN
    n = np.maximum(d, 1).astype(np.float32)
    large = MAX_EXACT + (np.log(n / MAX_EXACT) / math.log(MAX_DIST / MAX_EXACT) * (NBUCKET - MAX_EXACT)).astype(np.int32)
    bucket = np.where(d < MAX_EXACT, np.maximum(d, 0), np.minimum(large, NBUCKET - 1))
    hot = (np.arange(NBUCKET)[:, None] == bucket).astype(np.float32)
    hot[NBUCKET - 1] -= 1.0
    hot *= d >= 0
    onehot = np.concatenate([hot, hot, hot, (d < 0)[None].astype(np.float32)])
    q, x = np.arange(P)[:, None], np.arange(3 * P)[None, :]
    arrays = {
        "x": c(v["x"][0]), "mem": c(v["mem"][0]), "rel_bias": v["rel_bias"],
        "in": chunks(w_in[:, :2048]), "w_gate": c(w_in[:, 2048:].reshape(KC, P, 24).transpose(1, 0, 2)),
        "wout": v["w_out"][0], "wq": chunks(v["xa_wq"][0]), "wk": chunks(v["xa_wk"][0]), "wv": chunks(v["xa_wv"][0]),
        "wo": v["xa_wo"][0], "w1": chunks(v["mlp_w1"][0]), "w2": c(v["mlp_w2"][0].reshape(FF // P, P, D)),
        "pool_w": pool_w, "small": small, "conv_pw": v["conv_pw"][0],
        "cmp_k_w1": v["cmp_k_w1"][0], "cmp_k_w2": v["cmp_k_w2"][0], "cmp_v_w1": v["cmp_v_w1"][0], "cmp_v_w2": v["cmp_v_w2"][0],
        "onehot": onehot, "ident": np.eye(P, dtype=np.float32),
        "winmask": np.where((x < P) & (x <= q), np.float32(NEG), np.float32(0)),
    }
    for g in ("mix_pre_g", "mix_post_g", "xa_pre_g", "xa_post_g", "mem_g", "mlp_pre_g", "mlp_post_g"):
        arrays[g] = c(v[g][0])
    nc = _bacc.Bacc("TRN2", target_bir_lowering=False, num_devices=1)
    aps = {k: nc.dram_tensor("in_" + k, w.shape, mybir.dt.from_np(w.dtype), kind="ExternalInput").ap() for k, w in arrays.items()}
    for k, shape in (("x1", (SEQ, D)), ("x2", (SEQ, D)), ("kmd", (P, KC, MEM)), ("vmd", (P, MT, D))):
        aps[k] = nc.dram_tensor(k, shape, F32, kind="Internal").ap()
    aps["out"] = nc.dram_tensor("out", (SEQ, D), F32, kind="ExternalOutput").ap()
    hybrid_layer(nc, aps)
    r = _run(nc, [{"in_" + k: w for k, w in arrays.items()}], core_ids=[0])
    return r.results[0]["out"].reshape(1, SEQ, D)
```

```python
import math
import numpy as np
import concourse.bass as bass
from concourse import mybir

F32 = mybir.dt.float32
F32R = mybir.dt.float32r
BF16 = mybir.dt.bfloat16
ALU = mybir.AluOpType
ACT = mybir.ActivationFunctionType
AX = mybir.AxisListType

P = 128
SEQ, D = 1024, 1024
NT, KC = SEQ // P, D // P
MEM = 256
MT = MEM // P
HALF = 512
HD = 64
NH, NKV, QPK = 8, 2, 4
NCMP, CMP_STRIDE, CMP_LEN = 63, 16, 32
CPAD = 64
WIDE = 2 * P
KCW = CPAD * (NKV - 1) + WIDE
WIN_TILES = 512 // P
NEAR = 2 * P
TAPS = 31
CMP_HID = 256
XH = 4
FF = 4096
GROUP = 4
NGROUP = FF // P // GROUP
NBUCKET, MAX_EXACT, MAX_DIST = 32, 16, 128
NEG = -1e30
EPS = 1e-6
DMIN = -(CMP_STRIDE * (CPAD - 1) + CMP_LEN - 1)
ND = 992 - DMIN + 1
ZC = 120
OHR = 97

SM = {}
_at = 0
for _n, _w in (("conv_w", 2 * TAPS), ("conv_b", 2), ("ln_g", 2), ("ln_b", 2), ("pool_scale", 2),
               ("pos_k", 16), ("pos_v", 16), ("inv_win", 2), ("inv16", 32), ("valid", 1), ("eps", 1)):
    SM[_n] = (_at, _at + _w)
    _at += _w
SMW = _at

T_MEM = [("wk", m) for m in range(8)] + [("wv", m) for m in range(8)]
T_IN = [("in", m) for m in (2, 4, 3, 5, 0, 1, 13, 15, 16, 10, 11, 12, 14, 6, 7, 8, 9)]
TOK = (13, 15, 16)
T_Q = [("wq", m) for m in range(8)]
PIECES = T_MEM + T_IN + [("wout", k) for k in range(8)] + T_Q + [("wo", k) for k in range(8)]
N_IN = len(T_MEM)
N_OUT = N_IN + len(T_IN)
N_Q = N_OUT + 8
N_O = N_Q + 8
N_MLP = N_O + 8
J_Q = len(T_MEM) + len(T_IN)
J_MLP = J_Q + 8


POOL_STEPS = 24
CONV_PLAN = [0, 4, 9, 9, 9, 17, 25, 31, 37, 42, 45, 48, 52, 56, 60, 62]


def hybrid_layer(nc, a):
    def at(name, shape, dt, kb):
        return nc.alloc_sbuf_tensor_at(name, shape, dt, offset=BASE + int(kb * 1024))

    BASE = -(-nc.sbuf_base // 32) * 32
    hT_h = at("hT_h", [P, KC, SEQ], F32R, 0)
    hT_l = at("hT_l", [P, KC, SEQ], F32R, 32)
    cw1 = [at("cw1_k", [P, 16, CMP_HID], F32, 16), at("cw1_v", [P, 16, CMP_HID], F32, 48)]
    x_in = [at(f"x_in{s}", [P, D], F32, 64 + 4 * s) for s in range(2)]
    hn0 = [at(f"hn0{s}", [P, D], F32, 72 + 4 * s) for s in range(2)]
    gain_x = at("gain_x", [P, D], F32, 80)
    gain_m = at("gain_m", [P, D], F32, 84)
    mT_h = at("mT_h", [P, KC, MEM], F32R, 88)
    mT_l = at("mT_l", [P, KC, MEM], F32R, 96)
    km0 = at("km0", [P, KC, MEM], F32, 104)
    vm0 = at("vm0", [P, MT, D], F32, 112)
    junk0 = at("junk0", [P, D], F32, 120)
    vmt = [at(f"vmt{s}", [P, MEM], F32, 124 + s) for s in range(2)]
    tokT = [at(f"tokT{s}", [P, SEQ], F32, 84 + 4 * s) for s in range(3)]
    pool_a = at("pool_a", [P, SEQ], F32, 64)
    pool_b = at("pool_b", [P, SEQ], F32, 68)
    sig = at("sig", [P, SEQ], F32, 72)
    q_st = at("q_st", [P, NH, SEQ], F32R, 64)
    k_h = at("k_h", [P, 2, NKV, SEQ], F32R, 96)
    k_l = at("k_l", [P, 2, NKV, SEQ], F32R, 112)
    v_sw = at("v_sw", [P, NT, 2, P], F32, 128)
    c_st = [at("kc_st", [P, NKV, SEQ], F32, 136), at("vc_st", [P, NKV, SEQ], F32, 144)]
    pu = at("pu", [P, 2, SEQ], F32, 152)
    ch = at("ch", [P, 2, SEQ], F32, 160)
    ca = at("ca", [P, 2, SEQ], F32, 168)
    cm = [at("cm_k", [P, 16, NKV, NCMP], F32, 184), at("cm_v", [P, 16, NKV, NCMP], F32, 192)]
    ctmp = at("ctmp", [P, SEQ], F32, 176)
    cln = at("cln", [P, SEQ], F32, 180)
    tn = at("tn", [P, NH, NEAR], F32, 136)
    tc = at("tc", [P, NH, ZC], F32, 144)
    wm = at("wm", [P, 3 * P], F32, 194.5)
    p_sel = at("p_sel", [P, QPK, SEQ], F32, 148)
    p_win = at("p_win", [P, QPK, 5 * P + CPAD], F32, 164)
    v_st = at("v_st", [P, NT * 2 * NKV, 2 * HD], F32R, 176)
    pt_h = [at(f"pt_h{s}", [P, HALF], F32R, 128 + 2 * s) for s in range(3)]
    pt_l = [at(f"pt_l{s}", [P, HALF], F32R, (134, 196, 198)[s]) for s in range(3)]
    wb_h = at("wb_h", [P, KC, D], F32R, 64)
    wb_l = at("wb_l", [P, KC, D], F32R, 96)
    upd = [at(f"upd{s}", [P, D], F32, 128 + 4 * s) for s in range(2)]
    res = [at(f"res{s}", [P, D], F32, 136 + 4 * s) for s in range(2)]
    hn = [at(f"hn{s}", [P, D], F32, 144 + 4 * s) for s in range(2)]
    gain_post = at("gain_post", [P, D], F32, 152)
    gain_pre = at("gain_pre", [P, D], F32, 156)
    junk = at("junk", [P, D], F32, 160)
    xq = at("xq", [P, KC, SEQ], F32, 128)
    km = at("km", [P, KC, MEM], F32, 160)
    vm = at("vm", [P, MT, D], F32, 168)
    xp = [at(f"xp{s}", [P, XH, MEM], F32, 184 + 4 * s) for s in range(2)]
    xpt = [at(f"xpt{s}", [P, MT, XH, P], F32, 192 + 4 * s) for s in range(2)]
    acc = at("acc", [P, NT, D], F32, 64)
    hid_h = at("hid_h", [P, GROUP, SEQ], F32R, 96)
    hid_l = at("hid_l", [P, GROUP, SEQ], F32R, 112)
    w2_h = at("w2_h", [P, GROUP, D], F32R, 128)
    w2_l = at("w2_l", [P, GROUP, D], F32R, 144)
    rl = [at(f"rl{s}", [P, SEQ], F32, 160 + 4 * s) for s in range(2)]
    gain_f = at("gain_f", [P, D], F32, 168)
    junk_f = at("junk_f", [P, D], F32, 172)
    res_f = [at(f"res_f{s}", [P, D], F32, 176 + 4 * s) for s in range(2)]
    upd_f = [at(f"upd_f{s}", [P, D], F32, 160 + 4 * s) for s in range(2)]
    wraw = [at(f"wraw{s}", [P, D], F32, 176 + 4 * s) for s in range(2)]
    tw_h = [at(f"tw_h{s}", [P, KC, P], F32R, 184 + 8 * s) for s in range(2)]
    tw_l = [at(f"tw_l{s}", [P, KC, P], F32R, 188 + 8 * s) for s in range(2)]
    ident = at("ident", [P, P], F32, 200)
    ones = at("ones", [P, P], F32, 200.5)
    sm = at("sm", [P, SMW], F32, 201)
    gates = at("gates", [P, NT, 24], F32, 202)
    o_b = at("o_b", [HD, HALF], F32, 202.75)
    o_sum = at("o_sum", [P, 2, P], F32, 175)
    cw2k = at("cw2k", [P, 2, 2, HD], F32, 202.75)
    hid_c = at("hid_c", [P, 2, NKV * NCMP], F32, 203.75)
    kc_h = at("kc_h", [P, KCW], F32R, 192)
    kc_l = at("kc_l", [P, KCW], F32R, 193.25)
    vc = at("vc", [P, NKV, 2 * HD], F32R, 204.75)
    cw2v = at("cw2v", [P, 2, HD], F32, 206.25)
    half_neg = at("half_neg", [P, 16], F32, 206.75)
    ss = at("ss", [P, 10], F32, 206.875)
    rstd = at("rstd", [P, 10], F32, 206.9375)
    mx = at("mx", [P, 3], F32, 207)
    nmx = at("nmx", [P, 2, 2], F32, 207.0625)
    sums = at("sums", [P, 2, QPK, 3], F32, 205.75)
    rsum = at("rsum", [P, 2, QPK, 3], F32, 205.875)
    xs = at("xs", [P, 3, XH], F32, 207.3125)
    t16 = at("t16", [P, 16], F32, 207.375)
    ssb = at("ssb", [P, 2, 2], F32, 207.5)
    rsb = at("rsb", [P, 2, 2], F32, 207.5625)
    pw = at("pw", [P, 2, P], F32, 203.75)
    cpw = at("cpw", [P, 2, CMP_HID], F32, 44)
    oh = at("oh", [OHR, ND], BF16, 12)
    rb = at("rb", [3 * NBUCKET, NH], F32, 207.625)
    rb1 = at("rb1", [3 * NBUCKET, NH], F32, 207.65625)
    rb2 = at("rb2", [3 * NBUCKET, NH], F32, 207.6875)
    rhm = at("rhm", [3 * NBUCKET, 2, NH], BF16, 207.71875)
    relb = at("relb", [OHR, NH], BF16, 207.75)

    from contextlib import ExitStack
    ctx = ExitStack()
    with ctx:
        ps = ctx.enter_context(nc.psum_tensor("ps", [P, 8, HALF], F32))

        def sem(name):
            return ctx.enter_context(nc.semaphore(name))

        def pair(j):
            return ps[:, 2 * j:2 * j + 2, :].rearrange("p a b -> p (a b)")

        def smc(name, j=0, rows=slice(0, P)):
            return sm[rows, SM[name][0] + j:SM[name][0] + j + 1]

        raw_in = [sem("raw_in0"), sem("raw_in1")]
        wh_done, wl_done = sem("wh_done"), sem("wl_done")
        const_in, store0 = sem("const_in"), sem("store0")
        x_ld, mem_ld = [sem("x_ld0"), sem("x_ld1")], [sem("mem_ld0"), sem("mem_ld1")]
        ph_in, oh_in, wm_in, kv_in = sem("ph_in"), sem("oh_in"), sem("wm_in"), sem("kv_in")
        ss_n, rs_n, hn_n, tr_n, hh_n, hl_n, msq = (sem(n) for n in ("ss_n", "rs_n", "hn_n", "tr_n", "hh_n", "hl_n", "msq"))
        consts_set = sem("consts_set")
        gemm, ev_act, ev_dve, tok_tr, tok_ev = (sem(n) for n in ("gemm", "ev_act", "ev_dve", "tok_tr", "tok_ev"))
        sig_step, pool_step, conv_step = sem("sig_step"), sem("pool_step"), sem("conv_step")
        end = {n: sem("end_" + n) for n in ("pe", "act", "dve", "pool")}
        fb = {n: sem("fb_" + n) for n in (
            "rb", "relb", "tab", "tab_ev", "pool", "pool_h", "pool_l", "cm", "hid", "gelu", "kc", "kc_h", "kc_l",
            "vc", "vc_ev", "mean", "dev", "sq", "var", "sd", "z", "silu", "pw", "pw_h", "pw_l", "chain")}
        at_ = {n: sem("at_" + n) for n in (
            "qk", "chain", "max", "exp", "rs", "pn", "tr", "v_h", "v_l", "pt_h", "pt_l", "pv", "o_b", "o_sum", "o_h", "o_l")}
        bo = [{n: sem(f"bo{s}_" + n) for n in (
            "mm", "ss", "rs", "up", "x", "ss2", "rs2", "hn", "tr", "hh", "hl", "res0", "res1", "gain", "st0", "st1",
            "sq", "psq")}
            for s in range(2)]
        xa = {n: sem("xa_" + n) for n in ("q_ev", "s", "max", "exp", "pn", "tr", "pt", "pv", "oh", "ol", "chain")}
        ml = {n: sem("ml_" + n) for n in ("up", "relu", "sq", "hh", "hl", "dn", "acc", "ss", "rs", "y", "gain", "res0",
                                          "res1", "st0", "st1", "fin", "psq")}

        x_t = a["x"].rearrange("(t p) d -> t p d", p=P)
        x1_t = a["x1"].rearrange("(t p) d -> t p d", p=P)
        x2_t = a["x2"].rearrange("(t p) d -> t p d", p=P)
        out_t = a["out"].rearrange("(t p) d -> t p d", p=P)
        mem_t = a["mem"].rearrange("(t p) d -> t p d", p=P)

        def w_dram(name, c):
            if name in ("wout", "wo"):
                return a[name][c * P:(c + 1) * P, :]
            return a[name][c].rearrange("p k n -> p (k n)")

        def t_index(n):
            if n < N_OUT:
                return n
            return J_Q + n - N_Q if N_Q <= n < N_O else None

        def w_dest(n):
            j = t_index(n)
            if j is None:
                k = PIECES[n][1]
                return wb_h[:, k, :], wb_l[:, k, :]
            return (tw_h[j % 2][:, :, :].rearrange("p k n -> p (k n)"),
                    tw_l[j % 2][:, :, :].rearrange("p k n -> p (k n)"))

        READS = [PIECES[j][0] == "in" and PIECES[j][1] in (10, 11, 12, 14, 6, 7, 8, 9) for j in range(N_OUT)]

        def dve_reads(j):
            return sum(READS[:j + 1])

        TOK_AT = [j for j in range(N_OUT) if (8 <= j < N_IN) or (j >= N_IN and PIECES[j][1] in TOK)]

        SUB = [(i, g, kind) for i in range(NT) for g in range(NKV) for kind in (0, 1)]

        def tiles_of(s):
            i, _, kind = SUB[s]
            return i + 1 if kind == 0 else min(WIN_TILES + 1, i + 1) + 1

        def attention_order():
            n = len(SUB)
            out = [("row", 0, r) for r in range(QPK)]
            for s in range(n):
                tiles = tiles_of(s)
                before = [r * max(0, tiles - 2) // 3 for r in range(QPK)] if s + 1 < n else []
                for t in range(tiles + 1):
                    out += [("row", s + 1, r) for r, u in enumerate(before) if u == t]
                    if t < tiles:
                        out.append(("tile", s, t))
            return out

        ORDER = attention_order()
        TAKE, FINISH = {}, {}
        for _u in range(1, len(SUB) // 2):
            _tiles = [e for e in ORDER if e[0] == "tile" and e[1] >= 2 * _u]
            TAKE[_tiles[2]] = FINISH[_tiles[3]] = _u - 1

        TILE0 = [sum(tiles_of(s) for s in range(k)) for k in range(len(SUB) + 1)]

        def width(i, kind):
            return P * (i + 1) if kind == 0 else P * min(WIN_TILES + 1, i + 1)

        def row_at(i, kind):
            w = width(i, kind)
            return HALF - WIDE if w == 5 * P else (HALF if kind == 1 else 0)

        block = ctx.enter_context(nc.Block())

        @block.sync
        def _(sp):
            for n in range(N_MLP):
                if n == N_OUT:
                    sp.wait_ge(end["pe"], 3)
                if n >= 2:
                    sp.wait_ge(wl_done, n - 1)
                sp.dma_start(wraw[n % 2][:, :], w_dram(*PIECES[n])).then_inc(raw_in[n % 2], 16)

            def mlp_piece(g, c, w):
                n = N_MLP + c
                sp.wait_ge(wl_done, g * 8 + (n - 1))
                sp.dma_start(wraw[n % 2][:, :], w).then_inc(raw_in[n % 2], 16)

            with sp.Fori(0, NGROUP) as g:
                for c in range(GROUP):
                    mlp_piece(g, c, a["w1"][bass.ds(g * GROUP + c, 1)].rearrange("a p k n -> p (a k n)"))
                for c in range(GROUP):
                    mlp_piece(g, GROUP + c, a["w2"][bass.ds(g * GROUP + c, 1)].rearrange("a p n -> p (a n)"))

        @block.gpsimd
        def _(pool):
            pool.dma_start(gain_m[:, :], a["mem_g"].partition_broadcast(P)).then_inc(const_in, 16)
            pool.dma_start(gain_x[:, :], a["mix_pre_g"].partition_broadcast(P)).then_inc(const_in, 16)
            pool.dma_start(ident[:, :], a["ident"]).then_inc(const_in, 16)
            pool.dma_start(sm[:, :], a["small"]).then_inc(const_in, 16)
            pool.dma_start(pw[:, :, :], a["pool_w"]).then_inc(const_in, 16)
            for s in range(2):
                pool.dma_start(cw2k[:, :, s, :], a["cmp_k_w2"].rearrange("(t p) n -> p t n", p=P)).then_inc(const_in, 16)
            pool.dma_start(cw2v[:, :, :], a["cmp_v_w2"].rearrange("(t p) n -> p t n", p=P)).then_inc(const_in, 16)
            for s in range(3):
                pool.dma_start(rb[32 * s:32 * s + 32, :], a["rel_bias"]).then_inc(const_in, 16)
            pool.memset(half_neg[:, :], -0.5).then_inc(consts_set, 1)
            pool.memset(ones[:, :], 1.0 / 256).then_inc(consts_set, 1)
            pool.wait_ge(consts_set, 2)

            def inv_rms(src, dst, ready, chain, n, done):
                pool.wait_ge(ready[0], ready[1])
                pool.tensor_scalar(src, src, 1.0 / D, EPS, ALU.mult, ALU.add).then_inc(chain, 1)
                pool.wait_ge(chain, n)
                pool.tensor_tensor(dst, src, half_neg[:, 0:1], ALU.pow).then_inc(done, 1)

            for u in range(MT + NT):
                inv_rms(ss[:, u:u + 1], rstd[:, u:u + 1], (ss_n, u + 1), msq, u + 1, rs_n)
                if u + 2 < MT + NT:
                    pool.wait_ge(hn_n, u + 1)
                    pool.dma_start(x_in[u % 2][:, :], x_t[u + 2 - MT]).then_inc(x_ld[u % 2], 16)
            pool.wait_ge(ev_act, 8)
            pool.wait_ge(tok_ev, 8)
            pool.dma_start(a["kmd"], km0[:, :, :]).then_inc(store0, 16)
            pool.dma_start(a["vmd"], vm0[:, :, :]).then_inc(store0, 16)
            pool.wait_ge(store0, 32)

            pool.wait_ge(end["pe"], 1)
            pool.dma_start(oh[:, :], a["onehot"]).then_inc(oh_in, 16)
            pool.dma_start(cw1[0][:, :, :], a["cmp_k_w1"].rearrange("(j p) n -> p j n", p=P)).then_inc(ph_in, 16)
            pool.dma_start(cw1[1][:, :, :], a["cmp_v_w1"].rearrange("(j p) n -> p j n", p=P)).then_inc(ph_in, 16)
            pool.dma_start(cpw[:, :, :], a["conv_pw"].rearrange("(t p) n -> p t n", p=P)).then_inc(ph_in, 16)
            for n in ("pe", "act", "dve"):
                pool.wait_ge(end[n], 2)
            pool.dma_start(wm[:, :], a["winmask"]).then_inc(wm_in, 16)

            for what, s, r in ORDER:
                if what == "row":
                    i, g, kind = SUB[s]
                    h, w = QPK * g + r, width(i, kind)
                    c = rsum[:, kind, r, :]
                    pool.wait_ge(at_["rs"], s * QPK + r + 1)
                    if kind == 0:
                        pool.tensor_scalar(p_sel[:, r, 0:w], p_sel[:, r, 0:w], c[:, 1:2], gates[:, i, 3 * h + 1:3 * h + 2],
                                           ALU.mult, ALU.mult).then_inc(at_["pn"], 1)
                    else:
                        pool.tensor_scalar(p_win[:, r, 0:w], p_win[:, r, 0:w], c[:, 2:3], gates[:, i, 3 * h + 2:3 * h + 3],
                                           ALU.mult, ALU.mult)
                        cc = p_win[:, r, 5 * P:5 * P + CPAD]
                        pool.tensor_scalar(cc, cc, c[:, 0:1], gates[:, i, 3 * h:3 * h + 1], ALU.mult, ALU.mult)\
                            .then_inc(at_["pn"], 1)

            def block_out(s, src, dst, last_phase):
                b = bo[s]
                for n in ("pe", "act", "dve"):
                    pool.wait_ge(end[n], last_phase)
                pool.dma_start(gain_post[:, :], a[("mix_post_g", "xa_post_g")[s]].partition_broadcast(P)).then_inc(b["gain"], 16)
                pool.dma_start(gain_pre[:, :], a[("xa_pre_g", "mlp_pre_g")[s]].partition_broadcast(P)).then_inc(b["gain"], 16)
                for t in range(2):
                    pool.dma_start(res[t][:, :], src[t]).then_inc(b[f"res{t}"], 16)
                for t in range(NT):
                    inv_rms(ssb[:, 0, t % 2:t % 2 + 1], rsb[:, 0, t % 2:t % 2 + 1], (b["ss"], t + 1), b["sq"], 2 * t + 1, b["rs"])
                    inv_rms(ssb[:, 1, t % 2:t % 2 + 1], rsb[:, 1, t % 2:t % 2 + 1], (b["ss2"], t + 1), b["sq"], 2 * t + 2, b["rs2"])
                    pool.dma_start(dst[t], upd[t % 2][:, :]).then_inc(b[f"st{t % 2}"], 16)
                    if t + 2 < NT:
                        pool.dma_start(res[t % 2][:, :], src[t + 2]).then_inc(b[f"res{t % 2}"], 16)
                for t in range(2):
                    pool.wait_ge(b[f"st{t}"], 16 * (NT // 2))

            block_out(0, x_t, x1_t, 3)
            for n in ("pe", "act", "dve"):
                pool.wait_ge(end[n], 4)
            pool.dma_start(km[:, :, :], a["kmd"]).then_inc(kv_in, 16)
            pool.dma_start(vm[:, :, :], a["vmd"]).then_inc(kv_in, 16)
            block_out(1, x1_t, x2_t, 6)

            for n in ("pe", "act", "dve"):
                pool.wait_ge(end[n], 7)
            pool.dma_start(gain_f[:, :], a["mlp_post_g"].partition_broadcast(P)).then_inc(ml["gain"], 16)
            pool.wait_ge(wl_done, N_MLP + 8 * NGROUP)
            for t in range(2):
                pool.dma_start(res_f[t][:, :], x2_t[t]).then_inc(ml[f"res{t}"], 16)
            for t in range(NT):
                inv_rms(ssb[:, 0, t % 2:t % 2 + 1], rsb[:, 0, t % 2:t % 2 + 1], (ml["ss"], t + 1), ml["psq"], t + 1, ml["rs"])
                pool.wait_ge(ml["fin"], t + 1)
                pool.dma_start(out_t[t], upd_f[t % 2][:, :]).then_inc(ml[f"st{t % 2}"], 16)
                if t + 2 < NT:
                    pool.dma_start(res_f[t % 2][:, :], x2_t[t + 2]).then_inc(ml[f"res{t % 2}"], 16)
            for t in range(2):
                pool.wait_ge(ml[f"st{t}"], 16 * (NT // 2))

        def three_pass(pe, out, lh, ll, rh, rl_, first, last):
            nc.tensor.matmul(out, lh, rh, start=first, stop=False)
            nc.tensor.matmul(out, lh, rl_, start=False, stop=False)
            return nc.tensor.matmul(out, ll, rh, start=False, stop=last)

        def t_product(pe, j, rh, rl_, out, cols):
            for c0 in range(0, cols, HALF):
                w = min(HALF, cols - c0)
                for k in range(KC):
                    last = three_pass(pe, out[:, c0:c0 + w], tw_h[j % 2][:, k, :], tw_l[j % 2][:, k, :],
                                      rh[:, k, c0:c0 + w], rl_[:, k, c0:c0 + w], k == 0, k == KC - 1)
            return last

        def t_product_half(pe, j, out, hf):
            cs = slice(hf * HALF, (hf + 1) * HALF)
            return t_product(pe, j, hT_h[:, :, cs], hT_l[:, :, cs], out[:, cs], HALF)

        def n_product(pe, lh, ll, rh, rl_, out):
            for k in range(KC):
                last = three_pass(pe, out, lh[:, k], ll[:, k], rh[:, k], rl_[:, k], k == 0, k == KC - 1)
            return last

        @block.tensor
        def _(pe):
            pe.wait_ge(const_in, 16 * 11)

            def transposes(u, src, ready, need, done, free):
                pe.wait_ge(ready, need)
                if free is not None:
                    pe.wait_ge(*free)
                for k in range(KC):
                    last = nc.tensor.transpose(pair(2 + u % 2)[:, k * P:(k + 1) * P], src[:, k * P:(k + 1) * P], ident[:, :])
                last.then_inc(done, 1)

            def chunk(j):
                pe.wait_ge(wl_done, j + 1)
                if N_IN <= j < N_IN + 2:
                    pe.wait_ge(tok_ev, j - N_IN + 7)
                if j >= 2:
                    pe.wait_ge(ev_act, j - 1)
                    if dve_reads(j - 2):
                        pe.wait_ge(ev_dve, dve_reads(j - 2))
                if j < N_IN:
                    t_product(pe, j, mT_h, mT_l, pair(j % 2), MEM).then_inc(gemm, 1)
                else:
                    t_product(pe, j, hT_h, hT_l, pair(j % 2), SEQ).then_inc(gemm, 1)

            def tokens_first(j):
                n = TOK_AT.index(j)
                pe.wait_ge(ev_act, j + 1)
                if j < N_IN:
                    if n >= 2:
                        pe.wait_ge(tok_ev, n - 1)
                    for t in range(MT):
                        last = nc.tensor.transpose(ps[:, 2 * (j % 2) + 1, t * P:(t + 1) * P], vmt[j % 2][:, t * P:(t + 1) * P],
                                                   ident[:, :])
                else:
                    k = n - 8
                    if k == 2:
                        pe.wait_ge(tok_ev, 9)
                    w = 24 if k == 2 else P
                    for t in range(NT):
                        last = nc.tensor.transpose(pair(2 + k % 2)[:, w * t:w * t + w], tokT[k][0:w, t * P:(t + 1) * P],
                                                   ident[0:w, 0:w])
                last.then_inc(tok_tr, 1)

            for u in range(MT + NT):
                transposes(u, hn0[u % 2], hn_n, u + 1, tr_n, (hl_n, u - 1) if u >= 2 else None)
                if u >= MT:
                    if u == MT:
                        pe.wait_ge(hl_n, MT)
                    for j in (2 * (u - MT), 2 * (u - MT) + 1):
                        chunk(j)
                        if j - 1 in TOK_AT:
                            tokens_first(j - 1)
            pe.wait_ge(hl_n, MT + NT)
            for j in range(N_IN, N_OUT):
                if j == N_IN + 1:
                    tokens_first(N_IN - 1)
                chunk(j)
                if j - 1 in TOK_AT and j > N_IN:
                    tokens_first(j - 1)
            pe.drain().then_inc(end["pe"], 1)
            for n in ("act", "dve"):
                pe.wait_ge(end[n], 1)

            pe.wait_ge(consts_set, 2)
            pe.wait_ge(oh_in, 16)
            pe.wait_ge(fb["relb"], 1)
            for xcol in range(NEAR):
                o = P - xcol - DMIN
                last = nc.tensor.matmul(ps[:, xcol // 64, (xcol % 64) * 8:(xcol % 64) * 8 + 8], oh[:, o:o + P], relb[:, :],
                                        start=True, stop=True)
            last.then_inc(fb["tab"], 1)
            for z in range(ZC):
                o = -CMP_STRIDE * (z - 56) - (CMP_LEN - 1) - DMIN
                last = nc.tensor.matmul(ps[:, 4 + z // 64, (z % 64) * 8:(z % 64) * 8 + 8], oh[:, o:o + P], relb[:, :],
                                        start=True, stop=True)
            last.then_inc(fb["tab"], 1)
            for c in range(2):
                if c == 1:
                    pe.wait_ge(fb["tab_ev"], 2)
                for hf in range(2):
                    last = nc.tensor.matmul(ps[:, 6 - 2 * c + hf, :], pw[:, c, :], pu[:, c, hf * HALF:(hf + 1) * HALF],
                                            start=True, stop=True)
                last.then_inc(fb["pool"], 1)
            pe.wait_ge(fb["tab_ev"], 1)
            for hf in range(2):
                for c in range(2):
                    last = nc.tensor.matmul(ps[:, hf, :], ones[:, :], ca[:, c, hf * HALF:(hf + 1) * HALF],
                                            start=c == 0, stop=c == 1)
            last.then_inc(fb["mean"], 1)
            pe.wait_ge(ph_in, 48)
            for kv in range(2):
                pe.wait_ge(fb["cm"], kv + 1)
                for ht in range(2):
                    for j in range(16):
                        last = nc.tensor.matmul(ps[:, 2 + kv, 126 * ht:126 * ht + 126], cw1[kv][:, j, ht * P:(ht + 1) * P],
                                                cm[kv][:, j, :, :], start=j == 0, stop=j == 15)
                last.then_inc(fb["hid"], 1)
            pe.wait_ge(fb["sq"], 2)
            pe.wait_ge(fb["pool_l"], 2)
            pe.wait_ge(fb["dev"], 2)
            for hf in range(2):
                for c in range(2):
                    last = nc.tensor.matmul(ps[:, hf, :], ones[:, :], ch[:, c, hf * HALF:(hf + 1) * HALF],
                                            start=c == 0, stop=c == 1)
            last.then_inc(fb["var"], 1)
            for kv in range(2):
                pe.wait_ge(fb["gelu"], kv + 1)
                if kv == 0:
                    for ht in range(2):
                        last = nc.tensor.matmul(ps[:, 4, 0:126], cw2k[:, ht, :, :], hid_c[:, ht, :], start=ht == 0, stop=ht == 1)
                    last.then_inc(fb["kc"], 1)
                else:
                    for g in range(NKV):
                        for ht in range(2):
                            last = nc.tensor.matmul(ps[0:NCMP, 5, HD * g:HD * g + HD], hid_c[:, ht, g * NCMP:(g + 1) * NCMP],
                                                    cw2v[:, ht, :], start=ht == 0, stop=ht == 1)
                    last.then_inc(fb["vc"], 1)
            pe.wait_ge(fb["silu"], 2)
            for m in range(2):
                for hf in range(2):
                    for c in range(2):
                        last = nc.tensor.matmul(ps[:, 6 - 4 * m + hf, :], cpw[:, c, m * P:(m + 1) * P],
                                                ca[:, c, hf * HALF:(hf + 1) * HALF], start=c == 0, stop=c == 1)
                last.then_inc(fb["pw"], 1)
            pe.drain().then_inc(end["pe"], 1)
            for n in ("act", "dve"):
                pe.wait_ge(end[n], 2)

            def score_row(s, r):
                i, g, kind = SUB[s]
                n = s * QPK + r
                h = QPK * g + r
                if n >= 2:
                    pe.wait_ge(at_["exp"], n - 1)
                sc = pair(n % 2)
                qs = q_st[:, h, i * P:(i + 1) * P]
                w = width(i, kind)
                k0 = (i + 1) * P - w
                b0 = row_at(i, kind)
                w = max(w, WIDE)
                for c0 in range(b0 - b0 % HALF, b0 + w, HALF):
                    c, e = max(c0, b0), min(c0 + HALF, b0 + w)
                    ks = slice(k0 + c - b0, k0 + e - b0)
                    nc.tensor.matmul(sc[:, c:e], qs, k_h[:, kind, g, ks], start=True, stop=False)
                    last = nc.tensor.matmul(sc[:, c:e], qs, k_l[:, kind, g, ks], start=False, stop=True)
                if kind == 1:
                    cc, ks = sc[:, 0:WIDE], slice(g * CPAD, g * CPAD + WIDE)
                    nc.tensor.matmul(cc, qs, kc_h[:, ks], start=True, stop=False)
                    last = nc.tensor.matmul(cc, qs, kc_l[:, ks], start=False, stop=True)
                last.then_inc(at_["qk"], 1)

            def key_tile_transposed(s, t):
                i, g, kind = SUB[s]
                n = TILE0[s] + t
                if n >= 2:
                    pe.wait_ge(at_["pt_l"], n - 1)
                cmp_tile = kind == 1 and t == tiles_of(s) - 1
                for r in range(QPK):
                    src = p_sel[:, r, t * P:(t + 1) * P] if kind == 0 else (
                        p_win[:, r, 5 * P:5 * P + NCMP] if cmp_tile else p_win[:, r, t * P:(t + 1) * P])
                    rows = NCMP if cmp_tile else P
                    if t == 0:
                        pe.wait_ge(at_["pn"], QPK * s + r + 1)
                    last = nc.tensor.transpose(ps[0:rows, 4 + n % 2, r * P:(r + 1) * P], src, ident[:, :])
                last.then_inc(at_["tr"], 1)

            def key_tile_product(s, t):
                i, g, kind = SUB[s]
                n = TILE0[s] + t
                unit = s // 2
                first = kind == 0 and t == 0
                end_of_unit = kind == 1 and t == tiles_of(s) - 1
                pe.wait_ge(at_["pt_l"], n + 1)
                if first and unit >= 2:
                    pe.wait_ge(at_["o_sum"], unit - 1)
                o = ps[:, 6 + unit % 2, :]
                if end_of_unit:
                    w, rows = vc[0:NCMP, g, :], slice(0, NCMP)
                else:
                    kt = t if kind == 0 else max(0, i - WIN_TILES) + t
                    w, rows = v_st[:, (kt * 2 + kind) * NKV + g, :], slice(0, P)
                nc.tensor.matmul(o, w, pt_h[n % 3][rows, :], start=first, stop=False)
                last = nc.tensor.matmul(o, w, pt_l[n % 3][rows, :], start=False, stop=end_of_unit)
                last.then_inc(at_["pv"], 1)

            pe.wait_ge(at_["v_l"], 1)
            tiles = [(s, t) for what, s, t in ORDER if what == "tile"]
            at_tile = 0
            for what, s, k in ORDER:
                if what == "row":
                    score_row(s, k)
                else:
                    key_tile_transposed(s, k)
                    if at_tile >= 2:
                        key_tile_product(*tiles[at_tile - 2])
                    at_tile += 1
            key_tile_product(*tiles[-2])
            key_tile_product(*tiles[-1])
            pe.drain().then_inc(end["pe"], 1)

            def block_product(s, n0, j_next, n_next):
                b = bo[s]

                def operands(t, hf, k):
                    ts, c = slice(t * P, (t + 1) * P), slice(hf * HALF, (hf + 1) * HALF)
                    return pair(t % 2)[:, c], hT_h[:, k, ts], hT_l[:, k, ts], wb_h[:, k, c], wb_l[:, k, c]

                def tile_t(t):
                    if t >= 2:
                        pe.wait_ge(b["up"], t - 1)
                    for hf in range(2):
                        for k in range(KC):
                            last = three_pass(pe, *operands(t, hf, k), k == 0, k == KC - 1)
                    last.then_inc(b["mm"], 1)

                for k in range(KC):
                    pe.wait_ge(wl_done, n0 + k + 1)
                    for t in range(2):
                        for hf in range(2):
                            last = three_pass(pe, *operands(t, hf, k), k == 0, k == KC - 1)
                        if k == KC - 1:
                            last.then_inc(b["mm"], 1)
                for t in range(1, NT):
                    if t >= 2:
                        tile_t(t)
                    transposes(t - 1, hn[(t - 1) % 2], b["hn"], t, b["tr"], (b["hl"], t - 2) if t >= 3 else None)
                pe.wait_ge(b["hl"], NT // 2)
                for c in range(2):
                    pe.wait_ge(wl_done, n_next + c + 1)
                    pe.wait_ge(b["up"], NT - 1 + c)
                    t_product_half(pe, j_next + c, pair(c), 0)
                transposes(NT - 1, hn[(NT - 1) % 2], b["hn"], NT, b["tr"], (b["hl"], NT - 2))

            for n in ("act", "dve"):
                pe.wait_ge(end[n], 3)
            block_product(0, N_OUT, J_Q, N_Q)
            pe.drain().then_inc(end["pe"], 1)
            for n in ("act", "dve"):
                pe.wait_ge(end[n], 4)
            for m in range(8):
                pe.wait_ge(wl_done, N_Q + m + 1)
                if m >= 2:
                    pe.wait_ge(xa["q_ev"], m - 1)
                if m >= 2:
                    t_product_half(pe, J_Q + m, pair(m % 2), 0)
                t_product_half(pe, J_Q + m, pair(m % 2), 1).then_inc(gemm, 1)
            pe.drain().then_inc(end["pe"], 1)
            for n in ("act", "dve"):
                pe.wait_ge(end[n], 5)
            pe.wait_ge(kv_in, 32)

            def x_scores(t):
                if t >= 2:
                    pe.wait_ge(xa["exp"], XH * (t - 1))
                for h in range(XH):
                    for c in range(2):
                        last = nc.tensor.matmul(pair(t % 2)[:, h * MEM:(h + 1) * MEM], xq[:, 2 * h + c, t * P:(t + 1) * P],
                                                km[:, 2 * h + c, :], start=c == 0, stop=c == 1)
                last.then_inc(xa["s"], 1)

            def x_transposes(t):
                pe.wait_ge(xa["pn"], t + 1)
                if t >= 1:
                    pe.wait_ge(xa["pt"], t)
                for m in range(MT):
                    for h in range(XH):
                        last = nc.tensor.transpose(pair(2)[:, (m * XH + h) * P:(m * XH + h + 1) * P],
                                                   xp[t % 2][:, h, m * P:(m + 1) * P], ident[:, :])
                last.then_inc(xa["tr"], 1)

            def x_values(t):
                pe.wait_ge(xa["pt"], t + 1)
                if t >= 1:
                    pe.wait_ge(xa["ol"], t)
                for c in range(KC):
                    for m in range(MT):
                        last = nc.tensor.matmul(pair(3)[:, c * P:(c + 1) * P], vm[:, m, c * P:(c + 1) * P],
                                                xpt[t % 2][:, m, c // 2, :], start=m == 0, stop=m == MT - 1)
                last.then_inc(xa["pv"], 1)

            x_scores(0)
            for t in range(NT):
                if t + 1 < NT:
                    x_scores(t + 1)
                x_transposes(t)
                if t >= 1:
                    x_values(t - 1)
            x_values(NT - 1)
            pe.drain().then_inc(end["pe"], 1)
            for n in ("act", "dve"):
                pe.wait_ge(end[n], 6)
            block_product(1, N_O, J_MLP, N_MLP)
            pe.drain().then_inc(end["pe"], 1)
            for n in ("act", "dve"):
                pe.wait_ge(end[n], 7)

            def mlp_group(g, first_done=False):
                for c in range(GROUP):
                    if not (first_done and c < 2):
                        pe.wait_ge(wl_done, g * 8 + (N_MLP + c + 1))
                        pe.wait_ge(ml["relu"], g * GROUP + (c + 1))
                        t_product_half(pe, J_MLP + c, pair(c % 2), 0)
                    t_product_half(pe, J_MLP + c, pair(c % 2), 1).then_inc(ml["up"], 1)

                def down(idx, chunks):
                    t, hf = idx // 2, idx % 2
                    ts, cs = slice(t * P, (t + 1) * P), slice(hf * HALF, (hf + 1) * HALF)
                    if chunks[0] == 0:
                        pe.wait_ge(ml["acc"], g * (2 * NT) + (idx + 1))
                    for c in chunks:
                        if idx == 0:
                            pe.wait_ge(wl_done, g * 8 + (N_MLP + GROUP + c + 1))
                            pe.wait_ge(ml["hl"], g * GROUP + (c + 3))
                        last = three_pass(pe, ps[:, 4 + idx % 4, :], hid_h[:, c, ts], hid_l[:, c, ts],
                                          w2_h[:, c, cs], w2_l[:, c, cs], c == 0, c == GROUP - 1)
                    if c == GROUP - 1:
                        last.then_inc(ml["dn"], 1)

                for idx in range(4):
                    down(idx, range(GROUP - 1))
                for idx in range(4):
                    down(idx, [GROUP - 1])
                for idx in range(4, 2 * NT):
                    down(idx, range(GROUP))

            mlp_group(0, first_done=True)
            with pe.Fori(1, NGROUP) as g:
                mlp_group(g)

        @block.scalar
        def _(act):
            def w_hi(n):
                act.wait_ge(raw_in[n % 2], 16 * (n // 2 + 1))
                j = t_index(n)
                if j is not None and j >= 2:
                    act.wait_ge(gemm, j - 1)
                nc.scalar.activation(w_dest(n)[0], wraw[n % 2][:, :], ACT.Copy).then_inc(wh_done, 1)

            def sum_squares(src, out, scratch, done):
                nc.scalar.activation(scratch, src, ACT.Square, accum_out=out).then_inc(done, 1)

            for t in range(MT):
                act.dma_start(x_in[t][:, :], mem_t[t]).then_inc(mem_ld[t], 16)
            act.wait_ge(const_in, 16 * 11)
            w_hi(0)
            w_hi(1)

            def mem_copy(j):
                act.wait_ge(gemm, j + 1)
                if j < 8:
                    act.activation(km0[:, j, :], pair(j % 2)[:, 0:MEM], ACT.Copy).then_inc(ev_act, 1)
                else:
                    if j >= 10:
                        act.wait_ge(tok_tr, j - 9)
                    act.activation(vmt[j % 2][:, :], pair(j % 2)[:, 0:MEM], ACT.Copy).then_inc(ev_act, 1)

            def mem_values(j):
                act.wait_ge(tok_tr, j - 7)
                act.activation(vm0[:, :, (j - 8) * P:(j - 7) * P],
                               ps[:, 2 * (j % 2) + 1, 0:MEM].rearrange("p (t c) -> p t c", t=MT), ACT.Copy).then_inc(tok_ev, 1)

            for u in range(MT + NT + 1):
                if u < MT + NT:
                    if u < MT:
                        act.wait_ge(mem_ld[u], 16)
                    else:
                        act.wait_ge(x_ld[u % 2], 16 * (u // 2))
                    if u >= 1:
                        act.wait_ge(ss_n, u)
                    sum_squares(x_in[u % 2][:, :], ss[:, u:u + 1], junk0[:, :], ss_n)
                if u >= 1:
                    v = u - 1
                    act.wait_ge(tr_n, v + 1)
                    dst = mT_h[:, :, v * P:(v + 1) * P] if v < MT else hT_h[:, :, (v - MT) * P:(v - MT + 1) * P]
                    act.activation(dst, pair(2 + v % 2).rearrange("p (k c) -> p k c", k=KC), ACT.Copy).then_inc(hh_n, 1)
                    if v >= MT:
                        for j in (2 * (v - MT), 2 * (v - MT) + 1):
                            mem_copy(j)
                            w_hi(j + 2)
                            if j - 1 in TOK_AT:
                                mem_values(j - 1)

            def take_tokens(k):
                act.wait_ge(tok_tr, 9 + k)
                if k < 2:
                    act.activation(v_sw[:, :, k, :], pair(2 + k).rearrange("p (t c) -> p t c", t=NT), ACT.Copy).then_inc(tok_ev, 1)
                else:
                    act.activation(gates[:, :, :], pair(2)[:, 0:24 * NT].rearrange("p (t c) -> p t c", t=NT),
                                   ACT.Sigmoid).then_inc(tok_ev, 1)

            for j in range(N_IN, N_OUT):
                act.wait_ge(gemm, j + 1)
                pp = pair(j % 2)
                m = PIECES[j][1]
                if m in TOK:
                    w = 24 if m == 16 else P
                    act.activation(tokT[TOK.index(m)][0:w, :], pp[0:w, :], ACT.Copy).then_inc(ev_act, 1)
                elif m in (0, 1):
                    act.activation(pu[:, m, :], pp, ACT.Copy).then_inc(ev_act, 1)
                elif m in (2, 3):
                    act.activation(ch[:, m - 2, :], pp, ACT.Copy).then_inc(ev_act, 1)
                elif m in (4, 5):
                    if m == 5:
                        act.wait_ge(sig_step, 1)
                    act.activation(sig[:, :], pp, ACT.Sigmoid).then_inc(ev_act, 1)
                elif m in (10, 11):
                    st = c_st[m - 10]
                    act.activation(st[0:HD, 0, :], pp[0:HD, :], ACT.Copy)
                    act.activation(st[0:HD, 1, :], pp[HD:P, :], ACT.Copy).then_inc(ev_act, 1)
                elif m in (12, 14):
                    kd = (m - 12) // 2
                    if m == 12:
                        act.wait_ge(store0, 32)
                    act.activation(k_h[0:HD, kd, 0, :], pp[0:HD, :], ACT.Copy)
                    act.activation(k_h[HD:P, kd, 0, :], pp[0:HD, :], ACT.Copy)
                    act.activation(k_h[0:HD, kd, 1, :], pp[HD:P, :], ACT.Copy)
                    act.activation(k_h[HD:P, kd, 1, :], pp[HD:P, :], ACT.Copy).then_inc(ev_act, 1)
                else:
                    if m == 6:
                        act.wait_ge(sig_step, 2)
                        act.wait_ge(pool_step, POOL_STEPS)
                    h = 2 * (m - 6)
                    act.activation(q_st[0:HD, h, :], pp[0:HD, :], ACT.Copy, scale=-HD ** -0.5)
                    act.activation(q_st[HD:P, h + 1, :], pp[HD:P, :], ACT.Copy, scale=-HD ** -0.5).then_inc(ev_act, 1)
                if j + 2 < N_OUT:
                    w_hi(j + 2)
                if j == N_IN:
                    mem_values(N_IN - 1)
                if j - 1 in TOK_AT and j > N_IN:
                    take_tokens(TOK_AT.index(j - 1) - 8)
            act.drain().then_inc(end["act"], 1)
            for n in ("pe", "dve"):
                act.wait_ge(end[n], 1)

            act.wait_ge(fb["tab"], 1)
            act.wait_ge(fb["cm"], 2)
            act.activation(tn[:, :, :].rearrange("p h x -> p x h"), ps[:, 0:4, :].rearrange("p a (b h) -> p (a b) h", h=NH),
                           ACT.Copy).then_inc(fb["tab_ev"], 1)
            act.wait_ge(fb["tab"], 2)
            act.activation(tc[:, :, :].rearrange("p h x -> p x h"),
                           pair(2)[:, 0:NH * ZC].rearrange("p (z h) -> p z h", h=NH), ACT.Copy).then_inc(fb["tab_ev"], 1)
            for c in range(2):
                act.wait_ge(fb["pool"], c + 1)
                act.activation(hT_h[:, c, :], pair(3 - c), ACT.Copy, scale=smc("pool_scale", c)).then_inc(fb["pool_h"], 1)
            for c in range(2):
                act.wait_ge(fb["dev"], c + 1)
                act.activation(ch[:, c, :], ca[:, c, :], ACT.Square).then_inc(fb["sq"], 1)
            for kv in range(2):
                act.wait_ge(fb["hid"], kv + 1)
                if kv == 1:
                    act.wait_ge(fb["kc"], 1)
                act.activation(hid_c[:, :, :], ps[:, 2 + kv, 0:252].rearrange("p (t c) -> p t c", t=2),
                               ACT.Gelu_apprx_tanh).then_inc(fb["gelu"], 1)
                if kv == 0:
                    act.wait_ge(fb["kc"], 1)
                    act.wait_ge(fb["chain"], 2)
                    act.activation(kc_h[:, 0:2 * CPAD].rearrange("p (g c) -> p g c", g=NKV)[:, :, 0:NCMP], ps[:, 4, 0:126].rearrange("p (g c) -> p g c", g=NKV),
                                   ACT.Copy).then_inc(fb["kc_h"], 1)
            act.wait_ge(fb["vc"], 1)
            act.activation(vc[0:NCMP, :, 0:HD], ps[0:NCMP, 5, 0:P].rearrange("p (g c) -> p g c", g=NKV), ACT.Copy)\
                .then_inc(fb["vc_ev"], 1)
            act.wait_ge(fb["var"], 1)
            act.activation(cln[:, :], pair(0), ACT.Sqrt, bias=smc("eps")).then_inc(fb["sd"], 1)
            for c in range(2):
                act.wait_ge(fb["z"], c + 1)
                act.activation(ca[:, c, :], ca[:, c, :], ACT.Silu, bias=smc("ln_b", c), scale=smc("ln_g", c)).then_inc(fb["silu"], 1)
            for m in range(2):
                act.wait_ge(fb["pw"], m + 1)
                act.activation(hT_h[:, 2 + m, :], pair(3 - 2 * m), ACT.Copy).then_inc(fb["pw_h"], 1)
            act.drain().then_inc(end["act"], 1)
            for n in ("pe", "dve"):
                act.wait_ge(end[n], 2)

            def exp_row(s, r):
                i, g, kind = SUB[s]
                n = s * QPK + r
                act.wait_ge(at_["max"], n + 1)
                if s >= 2 and r == 0:
                    act.wait_ge(at_["tr"], TILE0[s - 1])
                w, b0 = width(i, kind), row_at(i, kind)
                nb = nmx[:, n % 2, :]
                sc = pair(n % 2)
                if kind == 0:
                    act.activation(p_sel[:, r, 0:w], sc[:, b0:b0 + w], ACT.Exp, bias=nb[:, 0:1], scale=-1.0,
                                   accum_out=sums[:, kind, r, 1:2]).then_inc(at_["exp"], 1)
                else:
                    act.activation(p_win[:, r, 0:w], sc[:, b0:b0 + w], ACT.Exp, bias=nb[:, 0:1], scale=-1.0,
                                   accum_out=sums[:, kind, r, 2:3])
                    act.activation(p_win[:, r, 5 * P:5 * P + CPAD], sc[:, 0:CPAD], ACT.Exp,
                                   bias=nb[:, 1:2], scale=-1.0, accum_out=sums[:, kind, r, 0:1]).then_inc(at_["exp"], 1)

            def copy_tile(s, t):
                n = TILE0[s] + t
                rows = NCMP if (SUB[s][2] == 1 and t == tiles_of(s) - 1) else P
                act.wait_ge(at_["tr"], n + 1)
                if n >= 3:
                    act.wait_ge(at_["pv"], n - 2)
                act.activation(pt_h[n % 3][0:rows, :], ps[0:rows, 4 + n % 2, :], ACT.Copy).then_inc(at_["pt_h"], 1)

            def take_output(unit):
                act.wait_ge(at_["pv"], TILE0[2 * unit + 2])
                if unit >= 1:
                    act.wait_ge(at_["o_sum"], unit)
                act.activation(o_b[:, :], ps[HD:P, 6 + unit % 2, :], ACT.Copy).then_inc(at_["o_b"], 1)

            def output_hi(unit):
                i, g = unit // NKV, unit % NKV
                act.wait_ge(at_["o_sum"], unit + 1)
                act.activation(hT_h[:, 4 + 2 * g:6 + 2 * g, i * P:(i + 1) * P], o_sum[:, :, :], ACT.Copy).then_inc(at_["o_h"], 1)

            act.activation(v_st[:, :, 0:HD], v_sw[:, :, :, :].rearrange("p t k (g d) -> p (t k g) d", g=NKV), ACT.Copy)\
                .then_inc(at_["v_h"], 1)
            act.wait_ge(at_["v_l"], 1)
            waiting = None
            for what, s, k in ORDER:
                if what == "tile":
                    copy_tile(s, k)
                if waiting:
                    exp_row(*waiting)
                waiting = (s, k) if what == "row" and k < QPK - 1 else None
                if what == "row" and not waiting:
                    exp_row(s, k)
                if (what, s, k) in TAKE:
                    take_output(TAKE[what, s, k])
                if (what, s, k) in FINISH:
                    output_hi(FINISH[what, s, k])
            take_output(len(SUB) // 2 - 1)
            output_hi(len(SUB) // 2 - 1)
            act.drain().then_inc(end["act"], 1)
            for n in ("pe", "dve"):
                act.wait_ge(end[n], 3)

            def block_out(s, split_next):
                b = bo[s]
                act.wait_ge(b["gain"], 32)
                for t in range(NT + 1):
                    if t < NT:
                        act.wait_ge(b["mm"], t + 1)
                        if t >= 2:
                            act.wait_ge(b["up"], t - 1)
                        if t >= 1:
                            act.wait_ge(b["ss2"], t)
                        sum_squares(pair(t % 2), ssb[:, 0, t % 2:t % 2 + 1], junk[:, :], b["ss"])
                    if t >= 1:
                        act.wait_ge(b["tr"], t)
                        ts = slice((t - 1) * P, t * P)
                        act.activation(hT_h[:, :, ts], pair(2 + (t - 1) % 2).rearrange("p (k c) -> p k c", k=KC),
                                       ACT.Copy).then_inc(b["hh"], 1)
                    if t < NT:
                        act.wait_ge(b["x"], t + 1)
                        act.wait_ge(b["ss"], t + 1)
                        sum_squares(upd[t % 2][:, :], ssb[:, 1, t % 2:t % 2 + 1], junk[:, :], b["ss2"])
                        if t == NT - 2:
                            split_next()

            for k in range(KC):
                w_hi(N_OUT + k)
            block_out(0, lambda: (w_hi(N_Q), w_hi(N_Q + 1)))
            act.drain().then_inc(end["act"], 1)
            for n in ("pe", "dve"):
                act.wait_ge(end[n], 4)
            for m in range(8):
                act.wait_ge(gemm, J_Q + m + 1)
                if m == 0:
                    for t in range(2):
                        act.wait_ge(bo[0][f"st{t}"], 16 * (NT // 2))
                act.activation(xq[:, m, :], pair(m % 2), ACT.Copy, scale=(D // XH) ** -0.5).then_inc(xa["q_ev"], 1)
                if m + 2 < 8:
                    w_hi(N_Q + m + 2)
            act.drain().then_inc(end["act"], 1)
            for n in ("pe", "dve"):
                act.wait_ge(end[n], 5)

            for t in range(NT + 2):
                if t < NT:
                    act.wait_ge(xa["max"], t + 1)
                    if t >= 2:
                        act.wait_ge(xa["tr"], t - 1)
                    for h in range(XH):
                        act.activation(xp[t % 2][:, h, :], pair(t % 2)[:, h * MEM:(h + 1) * MEM], ACT.Exp,
                                       bias=xs[:, 0, h:h + 1], accum_out=xs[:, 1, h:h + 1]).then_inc(xa["exp"], 1)
                if 1 <= t <= NT:
                    act.wait_ge(xa["tr"], t)
                    if t >= 3:
                        act.wait_ge(xa["pv"], t - 2)
                    act.activation(xpt[(t - 1) % 2][:, :, :, :].rearrange("p m h c -> p (m h c)"), pair(2), ACT.Copy).then_inc(xa["pt"], 1)
                if t >= 2:
                    act.wait_ge(xa["pv"], t - 1)
                    ts = slice((t - 2) * P, (t - 1) * P)
                    act.activation(hT_h[:, :, ts], pair(3).rearrange("p (k c) -> p k c", k=KC), ACT.Copy).then_inc(xa["oh"], 1)
                if t < NT:
                    w_hi(N_O + t)
            act.drain().then_inc(end["act"], 1)
            for n in ("pe", "dve"):
                act.wait_ge(end[n], 6)

            def w_hi_mlp(g, c):
                n = N_MLP + c
                k, c = divmod(c, 2 * GROUP)
                act.wait_ge(raw_in[n % 2], g * (16 * 4) + 16 * (n // 2 + 1))
                if c < GROUP:
                    j = J_MLP + c
                    act.wait_ge(ml["up"], g * GROUP + (k * GROUP + c + 1))
                    dst = tw_h[j % 2][:, :, :].rearrange("p k n -> p (k n)")
                else:
                    act.wait_ge(ml["dn"], g * (2 * NT) + 1)
                    dst = w2_h[:, c - GROUP, :]
                act.activation(dst, wraw[n % 2][:, :], ACT.Copy).then_inc(wh_done, 1)

            act.sem_inc(ml["relu"], 2)
            act.sem_inc(ml["up"], 2)
            act.sem_inc(ml["dn"], 1)
            block_out(1, lambda: (w_hi_mlp(0, 0), w_hi_mlp(0, 1)))
            act.drain().then_inc(end["act"], 1)
            for n in ("pe", "dve"):
                act.wait_ge(end[n], 7)
            for t in range(2):
                act.wait_ge(bo[1][f"st{t}"], 16 * (NT // 2))

            def hidden(g, c):
                act.wait_ge(ml["up"], g * GROUP + (c + 3))
                act.wait_ge(ml["hl"], g * GROUP + (c + 1))
                act.activation(rl[c % 2][:, :], pair(c % 2), ACT.Relu).then_inc(ml["relu"], 1)
                act.wait_ge(ml["relu"], g * GROUP + (c + 3))
                act.activation(rl[c % 2][:, :], rl[c % 2][:, :], ACT.Square).then_inc(ml["sq"], 1)
                act.wait_ge(ml["sq"], g * GROUP + (c + 1))
                act.wait_ge(ml["dn"], g * (2 * NT) + 1)
                act.activation(hid_h[:, c, :], rl[c % 2][:, :], ACT.Copy).then_inc(ml["hh"], 1)

            def mlp_group(g, last=False):
                hidden(g, 0)
                w_hi_mlp(g, 2)
                hidden(g, 1)
                w_hi_mlp(g, 3)
                w_hi_mlp(g, 4)
                hidden(g, 2)
                w_hi_mlp(g, 5)
                w_hi_mlp(g, 6)
                hidden(g, 3)
                w_hi_mlp(g, 7)
                if not last:
                    w_hi_mlp(g, 8)
                    w_hi_mlp(g, 9)

            with act.Fori(0, NGROUP - 1) as g:
                mlp_group(g)
            mlp_group(NGROUP - 1, last=True)
            for t in range(NT):
                act.wait_ge(ml["acc"], 2 * NT * (NGROUP - 1) + 4 + 2 * (t + 1))
                if t >= 2:
                    act.wait_ge(ml["y"], t - 1)
                if t >= 1:
                    act.wait_ge(ml["ss"], t)
                sum_squares(acc[:, t, :], ssb[:, 0, t % 2:t % 2 + 1], junk_f[:, :], ml["ss"])

        @block.vector
        def _(dve):
            V = nc.vector

            def w_lo(n):
                dve.wait_ge(wh_done, n + 1)
                dst, hi = w_dest(n)[1], w_dest(n)[0]
                V.tensor_tensor(dst, wraw[n % 2][:, :], hi.bitcast(F32), ALU.subtract).then_inc(wl_done, 1)

            dve.wait_ge(const_in, 16 * 11)
            w_lo(0)
            w_lo(1)
            for u in range(MT + NT + 1):
                if u < MT + NT:
                    dve.wait_ge(rs_n, u + 1)
                    if u >= 2:
                        dve.wait_ge(tr_n, u - 1)
                    V.scalar_tensor_tensor(hn0[u % 2][:, :], x_in[u % 2][:, :], rstd[:, u:u + 1],
                                           (gain_m if u < MT else gain_x)[:, :], ALU.mult, ALU.mult).then_inc(hn_n, 1)
                if u >= 1:
                    v = u - 1
                    dve.wait_ge(hh_n, v + 1)
                    hi, lo = (mT_h, mT_l) if v < MT else (hT_h, hT_l)
                    v0 = v if v < MT else v - MT
                    cs = slice(v0 * P, (v0 + 1) * P)
                    V.tensor_tensor(lo[:, :, cs], pair(2 + v % 2).rearrange("p (k c) -> p k c", k=KC),
                                    hi[:, :, cs].bitcast(F32), ALU.subtract).then_inc(hl_n, 1)
                    if v >= MT:
                        for j in (2 * (v - MT), 2 * (v - MT) + 1):
                            w_lo(j + 2)

            pstep = [0]

            def pooled(ins):
                pstep[0] += 1
                ins.then_inc(pool_step, 1)
                dve.wait_ge(pool_step, pstep[0])

            def window_sum(dst, src, d, rows):
                pooled(V.tensor_tensor(dst[rows, d:], src[rows, d:], src[rows, 0:SEQ - d], ALU.add))
                pooled(V.tensor_copy(dst[rows, 0:d], src[rows, 0:d]))

            def mean_minus(c, src, rows):
                u = pu[:, c, :]
                pooled(V.tensor_tensor(t16[rows, :], src[rows, 0:16], sm[rows, SM["inv16"][0] + 16 * c:SM["inv16"][0] + 16 * c + 16], ALU.mult))
                pooled(V.tensor_tensor(u[rows, 0:16], t16[rows, :], u[rows, 0:16], ALU.subtract))
                pooled(V.scalar_tensor_tensor(u[rows, 16:], src[rows, 16:], smc("inv_win", c, rows), u[rows, 16:], ALU.mult, ALU.subtract))

            lo_rows, hi_rows, all_rows = slice(0, HD), slice(HD, P), slice(0, P)

            def pool_tile(c):
                a_, b_ = pool_a, pool_b
                window_sum(a_, pu[:, c, :], 1, all_rows)
                if c == 0:
                    window_sum(b_, a_, 2, hi_rows)
                    mean_minus(0, a_, lo_rows)
                    mean_minus(0, b_, hi_rows)
                else:
                    window_sum(b_, a_, 2, all_rows)
                    window_sum(a_, b_, 4, all_rows)
                    window_sum(b_, a_, 8, hi_rows)
                    mean_minus(1, a_, lo_rows)
                    mean_minus(1, b_, hi_rows)

            cstep = [0]

            def conv_taps(n0, n1):
                for n in range(n0, min(n1, 2 * TAPS)):
                    c, d = n // TAPS, n % TAPS
                    w = smc("conv_w", c * TAPS + TAPS - 1 - d)
                    if d == 0:
                        ins = V.tensor_scalar(ca[:, c, :], ch[:, c, :], w, smc("conv_b", c), ALU.mult, ALU.add)
                    else:
                        ins = V.scalar_tensor_tensor(ca[:, c, d:], ch[:, c, 0:SEQ - d], w, ca[:, c, d:], ALU.mult, ALU.add)
                    ins.then_inc(conv_step, 1)
                    dve.wait_ge(conv_step, n + 1)

            def glu(c):
                V.tensor_tensor(ch[:, c, :], ch[:, c, :], sig[:, :], ALU.mult).then_inc(sig_step, 1)
                dve.wait_ge(sig_step, c + 1)

            for j in range(N_IN, N_OUT):
                m = PIECES[j][1]
                pp = pair(j % 2)
                if m in (0, 1, 4, 5) or READS[j]:
                    dve.wait_ge(ev_act, j + 1)
                if m in (4, 5):
                    glu(m - 4)
                elif m in (10, 11):
                    st = c_st[m - 10]
                    V.tensor_copy(st[HD:P, 0, 0:SEQ - 1], pp[0:HD, 1:SEQ])
                    V.tensor_copy(st[HD:P, 1, 0:SEQ - 1], pp[HD:P, 1:SEQ]).then_inc(ev_dve, 1)
                elif m in (12, 14):
                    kd = (m - 12) // 2
                    for g in range(NKV):
                        rows = slice(HD * g, HD * g + HD)
                        for e in range(2):
                            last = V.tensor_tensor(k_l[HD * e:HD * e + HD, kd, g, :], pp[rows, :],
                                                   k_h[rows, kd, g, :].bitcast(F32), ALU.subtract)
                    last.then_inc(ev_dve, 1)
                elif m in (6, 7, 8, 9):
                    h = 2 * (m - 6)
                    V.scalar_tensor_tensor(q_st[HD:P, h, :], pp[0:HD, :], -HD ** -0.5, q_st[0:HD, h, :].bitcast(F32),
                                           ALU.mult, ALU.subtract)
                    V.scalar_tensor_tensor(q_st[0:HD, h + 1, :], pp[HD:P, :], -HD ** -0.5, q_st[HD:P, h + 1, :].bitcast(F32),
                                           ALU.mult, ALU.subtract).then_inc(ev_dve, 1)
                if j + 2 < N_OUT:
                    w_lo(j + 2)
                if m in (0, 1):
                    pool_tile(m)
                elif j >= N_IN + 2:
                    n = j - N_IN - 2
                    conv_taps(CONV_PLAN[n], CONV_PLAN[n + 1])
            dve.wait_ge(tok_ev, 11)
            V.tensor_scalar(gates[:, 0, 0:24:3], gates[:, 0, 0:24:3], smc("valid"), None, ALU.mult)
            dve.drain().then_inc(end["dve"], 1)
            for n in ("pe", "act"):
                dve.wait_ge(end[n], 1)

            fbc = [0]

            def chained(ins, s=fb["rb"]):
                fbc[0] += 1
                ins.then_inc(s, 1)
                dve.wait_ge(s, fbc[0])

            R = slice(0, 3 * NBUCKET)
            chained(V.memset(relb[96:97, :], -NEG))
            chained(V.tensor_scalar(rb[R, :], rb[R, :], -1.0, None, ALU.mult))
            chained(V.tensor_copy(rhm[R, 0, :], rb[R, :]))
            chained(V.tensor_tensor(rb1[R, :], rb[R, :], rhm[R, 0, :], ALU.subtract))
            chained(V.tensor_copy(rhm[R, 1, :], rb1[R, :]))
            chained(V.tensor_tensor(rb2[R, :], rb1[R, :], rhm[R, 1, :], ALU.subtract))
            chained(V.tensor_copy(relb[0:32, :], rhm[0:32, 0, :]))
            chained(V.tensor_copy(relb[32:64, :], rhm[32:64, 1, :]))
            V.tensor_copy(relb[64:96, :], rb2[64:96, :]).then_inc(fb["relb"], 1)
            for kv in range(2):
                for j in range(16):
                    last = V.tensor_scalar(cm[kv][:, j, :, :], c_st[kv][:, :, 2 * j:2 * j + CMP_STRIDE * (NCMP - 1) + 1:CMP_STRIDE],
                                           smc(("pos_k", "pos_v")[kv], j), None, ALU.add)
                last.then_inc(fb["cm"], 1)
            for c in range(2):
                dve.wait_ge(fb["pool_h"], c + 1)
                V.scalar_tensor_tensor(hT_l[:, c, :], pair(3 - c), smc("pool_scale", c), hT_h[:, c, :].bitcast(F32),
                                       ALU.mult, ALU.subtract).then_inc(fb["pool_l"], 1)
            dve.wait_ge(fb["hid"], 2)
            V.memset(kc_h[:, :].bitcast(F32), 0.0).then_inc(fb["chain"], 1)
            V.memset(kc_l[:, :].bitcast(F32), 0.0).then_inc(fb["chain"], 1)
            dve.wait_ge(fb["chain"], 2)
            dve.wait_ge(fb["mean"], 1)
            for c in range(2):
                V.tensor_tensor(ca[:, c, :], ca[:, c, :], pair(0), ALU.subtract).then_inc(fb["dev"], 1)
            dve.wait_ge(fb["kc_h"], 1)
            V.tensor_tensor(kc_l[:, 0:2 * CPAD].rearrange("p (g c) -> p g c", g=NKV)[:, :, 0:NCMP], ps[:, 4, 0:126].rearrange("p (g c) -> p g c", g=NKV),
                            kc_h[:, 0:2 * CPAD].rearrange("p (g c) -> p g c", g=NKV)[:, :, 0:NCMP].bitcast(F32), ALU.subtract).then_inc(fb["kc_l"], 1)
            dve.wait_ge(fb["vc_ev"], 1)
            V.tensor_tensor(vc[0:NCMP, :, HD:P], ps[0:NCMP, 5, 0:P].rearrange("p (g c) -> p g c", g=NKV),
                            vc[0:NCMP, :, 0:HD].bitcast(F32), ALU.subtract)
            dve.wait_ge(fb["sd"], 1)
            V.reciprocal(ctmp[:, :], cln[:, :]).then_inc(fb["chain"], 1)
            dve.wait_ge(fb["chain"], 3)
            for c in range(2):
                V.tensor_tensor(ca[:, c, :], ca[:, c, :], ctmp[:, :], ALU.mult).then_inc(fb["z"], 1)
            for m in range(2):
                dve.wait_ge(fb["pw_h"], m + 1)
                V.tensor_tensor(hT_l[:, 2 + m, :], pair(3 - 2 * m), hT_h[:, 2 + m, :].bitcast(F32),
                                ALU.subtract).then_inc(fb["pw_l"], 1)
            dve.drain().then_inc(end["dve"], 1)
            for n in ("pe", "act"):
                dve.wait_ge(end[n], 2)

            step = [0]

            def link(ins):
                step[0] += 1
                ins.then_inc(at_["chain"], 1)
                dve.wait_ge(at_["chain"], step[0])

            def row_max(s, r):
                i, g, kind = SUB[s]
                n = s * QPK + r
                h = QPK * g + r
                w, b0 = width(i, kind), row_at(i, kind)
                sc = pair(n % 2)[:, b0:b0 + w]
                near = min(w, NEAR)
                far = w - near
                dve.wait_ge(at_["qk"], n + 1)
                if n >= 2:
                    dve.wait_ge(at_["exp"], n - 1)
                part, top = mx[:, n % 2:n % 2 + 1], nmx[:, n % 2, :]
                init = 3.0e38
                if kind == 1 and w == 5 * P:
                    link(V.tensor_tensor_reduce(sc[:, 0:far], sc[:, 0:far], wm[:, :], 1.0, init, ALU.add, ALU.min, part))
                    init = part
                elif far:
                    link(V.tensor_reduce(part, sc[:, 0:far], AX.X, ALU.min))
                    init = part
                last = V.tensor_tensor_reduce(sc[:, far:w], sc[:, far:w], tn[:, h, NEAR - near:NEAR], 1.0, init, ALU.add,
                                              ALU.min, top[:, 0:1])
                if kind == 1:
                    cc = pair(n % 2)[:, 0:CPAD]
                    z0 = 56 - 8 * i
                    last = V.tensor_tensor_reduce(cc, cc, tc[:, h, z0:z0 + CPAD], 1.0, 3.0e38, ALU.add, ALU.min, top[:, 1:2])
                last.then_inc(at_["max"], 1)

            def row_sum(s, r):
                dve.wait_ge(at_["exp"], s * QPK + r + 1)
                cs = slice(1, 2) if SUB[s][2] == 0 else slice(0, 3, 2)
                if s * QPK + r >= 2 * QPK:
                    dve.wait_ge(at_["pn"], s * QPK + r - 2 * QPK + 2)
                V.reciprocal(rsum[:, SUB[s][2], r, cs], sums[:, SUB[s][2], r, cs]).then_inc(at_["rs"], 1)

            def copy_lo(s, t):
                n = TILE0[s] + t
                rows = NCMP if (SUB[s][2] == 1 and t == tiles_of(s) - 1) else P
                dve.wait_ge(at_["pt_h"], n + 1)
                V.tensor_tensor(pt_l[n % 3][0:rows, :], ps[0:rows, 4 + n % 2, :], pt_h[n % 3][0:rows, :].bitcast(F32),
                                ALU.subtract).then_inc(at_["pt_l"], 1)

            def output_sum(unit):
                dve.wait_ge(at_["o_b"], unit + 1)
                if unit >= 1:
                    dve.wait_ge(at_["o_l"], unit)
                for e in range(2):
                    parts = (x.rearrange("p (c e q) -> p c e q", e=2, q=P)[:, :, e, :] for x in (o_b[:, :], ps[0:HD, 6 + unit % 2, :]))
                    last = V.tensor_tensor(o_sum[HD * e:HD * e + HD, :, :], *parts, ALU.add)
                last.then_inc(at_["o_sum"], 1)

            def output_lo(unit):
                i, g = unit // NKV, unit % NKV
                dve.wait_ge(at_["o_h"], unit + 1)
                dst = (slice(0, P), slice(4 + 2 * g, 6 + 2 * g), slice(i * P, (i + 1) * P))
                V.tensor_tensor(hT_l[dst], o_sum[:, :, :], hT_h[dst].bitcast(F32), ALU.subtract).then_inc(at_["o_l"], 1)

            dve.wait_ge(at_["v_h"], 1)
            V.tensor_tensor(v_st[:, :, HD:P], v_sw[:, :, :, :].rearrange("p t k (g d) -> p (t k g) d", g=NKV),
                            v_st[:, :, 0:HD].bitcast(F32), ALU.subtract).then_inc(at_["v_l"], 1)
            dve.wait_ge(wm_in, 16)
            waiting = None
            for what, s, k in ORDER:
                if what == "row":
                    row_max(s, k)
                else:
                    copy_lo(s, k)
                if waiting:
                    row_sum(*waiting)
                waiting = (s, k) if what == "row" and k < QPK - 1 else None
                if what == "row" and not waiting:
                    row_sum(s, k)
                if (what, s, k) in TAKE:
                    output_sum(TAKE[what, s, k])
                if (what, s, k) in FINISH:
                    output_lo(FINISH[what, s, k])
            output_sum(len(SUB) // 2 - 1)
            output_lo(len(SUB) // 2 - 1)
            dve.drain().then_inc(end["dve"], 1)
            for n in ("pe", "act"):
                dve.wait_ge(end[n], 3)

            def block_out(s, split_next):
                b = bo[s]
                dve.wait_ge(b["gain"], 32)
                for t in range(NT + 1):
                    if t < NT:
                        u = upd[t % 2][:, :]
                        dve.wait_ge(b["rs"], t + 1)
                        if t >= 2:
                            dve.wait_ge(b[f"st{t % 2}"], 16 * (t // 2))
                        V.scalar_tensor_tensor(u, pair(t % 2), rsb[:, 0, t % 2:t % 2 + 1], gain_post[:, :],
                                               ALU.mult, ALU.mult).then_inc(b["up"], 1)
                        dve.wait_ge(b["up"], t + 1)
                        dve.wait_ge(b[f"res{t % 2}"], 16 * (t // 2 + 1))
                        V.tensor_tensor(u, u, res[t % 2][:, :], ALU.add).then_inc(b["x"], 1)
                    if t >= 1:
                        dve.wait_ge(b["hh"], t)
                        ts = slice((t - 1) * P, t * P)
                        V.tensor_tensor(hT_l[:, :, ts], pair(2 + (t - 1) % 2).rearrange("p (k c) -> p k c", k=KC),
                                        hT_h[:, :, ts].bitcast(F32), ALU.subtract).then_inc(b["hl"], 1)
                    if t < NT:
                        dve.wait_ge(b["rs2"], t + 1)
                        if t >= 2:
                            dve.wait_ge(b["tr"], t - 1)
                        V.scalar_tensor_tensor(hn[t % 2][:, :], upd[t % 2][:, :], rsb[:, 1, t % 2:t % 2 + 1], gain_pre[:, :],
                                               ALU.mult, ALU.mult).then_inc(b["hn"], 1)
                        if t == NT - 2:
                            split_next()

            for k in range(KC):
                w_lo(N_OUT + k)
            block_out(0, lambda: (w_lo(N_Q), w_lo(N_Q + 1)))
            dve.drain().then_inc(end["dve"], 1)
            for n in ("pe", "act"):
                dve.wait_ge(end[n], 4)
            for m in range(2, 8):
                w_lo(N_Q + m)
            dve.drain().then_inc(end["dve"], 1)
            for n in ("pe", "act"):
                dve.wait_ge(end[n], 5)

            xstep = [0]

            def x_link(ins):
                xstep[0] += 1
                ins.then_inc(xa["chain"], 1)
                dve.wait_ge(xa["chain"], xstep[0])

            for t in range(NT + 2):
                if t < NT:
                    dve.wait_ge(xa["s"], t + 1)
                    V.tensor_reduce(xs[:, 0, :], pair(t % 2).rearrange("p (h m) -> p h m", h=XH), AX.X, ALU.max,
                                    negate=True).then_inc(xa["max"], 1)
                    dve.wait_ge(xa["exp"], XH * (t + 1))
                    x_link(V.reciprocal(xs[:, 2, :], xs[:, 1, :]))
                    for h in range(XH):
                        last = V.tensor_scalar(xp[t % 2][:, h, :], xp[t % 2][:, h, :], xs[:, 2, h:h + 1], None, ALU.mult)
                    last.then_inc(xa["pn"], 1)
                if t >= 2:
                    dve.wait_ge(xa["oh"], t - 1)
                    ts = slice((t - 2) * P, (t - 1) * P)
                    V.tensor_tensor(hT_l[:, :, ts], pair(3).rearrange("p (k c) -> p k c", k=KC), hT_h[:, :, ts].bitcast(F32),
                                    ALU.subtract).then_inc(xa["ol"], 1)
                if t < NT:
                    w_lo(N_O + t)
            dve.drain().then_inc(end["dve"], 1)
            for n in ("pe", "act"):
                dve.wait_ge(end[n], 6)

            def w_lo_mlp(g, c):
                n = N_MLP + c
                dve.wait_ge(wh_done, g * 8 + (n + 1))
                c %= 2 * GROUP
                if c < GROUP:
                    j = J_MLP + c
                    hi, lo = (w[j % 2][:, :, :].rearrange("p k n -> p (k n)") for w in (tw_h, tw_l))
                else:
                    hi, lo = w2_h[:, c - GROUP, :], w2_l[:, c - GROUP, :]
                V.tensor_tensor(lo, wraw[n % 2][:, :], hi.bitcast(F32), ALU.subtract).then_inc(wl_done, 1)

            dve.sem_inc(ml["acc"], 4)
            dve.sem_inc(ml["hl"], 2)
            block_out(1, lambda: (w_lo_mlp(0, 0), w_lo_mlp(0, 1)))
            dve.drain().then_inc(end["dve"], 1)
            for n in ("pe", "act"):
                dve.wait_ge(end[n], 7)

            def hidden_lo(g, c):
                dve.wait_ge(ml["hh"], g * GROUP + (c + 1))
                V.tensor_tensor(hid_l[:, c, :], rl[c % 2][:, :], hid_h[:, c, :].bitcast(F32), ALU.subtract).then_inc(ml["hl"], 1)

            def split_group(g):
                hidden_lo(g, 0)
                w_lo_mlp(g, 2)
                hidden_lo(g, 1)
                w_lo_mlp(g, 3)
                w_lo_mlp(g, 4)
                hidden_lo(g, 2)
                w_lo_mlp(g, 5)
                w_lo_mlp(g, 6)
                hidden_lo(g, 3)
                w_lo_mlp(g, 7)

            def add(g, idx, first=False):
                t, hf = idx // 2, idx % 2
                o = acc[:, t, hf * HALF:(hf + 1) * HALF]
                dve.wait_ge(ml["dn"], g * (2 * NT) + (idx + 2))
                if first:
                    V.tensor_copy(o, ps[:, 4 + idx % 4, :]).then_inc(ml["acc"], 1)
                else:
                    V.tensor_tensor(o, o, ps[:, 4 + idx % 4, :], ALU.add).then_inc(ml["acc"], 1)

            def mlp_group(g, first=False):
                split_group(g)
                for idx in range(2 * NT):
                    add(g, idx, first)
                    if idx in (3, 5):
                        w_lo_mlp(g, 8 + (idx - 3) // 2)

            def output_tile(t):
                u = upd_f[t % 2][:, :]
                dve.wait_ge(ml["rs"], t + 1)
                if t >= 2:
                    dve.wait_ge(ml[f"st{t % 2}"], 16 * (t // 2))
                V.scalar_tensor_tensor(u, acc[:, t, :], rsb[:, 0, t % 2:t % 2 + 1], gain_f[:, :], ALU.mult,
                                       ALU.mult).then_inc(ml["y"], 1)
                dve.wait_ge(ml["y"], t + 1)
                dve.wait_ge(ml[f"res{t % 2}"], 16 * (t // 2 + 1))
                V.tensor_tensor(u, u, res_f[t % 2][:, :], ALU.add).then_inc(ml["fin"], 1)

            mlp_group(0, first=True)
            with dve.Fori(1, NGROUP - 1) as g:
                mlp_group(g)
            split_group(NGROUP - 1)
            dve.wait_ge(ml["gain"], 16)
            dve.wait_ge(ml["hl"], GROUP * NGROUP + 2)
            for t in range(NT):
                add(NGROUP - 1, 2 * t)
                add(NGROUP - 1, 2 * t + 1)
                if t >= 1:
                    output_tile(t - 1)
            output_tile(NT - 1)


def kernel(**inputs):
    import concourse.bacc as _bacc
    from concourse.bass_utils import run_bass_kernel_spmd as _run

    c = np.ascontiguousarray
    v = {n: np.asarray(x) for n, x in inputs.items()}

    def chunks(w):
        return c(w.reshape(KC, P, -1, P).transpose(2, 1, 0, 3))

    def cols(w):
        return w.reshape(2, P).T

    w_in = v["w_in"][0]
    small = np.zeros((P, SMW), np.float32)

    def put(name, x):
        small[:, SM[name][0]:SM[name][1]] = x

    put("conv_w", v["conv_w"][0].T.reshape(2, P, TAPS).transpose(1, 0, 2).reshape(P, 2 * TAPS))
    put("conv_b", cols(v["conv_b"][0]))
    put("ln_g", cols(v["conv_ln_g"][0]))
    put("ln_b", cols(v["conv_ln_b"][0]))
    put("pool_scale", cols(v["pool_scale"][0]))
    put("pos_k", v["cmp_k_pos"][0].reshape(16, P).T)
    put("pos_v", v["cmp_v_pos"][0].reshape(16, P).T)
    win = np.repeat(np.array([[2, 8], [4, 16]], np.float32), HD, axis=0)
    put("inv_win", 1 / win)
    put("inv16", (1 / np.minimum(np.arange(1, 17, dtype=np.float32), win[:, :, None])).reshape(P, 32))
    put("valid", (np.arange(P)[:, None] >= CMP_LEN - 1).astype(np.float32))
    put("eps", EPS)
    pool_w = np.zeros((P, 2, P), np.float32)
    for g in range(4):
        r = slice(HD * (g % 2), HD * (g % 2) + HD)
        pool_w[r, g // 2, r] = v["pool_w"][0, g]
    d = np.arange(ND) + DMIN
    n = np.maximum(d, 1).astype(np.float32)
    large = MAX_EXACT + (np.log(n / MAX_EXACT) / math.log(MAX_DIST / MAX_EXACT) * (NBUCKET - MAX_EXACT)).astype(np.int32)
    bucket = np.where(d < MAX_EXACT, np.maximum(d, 0), np.minimum(large, NBUCKET - 1))
    hot = (np.arange(NBUCKET)[:, None] == bucket).astype(np.float32)
    hot[NBUCKET - 1] -= 1.0
    hot *= d >= 0
    onehot = np.concatenate([hot, hot, hot, (d < 0)[None].astype(np.float32)])
    q, x = np.arange(P)[:, None], np.arange(3 * P)[None, :]
    arrays = {
        "x": c(v["x"][0]), "mem": c(v["mem"][0]), "rel_bias": v["rel_bias"],
        "in": chunks(np.concatenate([w_in, np.zeros((D, P - 24), np.float32)], axis=1)),
        "wout": v["w_out"][0], "wq": chunks(v["xa_wq"][0]), "wk": chunks(v["xa_wk"][0]), "wv": chunks(v["xa_wv"][0]),
        "wo": v["xa_wo"][0], "w1": chunks(v["mlp_w1"][0]), "w2": c(v["mlp_w2"][0].reshape(FF // P, P, D)),
        "pool_w": pool_w, "small": small, "conv_pw": v["conv_pw"][0],
        "cmp_k_w1": v["cmp_k_w1"][0], "cmp_k_w2": v["cmp_k_w2"][0], "cmp_v_w1": v["cmp_v_w1"][0], "cmp_v_w2": v["cmp_v_w2"][0],
        "onehot": onehot, "ident": np.eye(P, dtype=np.float32),
        "winmask": np.where((x < P) & (x <= q), np.float32(-NEG), np.float32(0)),
    }
    for g in ("mix_pre_g", "mix_post_g", "xa_pre_g", "xa_post_g", "mem_g", "mlp_pre_g", "mlp_post_g"):
        arrays[g] = c(v[g][0])
    nc = _bacc.Bacc("TRN2", target_bir_lowering=False, num_devices=1)
    aps = {k: nc.dram_tensor("in_" + k, w.shape, mybir.dt.from_np(w.dtype), kind="ExternalInput").ap() for k, w in arrays.items()}
    for k, shape in (("x1", (SEQ, D)), ("x2", (SEQ, D)), ("kmd", (P, KC, MEM)), ("vmd", (P, MT, D))):
        aps[k] = nc.dram_tensor(k, shape, F32, kind="Internal").ap()
    aps["out"] = nc.dram_tensor("out", (SEQ, D), F32, kind="ExternalOutput").ap()
    hybrid_layer(nc, aps)
    r = _run(nc, [{"in_" + k: w for k, w in arrays.items()}], core_ids=[0])
    return r.results[0]["out"].reshape(1, SEQ, D)
```

```python
import math
import numpy as np
import concourse.bass as bass
from concourse import mybir

F32 = mybir.dt.float32
F32R = mybir.dt.float32r
BF16 = mybir.dt.bfloat16
ALU = mybir.AluOpType
ACT = mybir.ActivationFunctionType
AX = mybir.AxisListType

P = 128
SEQ, D = 1024, 1024
NT, KC = SEQ // P, D // P
MEM = 256
MT = MEM // P
HALF = 512
HD = 64
NH, NKV, QPK = 8, 2, 4
NCMP, CMP_STRIDE, CMP_LEN = 63, 16, 32
CPAD = 64
WIDE = 2 * P
KCW = CPAD * (NKV - 1) + WIDE
WIN_TILES = 512 // P
NEAR = 2 * P
TAPS = 31
CMP_HID = 256
XH = 4
FF = 4096
GROUP = 4
NGROUP = FF // P // GROUP
NBUCKET, MAX_EXACT, MAX_DIST = 32, 16, 128
NEG = -1e30
EPS = 1e-6
DMIN = -(CMP_STRIDE * (CPAD - 1) + CMP_LEN - 1)
ND = 992 - DMIN + 1
ZC = 120
OHR = 97

SM = {}
_at = 0
for _n, _w in (("conv_w", 2 * TAPS), ("conv_b", 2), ("ln_g", 2), ("ln_b", 2), ("pool_scale", 2),
               ("pos_k", 16), ("pos_v", 16), ("inv_win", 2), ("inv16", 32), ("valid", 1), ("eps", 1)):
    SM[_n] = (_at, _at + _w)
    _at += _w
SMW = _at

T_MEM = [("wk", m) for m in range(8)] + [("wv", m) for m in range(8)]
T_IN = [("in", m) for m in (2, 4, 3, 5, 0, 1, 13, 15, 16, 10, 11, 12, 14, 6, 7, 8, 9)]
TOK = (13, 15, 16)
T_Q = [("wq", m) for m in range(8)]
PIECES = T_MEM + T_IN + [("wout", k) for k in range(8)] + T_Q + [("wo", k) for k in range(8)]
N_IN = len(T_MEM)
N_OUT = N_IN + len(T_IN)
N_Q = N_OUT + 8
N_O = N_Q + 8
N_MLP = N_O + 8
J_Q = len(T_MEM) + len(T_IN)
J_MLP = J_Q + 8


POOL_STEPS = 24
CONV_PLAN = [0, 4, 9, 9, 9, 17, 25, 31, 37, 42, 45, 48, 52, 56, 60, 62]


def hybrid_layer(nc, a):
    def at(name, shape, dt, kb):
        return nc.alloc_sbuf_tensor_at(name, shape, dt, offset=BASE + int(kb * 1024))

    BASE = -(-nc.sbuf_base // 32) * 32
    hT_h = at("hT_h", [P, KC, SEQ], F32R, 0)
    hT_l = at("hT_l", [P, KC, SEQ], F32R, 32)
    cw1 = [at("cw1_k", [P, 16, CMP_HID], F32, 16), at("cw1_v", [P, 16, CMP_HID], F32, 48)]
    x_in = [at(f"x_in{s}", [P, D], F32, 64 + 4 * s) for s in range(2)]
    hn0 = [at(f"hn0{s}", [P, D], F32, 72 + 4 * s) for s in range(2)]
    gain_x = at("gain_x", [P, D], F32, 80)
    gain_m = at("gain_m", [P, D], F32, 84)
    mT_h = at("mT_h", [P, KC, MEM], F32R, 88)
    mT_l = at("mT_l", [P, KC, MEM], F32R, 96)
    km0 = at("km0", [P, KC, MEM], F32, 104)
    vm0 = at("vm0", [P, MT, D], F32, 112)
    junk0 = at("junk0", [P, D], F32, 120)
    vmt = [at(f"vmt{s}", [P, MEM], F32, 124 + s) for s in range(2)]
    tokT = [at(f"tokT{s}", [P, SEQ], F32, 84 + 4 * s) for s in range(3)]
    pool_a = at("pool_a", [P, SEQ], F32, 64)
    pool_b = at("pool_b", [P, SEQ], F32, 68)
    sig = at("sig", [P, SEQ], F32, 72)
    q_st = at("q_st", [P, NH, SEQ], F32R, 64)
    k_h = at("k_h", [P, 2, NKV, SEQ], F32R, 96)
    k_l = at("k_l", [P, 2, NKV, SEQ], F32R, 112)
    v_sw = at("v_sw", [P, NT, 2, P], F32, 128)
    c_st = [at("kc_st", [P, NKV, SEQ], F32, 136), at("vc_st", [P, NKV, SEQ], F32, 144)]
    pu = at("pu", [P, 2, SEQ], F32, 152)
    ch = at("ch", [P, 2, SEQ], F32, 160)
    ca = at("ca", [P, 2, SEQ], F32, 168)
    cm = [at("cm_k", [P, 16, NKV, NCMP], F32, 184), at("cm_v", [P, 16, NKV, NCMP], F32, 192)]
    ctmp = at("ctmp", [P, SEQ], F32, 176)
    cln = at("cln", [P, SEQ], F32, 180)
    tn = at("tn", [P, NH, NEAR], F32, 136)
    tc = at("tc", [P, NH, ZC], F32, 144)
    wm = at("wm", [P, 3 * P], F32, 194.5)
    p_sel = at("p_sel", [P, QPK, SEQ], F32, 148)
    p_win = at("p_win", [P, QPK, 5 * P + CPAD], F32, 164)
    v_st = at("v_st", [P, NT * 2 * NKV, 2 * HD], F32R, 176)
    pt_h = [at(f"pt_h{s}", [P, HALF], F32R, 128 + 2 * s) for s in range(3)]
    pt_l = [at(f"pt_l{s}", [P, HALF], F32R, (134, 196, 198)[s]) for s in range(3)]
    wb_h = at("wb_h", [P, KC, D], F32R, 64)
    wb_l = at("wb_l", [P, KC, D], F32R, 96)
    upd = [at(f"upd{s}", [P, D], F32, 128 + 4 * s) for s in range(2)]
    res = [at(f"res{s}", [P, D], F32, 136 + 4 * s) for s in range(2)]
    hn = [at(f"hn{s}", [P, D], F32, 144 + 4 * s) for s in range(2)]
    gain_post = at("gain_post", [P, D], F32, 152)
    gain_pre = at("gain_pre", [P, D], F32, 156)
    junk = at("junk", [P, D], F32, 160)
    xq = at("xq", [P, KC, SEQ], F32, 128)
    km = at("km", [P, KC, MEM], F32, 160)
    vm = at("vm", [P, MT, D], F32, 168)
    xp = [at(f"xp{s}", [P, XH, MEM], F32, 184 + 4 * s) for s in range(2)]
    xpt = [at(f"xpt{s}", [P, MT, XH, P], F32, 192 + 4 * s) for s in range(2)]
    acc = at("acc", [P, NT, D], F32, 64)
    hid_h = at("hid_h", [P, GROUP, SEQ], F32R, 96)
    hid_l = at("hid_l", [P, GROUP, SEQ], F32R, 112)
    w2_h = at("w2_h", [P, GROUP, D], F32R, 128)
    w2_l = at("w2_l", [P, GROUP, D], F32R, 144)
    rl = [at(f"rl{s}", [P, SEQ], F32, 160 + 4 * s) for s in range(2)]
    gain_f = at("gain_f", [P, D], F32, 168)
    junk_f = at("junk_f", [P, D], F32, 172)
    res_f = [at(f"res_f{s}", [P, D], F32, 176 + 4 * s) for s in range(2)]
    upd_f = [at(f"upd_f{s}", [P, D], F32, 160 + 4 * s) for s in range(2)]
    wraw = [at(f"wraw{s}", [P, D], F32, 176 + 4 * s) for s in range(2)]
    wmore = [at(f"wmore{s}", [P, D], F32, 184 + 4 * s) for s in range(4)]
    tw_h = [at(f"tw_h{s}", [P, KC, P], F32R, 184 + 8 * s) for s in range(2)]
    tw_l = [at(f"tw_l{s}", [P, KC, P], F32R, 188 + 8 * s) for s in range(2)]
    ident = at("ident", [P, P], F32, 200)
    ones = at("ones", [P, P], F32, 200.5)
    sm = at("sm", [P, SMW], F32, 201)
    gates = at("gates", [P, NT, 24], F32, 202)
    o_b = at("o_b", [HD, HALF], F32, 202.75)
    o_sum = at("o_sum", [P, 2, P], F32, 175)
    cw2k = at("cw2k", [P, 2, 2, HD], F32, 202.75)
    hid_c = at("hid_c", [P, 2, NKV * NCMP], F32, 203.75)
    kc_h = at("kc_h", [P, KCW], F32R, 192)
    kc_l = at("kc_l", [P, KCW], F32R, 193.25)
    vc = at("vc", [P, NKV, 2 * HD], F32R, 204.75)
    cw2v = at("cw2v", [P, 2, HD], F32, 206.25)
    half_neg = at("half_neg", [P, 16], F32, 206.75)
    neg_one = at("neg_one", [P, 1], F32, 207.125)
    ss = at("ss", [P, 10], F32, 206.875)
    rstd = at("rstd", [P, 10], F32, 206.9375)
    mx = at("mx", [P, 3], F32, 207)
    nmx = at("nmx", [P, 2, 2], F32, 207.0625)
    sums = at("sums", [P, 2, QPK, 3], F32, 205.75)
    rsum = at("rsum", [P, 2, QPK, 3], F32, 205.875)
    xs = at("xs", [P, 3, XH], F32, 207.3125)
    t16 = at("t16", [P, 16], F32, 207.375)
    ssb = at("ssb", [P, 2, 2], F32, 207.5)
    rsb = at("rsb", [P, 2, 2], F32, 207.5625)
    pw = at("pw", [P, 2, P], F32, 203.75)
    cpw = at("cpw", [P, 2, CMP_HID], F32, 44)
    oh = at("oh", [OHR, ND], BF16, 12)
    rb = at("rb", [3 * NBUCKET, NH], F32, 207.625)
    rb1 = at("rb1", [3 * NBUCKET, NH], F32, 207.65625)
    rb2 = at("rb2", [3 * NBUCKET, NH], F32, 207.6875)
    rhm = at("rhm", [3 * NBUCKET, 2, NH], BF16, 207.71875)
    relb = at("relb", [OHR, NH], BF16, 207.75)

    from contextlib import ExitStack
    ctx = ExitStack()
    with ctx:
        ps = ctx.enter_context(nc.psum_tensor("ps", [P, 8, HALF], F32))

        def sem(name):
            return ctx.enter_context(nc.semaphore(name))

        def pair(j):
            return ps[:, 2 * j:2 * j + 2, :].rearrange("p a b -> p (a b)")

        def smc(name, j=0, rows=slice(0, P)):
            return sm[rows, SM[name][0] + j:SM[name][0] + j + 1]

        raw_in = [sem("raw_in0"), sem("raw_in1")]
        more_in = [sem(f"more_in{s}") for s in range(4)]
        wh_done, wl_done = sem("wh_done"), sem("wl_done")
        first_in, gain_in = sem("first_in"), sem("gain_in")
        const_in, store0 = sem("const_in"), sem("store0")
        x_ld, mem_ld = [sem("x_ld0"), sem("x_ld1")], [sem("mem_ld0"), sem("mem_ld1")]
        ph_in, oh_in, wm_in, kv_in = sem("ph_in"), sem("oh_in"), sem("wm_in"), sem("kv_in")
        ss_n, rs_n, hn_n, tr_n, hh_n, hl_n, msq = (sem(n) for n in ("ss_n", "rs_n", "hn_n", "tr_n", "hh_n", "hl_n", "msq"))
        consts_set = sem("consts_set")
        gemm, ev_act, ev_dve, tok_tr, tok_ev = (sem(n) for n in ("gemm", "ev_act", "ev_dve", "tok_tr", "tok_ev"))
        sig_step, pool_step, conv_step = sem("sig_step"), sem("pool_step"), sem("conv_step")
        end = {n: sem("end_" + n) for n in ("pe", "act", "dve")}
        fb = {n: sem("fb_" + n) for n in (
            "rb", "relb", "tab", "tab_ev", "pool", "pool_h", "pool_l", "cm", "hid", "gelu", "kc", "kc_h",
            "vc", "vc_ev", "mean", "dev", "sq", "var", "sd", "rec", "z", "silu", "pw", "pw_h", "chain")}
        at_ = {n: sem("at_" + n) for n in (
            "qk", "chain", "max", "exp", "rs", "pn", "tr", "v_h", "v_l", "pt_h", "pt_l", "pv", "o_b", "o_sum", "o_h", "o_l")}
        bo = [{n: sem(f"bo{s}_" + n) for n in (
            "mm", "ss", "rs", "up", "x", "ss2", "rs2", "hn", "tr", "hh", "hl", "res0", "res1", "gain", "st0", "st1",
            "sq", "psq")}
            for s in range(2)]
        xa = {n: sem("xa_" + n) for n in ("q_ev", "s", "max", "exp", "pn", "tr", "pt", "pv", "oh", "ol", "chain")}
        ml = {n: sem("ml_" + n) for n in ("up", "relu", "sq", "hh", "hl", "dn", "acc", "ss", "rs", "y", "gain", "res0",
                                          "res1", "st0", "st1", "fin", "psq")}

        x_t = a["x"].rearrange("(t p) d -> t p d", p=P)
        x1_t = a["x1"].rearrange("(t p) d -> t p d", p=P)
        x2_t = a["x2"].rearrange("(t p) d -> t p d", p=P)
        out_t = a["out"].rearrange("(t p) d -> t p d", p=P)
        mem_t = a["mem"].rearrange("(t p) d -> t p d", p=P)

        def w_dram(name, c):
            if name in ("wout", "wo"):
                return a[name][c * P:(c + 1) * P, :]
            return a[name][c].rearrange("p k n -> p (k n)")

        def raw(n):
            i = n - N_OUT - 2
            if 0 <= i < 4:
                return wmore[i][:, :], more_in[i], 16
            return wraw[n % 2][:, :], raw_in[n % 2], 16 * (n // 2 + 1 - (2 if i >= 4 else 0))

        def t_index(n):
            if n < N_OUT:
                return n
            return J_Q + n - N_Q if N_Q <= n < N_O else None

        def w_dest(n):
            j = t_index(n)
            if j is None:
                k = PIECES[n][1]
                return wb_h[:, k, :], wb_l[:, k, :]
            return (tw_h[j % 2][:, :, :].rearrange("p k n -> p (k n)"),
                    tw_l[j % 2][:, :, :].rearrange("p k n -> p (k n)"))

        READS = [PIECES[j][0] == "in" and PIECES[j][1] in (10, 11, 12, 14, 6, 7, 8, 9) for j in range(N_OUT)]

        def dve_reads(j):
            return sum(READS[:j + 1])

        TOK_AT = [j for j in range(N_OUT) if (8 <= j < N_IN) or (j >= N_IN and PIECES[j][1] in TOK)]

        SUB = [(i, g, kind) for i in range(NT) for g in range(NKV) for kind in (0, 1)]

        def tiles_of(s):
            i, _, kind = SUB[s]
            return i + 1 if kind == 0 else min(WIN_TILES + 1, i + 1) + 1

        def attention_order():
            n = len(SUB)
            out = [("row", 0, r) for r in range(QPK)]
            for s in range(n):
                tiles = tiles_of(s)
                before = [r * tiles // (QPK + 1) if tiles > 3 else 0 for r in range(QPK)] if s + 1 < n else []
                for t in range(tiles + 1):
                    out += [("row", s + 1, r) for r, u in enumerate(before) if u == t]
                    if t < tiles:
                        out.append(("tile", s, t))
            return out

        ORDER = attention_order()

        def exp_order():
            out, waiting = [], []
            for what, s, k in ORDER:
                if what == "row":
                    if len(waiting) == 2:
                        out.append(waiting.pop(0))
                    waiting.append((what, s, k))
                else:
                    out += [e for e in waiting if e[1] == s]
                    out.append((what, s, k))
                    out += [e for e in waiting if e[1] > s]
                    waiting = []
            return out

        TAKE, FINISH = {}, {}
        for _u in range(1, len(SUB) // 2):
            _tiles = [e for e in ORDER if e[0] == "tile" and e[1] >= 2 * _u]
            TAKE[_tiles[2]] = FINISH[_tiles[3]] = _u - 1

        TILE0 = [sum(tiles_of(s) for s in range(k)) for k in range(len(SUB) + 1)]

        def width(i, kind):
            return P * (i + 1) if kind == 0 else P * min(WIN_TILES + 1, i + 1)

        def row_at(i, kind):
            w = width(i, kind)
            return HALF - WIDE if w == 5 * P else (HALF if kind == 1 else 0)

        block = ctx.enter_context(nc.Block())

        @block.sync
        def _(sp):
            sp.dma_start(gain_m[:, :], a["mem_g"].partition_broadcast(P)).then_inc(first_in, 16)
            sp.dma_start(ident[:, :], a["ident"]).then_inc(first_in, 16)
            for n in range(N_MLP):
                if n == 2:
                    sp.dma_start(gain_x[:, :], a["mix_pre_g"].partition_broadcast(P)).then_inc(gain_in, 16)
                if n == N_OUT:
                    sp.wait_ge(at_["pv"], TILE0[-2] + 1)
                if n == N_OUT + 2:
                    sp.wait_ge(end["pe"], 3)
                elif N_OUT + 6 <= n < N_OUT + 8:
                    sp.wait_ge(wl_done, n - 5)
                elif n >= 2 and not N_OUT + 2 < n < N_OUT + 6:
                    sp.wait_ge(wl_done, n - 1)
                sp.dma_start(raw(n)[0], w_dram(*PIECES[n])).then_inc(raw(n)[1], 16)

            def mlp_piece(g, c, w):
                n = N_MLP + c
                sp.wait_ge(wl_done, g * 8 + (n - 1))
                sp.dma_start(wraw[n % 2][:, :], w).then_inc(raw_in[n % 2], 16)

            with sp.Fori(0, NGROUP) as g:
                for c in range(GROUP):
                    mlp_piece(g, c, a["w1"][bass.ds(g * GROUP + c, 1)].rearrange("a p k n -> p (a k n)"))
                for c in range(GROUP):
                    mlp_piece(g, GROUP + c, a["w2"][bass.ds(g * GROUP + c, 1)].rearrange("a p n -> p (a n)"))

            sp.wait_ge(wl_done, N_MLP + 2 * GROUP * NGROUP)
            for t in range(2):
                sp.dma_start(res_f[t][:, :], x2_t[t]).then_inc(ml[f"res{t}"], 16)
            for t in range(NT):
                sp.wait_ge(ml["fin"], t + 1)
                sp.dma_start(out_t[t], upd_f[t % 2][:, :]).then_inc(ml[f"st{t % 2}"], 16)
                if t + 2 < NT:
                    sp.dma_start(res_f[t % 2][:, :], x2_t[t + 2]).then_inc(ml[f"res{t % 2}"], 16)
            for t in range(2):
                sp.wait_ge(ml[f"st{t}"], 16 * (NT // 2))

        @block.gpsimd
        def _(pool):
            pool.memset(half_neg[:, :], -0.5).then_inc(consts_set, 1)
            pool.memset(neg_one[:, :], -1.0).then_inc(consts_set, 1)
            pool.memset(ones[:, :], 1.0 / 256).then_inc(consts_set, 1)
            pool.wait_ge(consts_set, 3)

            def inv_rms(src, dst, ready, chain, n, done):
                pool.wait_ge(ready[0], ready[1])
                pool.tensor_scalar(src, src, 1.0 / D, EPS, ALU.mult, ALU.add).then_inc(chain, 1)
                pool.wait_ge(chain, n)
                pool.tensor_tensor(dst, src, half_neg[:, 0:1], ALU.pow).then_inc(done, 1)

            small_loads = [(sm[:, :], a["small"]), (pw[:, :, :], a["pool_w"]),
                           (cw2v[:, :, :], a["cmp_v_w2"].rearrange("(t p) n -> p t n", p=P))]
            small_loads += [(cw2k[:, :, s, :], a["cmp_k_w2"].rearrange("(t p) n -> p t n", p=P)) for s in range(2)]
            small_loads += [(rb[32 * s:32 * s + 32, :], a["rel_bias"]) for s in range(3)]
            for u in range(MT + NT):
                inv_rms(ss[:, u:u + 1], rstd[:, u:u + 1], (ss_n, u + 1), msq, u + 1, rs_n)
                if u + 2 < MT + NT:
                    pool.wait_ge(hn_n, u + 1)
                    pool.dma_start(x_in[u % 2][:, :], x_t[u + 2 - MT]).then_inc(x_ld[u % 2], 16)
                if 2 <= u < 2 + len(small_loads):
                    pool.dma_start(*small_loads[u - 2]).then_inc(const_in, 16)
            pool.wait_ge(ev_act, 8)
            pool.wait_ge(tok_ev, 8)
            pool.dma_start(a["kmd"], km0[:, :, :]).then_inc(store0, 16)
            pool.dma_start(a["vmd"], vm0[:, :, :]).then_inc(store0, 16)
            pool.wait_ge(store0, 32)

            pool.wait_ge(end["pe"], 1)
            pool.dma_start(oh[:, :], a["onehot"]).then_inc(oh_in, 16)
            pool.dma_start(cw1[0][:, :, :], a["cmp_k_w1"].rearrange("(j p) n -> p j n", p=P)).then_inc(ph_in, 16)
            pool.dma_start(cw1[1][:, :, :], a["cmp_v_w1"].rearrange("(j p) n -> p j n", p=P)).then_inc(ph_in, 16)
            pool.dma_start(cpw[:, :, :], a["conv_pw"].rearrange("(t p) n -> p t n", p=P)).then_inc(ph_in, 16)
            pool.wait_ge(fb["hid"], 2)
            pool.dma_start(wm[:, :], a["winmask"]).then_inc(wm_in, 16)

            for what, s, r in ORDER:
                if what == "row":
                    i, g, kind = SUB[s]
                    h, w = QPK * g + r, width(i, kind)
                    c = rsum[:, kind, r, :]
                    pool.wait_ge(at_["exp"], s * QPK + r + 1)
                    cs = slice(1, 2) if kind == 0 else slice(0, 3, 2)
                    pool.tensor_tensor(rsum[:, kind, r, cs], sums[:, kind, r, cs],
                                       neg_one[:, 0:1].to_broadcast([P, 1 + kind]), ALU.pow).then_inc(at_["rs"], 1)
                    pool.wait_ge(at_["rs"], s * QPK + r + 1)
                    if kind == 0:
                        pool.tensor_scalar(p_sel[:, r, 0:w], p_sel[:, r, 0:w], c[:, 1:2], gates[:, i, 3 * h + 1:3 * h + 2],
                                           ALU.mult, ALU.mult).then_inc(at_["pn"], 1)
                    else:
                        pool.tensor_scalar(p_win[:, r, 0:w], p_win[:, r, 0:w], c[:, 2:3], gates[:, i, 3 * h + 2:3 * h + 3],
                                           ALU.mult, ALU.mult)
                        cc = p_win[:, r, 5 * P:5 * P + CPAD]
                        pool.tensor_scalar(cc, cc, c[:, 0:1], gates[:, i, 3 * h:3 * h + 1], ALU.mult, ALU.mult)\
                            .then_inc(at_["pn"], 1)

            def block_out(s, src, dst, last_phase):
                b = bo[s]
                for n in ("pe", "act", "dve"):
                    pool.wait_ge(end[n], last_phase)
                pool.dma_start(gain_post[:, :], a[("mix_post_g", "xa_post_g")[s]].partition_broadcast(P)).then_inc(b["gain"], 16)
                pool.dma_start(gain_pre[:, :], a[("xa_pre_g", "mlp_pre_g")[s]].partition_broadcast(P)).then_inc(b["gain"], 16)
                for t in range(2):
                    pool.dma_start(res[t][:, :], src[t]).then_inc(b[f"res{t}"], 16)
                for t in range(NT):
                    inv_rms(ssb[:, 0, t % 2:t % 2 + 1], rsb[:, 0, t % 2:t % 2 + 1], (b["ss"], t + 1), b["sq"], 2 * t + 1, b["rs"])
                    inv_rms(ssb[:, 1, t % 2:t % 2 + 1], rsb[:, 1, t % 2:t % 2 + 1], (b["ss2"], t + 1), b["sq"], 2 * t + 2, b["rs2"])
                    pool.dma_start(dst[t], upd[t % 2][:, :]).then_inc(b[f"st{t % 2}"], 16)
                    if t + 2 < NT:
                        pool.dma_start(res[t % 2][:, :], src[t + 2]).then_inc(b[f"res{t % 2}"], 16)
                for t in range(2):
                    pool.wait_ge(b[f"st{t}"], 16 * (NT // 2))

            block_out(0, x_t, x1_t, 3)
            for n in ("pe", "act", "dve"):
                pool.wait_ge(end[n], 4)
            pool.dma_start(km[:, :, :], a["kmd"]).then_inc(kv_in, 16)
            pool.dma_start(vm[:, :, :], a["vmd"]).then_inc(kv_in, 16)
            block_out(1, x1_t, x2_t, 6)

            for n in ("pe", "act", "dve"):
                pool.wait_ge(end[n], 7)
            pool.dma_start(gain_f[:, :], a["mlp_post_g"].partition_broadcast(P)).then_inc(ml["gain"], 16)
            for t in range(NT):
                inv_rms(ssb[:, 0, t % 2:t % 2 + 1], rsb[:, 0, t % 2:t % 2 + 1], (ml["ss"], t + 1), ml["psq"], t + 1, ml["rs"])

        def three_pass(pe, out, lh, ll, rh, rl_, first, last):
            nc.tensor.matmul(out, lh, rh, start=first, stop=False)
            nc.tensor.matmul(out, lh, rl_, start=False, stop=False)
            return nc.tensor.matmul(out, ll, rh, start=False, stop=last)

        def t_product(pe, j, rh, rl_, out, cols):
            for c0 in range(0, cols, HALF):
                w = min(HALF, cols - c0)
                for k in range(KC):
                    last = three_pass(pe, out[:, c0:c0 + w], tw_h[j % 2][:, k, :], tw_l[j % 2][:, k, :],
                                      rh[:, k, c0:c0 + w], rl_[:, k, c0:c0 + w], k == 0, k == KC - 1)
            return last

        def t_product_half(pe, j, out, hf):
            cs = slice(hf * HALF, (hf + 1) * HALF)
            return t_product(pe, j, hT_h[:, :, cs], hT_l[:, :, cs], out[:, cs], HALF)

        def n_product(pe, lh, ll, rh, rl_, out):
            for k in range(KC):
                last = three_pass(pe, out, lh[:, k], ll[:, k], rh[:, k], rl_[:, k], k == 0, k == KC - 1)
            return last

        @block.tensor
        def _(pe):
            pe.wait_ge(first_in, 32)

            def transposes(u, src, ready, need, done, free):
                pe.wait_ge(ready, need)
                if free is not None:
                    pe.wait_ge(*free)
                for k in range(KC):
                    last = nc.tensor.transpose(pair(2 + u % 2)[:, k * P:(k + 1) * P], src[:, k * P:(k + 1) * P], ident[:, :])
                last.then_inc(done, 1)

            def chunk(j):
                pe.wait_ge(wl_done, j + 1)
                if N_IN <= j < N_IN + 2:
                    pe.wait_ge(tok_ev, j - N_IN + 7)
                if j >= 2:
                    pe.wait_ge(ev_act, j - 1)
                    if dve_reads(j - 2):
                        pe.wait_ge(ev_dve, dve_reads(j - 2))
                if j < N_IN:
                    t_product(pe, j, mT_h, mT_l, pair(j % 2), MEM).then_inc(gemm, 1)
                else:
                    t_product(pe, j, hT_h, hT_l, pair(j % 2), SEQ).then_inc(gemm, 1)

            def tokens_first(j):
                n = TOK_AT.index(j)
                pe.wait_ge(ev_act, j + 1)
                if j < N_IN:
                    if n >= 2:
                        pe.wait_ge(tok_ev, n - 1)
                    for t in range(MT):
                        last = nc.tensor.transpose(ps[:, 2 * (j % 2) + 1, t * P:(t + 1) * P], vmt[j % 2][:, t * P:(t + 1) * P],
                                                   ident[:, :])
                else:
                    k = n - 8
                    if k == 2:
                        pe.wait_ge(tok_ev, 9)
                    w = 24 if k == 2 else P
                    for t in range(NT):
                        last = nc.tensor.transpose(pair(2 + k % 2)[:, w * t:w * t + w], tokT[k][0:w, t * P:(t + 1) * P],
                                                   ident[0:w, 0:w])
                last.then_inc(tok_tr, 1)

            for u in range(MT + NT):
                transposes(u, hn0[u % 2], hn_n, u + 1, tr_n, (hl_n, u - 1) if u >= 2 else None)
                if u >= MT:
                    if u == MT:
                        pe.wait_ge(hl_n, MT)
                    for j in (2 * (u - MT), 2 * (u - MT) + 1):
                        chunk(j)
                        if j - 1 in TOK_AT:
                            tokens_first(j - 1)
            pe.wait_ge(hl_n, MT + NT)
            tokens_first(N_IN - 1)
            for j in range(N_IN, N_OUT):
                chunk(j)
                if j - 1 in TOK_AT and j > N_IN:
                    tokens_first(j - 1)
            pe.drain().then_inc(end["pe"], 1)
            def pool_product(c, out):
                for hf in range(2):
                    last = nc.tensor.matmul(out[:, hf * HALF:(hf + 1) * HALF], pw[:, c, :], pu[:, c, hf * HALF:(hf + 1) * HALF],
                                            start=True, stop=True)
                last.then_inc(fb["pool"], 1)

            def channel_mean(src, out, done):
                for hf in range(2):
                    for c in range(2):
                        last = nc.tensor.matmul(out[:, hf * HALF:(hf + 1) * HALF], ones[:, :], src[:, c, hf * HALF:(hf + 1) * HALF],
                                                start=c == 0, stop=c == 1)
                last.then_inc(done, 1)

            pe.wait_ge(const_in, 16 * 8)
            pe.wait_ge(pool_step, POOL_STEPS)
            pe.wait_ge(ev_act, N_OUT - 1)
            pe.wait_ge(ev_dve, dve_reads(N_OUT - 2))
            pool_product(0, pair(1))
            pe.wait_ge(tok_ev, 11)
            pe.wait_ge(oh_in, 16)
            pe.wait_ge(fb["relb"], 1)
            for xcol in range(NEAR):
                o = P - xcol - DMIN
                last = nc.tensor.matmul(ps[:, 4 + xcol // 64, (xcol % 64) * 8:(xcol % 64) * 8 + 8], oh[:, o:o + P], relb[:, :],
                                        start=True, stop=True)
            last.then_inc(fb["tab"], 1)
            for n in ("act", "dve"):
                pe.wait_ge(end[n], 1)
            pe.wait_ge(consts_set, 3)
            channel_mean(ca, pair(0), fb["mean"])
            pe.wait_ge(fb["pool_l"], 1)
            for z in range(ZC):
                o = -CMP_STRIDE * (z - 56) - (CMP_LEN - 1) - DMIN
                last = nc.tensor.matmul(ps[:, 2 + z // 64, (z % 64) * 8:(z % 64) * 8 + 8], oh[:, o:o + P], relb[:, :],
                                        start=True, stop=True)
            last.then_inc(fb["tab"], 1)
            pe.wait_ge(fb["sq"], 2)
            channel_mean(ch, pair(0), fb["var"])
            pe.wait_ge(ph_in, 48)
            pe.wait_ge(fb["tab_ev"], 1)
            pool_product(1, pair(3))
            for kv in range(2):
                pe.wait_ge(fb["cm"], kv + 1)
                for ht in range(2):
                    for j in range(16):
                        last = nc.tensor.matmul(ps[:, 4 + kv, 126 * ht:126 * ht + 126], cw1[kv][:, j, ht * P:(ht + 1) * P],
                                                cm[kv][:, j, :, :], start=j == 0, stop=j == 15)
                last.then_inc(fb["hid"], 1)
            pe.wait_ge(fb["gelu"], 1)
            for ht in range(2):
                last = nc.tensor.matmul(ps[:, 4, 256:382], cw2k[:, ht, :, :], hid_c[:, ht, :], start=ht == 0, stop=ht == 1)
            last.then_inc(fb["kc"], 1)
            pe.wait_ge(fb["silu"], 2)
            pe.wait_ge(fb["tab_ev"], 2)
            for m in range(2):
                for hf in range(2):
                    for c in range(2):
                        last = nc.tensor.matmul(ps[:, 2 - 2 * m + hf, :], cpw[:, c, m * P:(m + 1) * P],
                                                ca[:, c, hf * HALF:(hf + 1) * HALF], start=c == 0, stop=c == 1)
                last.then_inc(fb["pw"], 1)
                if m == 0:
                    pe.wait_ge(fb["gelu"], 2)
                    for g in range(NKV):
                        for ht in range(2):
                            last = nc.tensor.matmul(ps[0:NCMP, 5, 256 + HD * g:256 + HD * g + HD],
                                                    hid_c[:, ht, g * NCMP:(g + 1) * NCMP], cw2v[:, ht, :],
                                                    start=ht == 0, stop=ht == 1)
                    last.then_inc(fb["vc"], 1)
            pe.drain().then_inc(end["pe"], 1)
            for n in ("act", "dve"):
                pe.wait_ge(end[n], 2)

            def score_row(s, r):
                i, g, kind = SUB[s]
                n = s * QPK + r
                h = QPK * g + r
                if n >= 2:
                    pe.wait_ge(at_["exp"], n - 1)
                sc = pair(n % 2)
                qs = q_st[:, h, i * P:(i + 1) * P]
                w = width(i, kind)
                k0 = (i + 1) * P - w
                b0 = row_at(i, kind)
                w = max(w, WIDE)
                for c0 in range(b0 - b0 % HALF, b0 + w, HALF):
                    c, e = max(c0, b0), min(c0 + HALF, b0 + w)
                    ks = slice(k0 + c - b0, k0 + e - b0)
                    nc.tensor.matmul(sc[:, c:e], qs, k_h[:, kind, g, ks], start=True, stop=False)
                    last = nc.tensor.matmul(sc[:, c:e], qs, k_l[:, kind, g, ks], start=False, stop=True)
                if kind == 1:
                    cc, ks = sc[:, 0:WIDE], slice(g * CPAD, g * CPAD + WIDE)
                    nc.tensor.matmul(cc, qs, kc_h[:, ks], start=True, stop=False)
                    last = nc.tensor.matmul(cc, qs, kc_l[:, ks], start=False, stop=True)
                last.then_inc(at_["qk"], 1)

            def key_tile_transposed(s, t):
                i, g, kind = SUB[s]
                n = TILE0[s] + t
                if n >= 2:
                    pe.wait_ge(at_["pt_l"], n - 1)
                cmp_tile = kind == 1 and t == tiles_of(s) - 1
                for r in range(QPK):
                    src = p_sel[:, r, t * P:(t + 1) * P] if kind == 0 else (
                        p_win[:, r, 5 * P:5 * P + NCMP] if cmp_tile else p_win[:, r, t * P:(t + 1) * P])
                    rows = NCMP if cmp_tile else P
                    if t == 0:
                        pe.wait_ge(at_["pn"], QPK * s + r + 1)
                    last = nc.tensor.transpose(ps[0:rows, 4 + n % 2, r * P:(r + 1) * P], src, ident[:, :])
                last.then_inc(at_["tr"], 1)

            def key_tile_product(s, t):
                i, g, kind = SUB[s]
                n = TILE0[s] + t
                unit = s // 2
                first = kind == 0 and t == 0
                end_of_unit = kind == 1 and t == tiles_of(s) - 1
                pe.wait_ge(at_["pt_l"], n + 1)
                if first and unit >= 2:
                    pe.wait_ge(at_["o_sum"], unit - 1)
                o = ps[:, 6 + unit % 2, :]
                if end_of_unit:
                    w, rows = vc[0:NCMP, g, :], slice(0, NCMP)
                else:
                    kt = t if kind == 0 else max(0, i - WIN_TILES) + t
                    w, rows = v_st[:, (kt * 2 + kind) * NKV + g, :], slice(0, P)
                nc.tensor.matmul(o, w, pt_h[n % 3][rows, :], start=first, stop=False)
                last = nc.tensor.matmul(o, w, pt_l[n % 3][rows, :], start=False, stop=end_of_unit)
                last.then_inc(at_["pv"], 1)

            pe.wait_ge(at_["v_l"], 1)
            tiles = [(s, t) for what, s, t in ORDER if what == "tile"]
            at_tile = 0
            for what, s, k in ORDER:
                if what == "row":
                    score_row(s, k)
                else:
                    key_tile_transposed(s, k)
                    if at_tile >= 2:
                        key_tile_product(*tiles[at_tile - 2])
                    at_tile += 1
            key_tile_product(*tiles[-2])
            key_tile_product(*tiles[-1])
            pe.drain().then_inc(end["pe"], 1)

            def block_operands(t, hf, k):
                ts, c = slice(t * P, (t + 1) * P), slice(hf * HALF, (hf + 1) * HALF)
                return pair(t % 2)[:, c], hT_h[:, k, ts], hT_l[:, k, ts], wb_h[:, k, c], wb_l[:, k, c]

            def block_start(s, n0, between):
                def step(t, k):
                    for hf in range(2):
                        last = three_pass(pe, *block_operands(t, hf, k), k == 0, k == KC - 1)
                    return last

                for k in range(KC - 2):
                    pe.wait_ge(wl_done, n0 + k + 1)
                    for t in range(2):
                        step(t, k)
                    if k == 1:
                        between()
                for t in range(2):
                    pe.wait_ge(wl_done, n0 + KC - 1)
                    step(t, KC - 2)
                    pe.wait_ge(wl_done, n0 + KC)
                    step(t, KC - 1).then_inc(bo[s]["mm"], 1)

            def block_rest(s, j_next, n_next):
                b = bo[s]

                def tile_t(t):
                    pe.wait_ge(b["up"], t - 1)
                    for hf in range(2):
                        for k in range(KC):
                            last = three_pass(pe, *block_operands(t, hf, k), k == 0, k == KC - 1)
                    last.then_inc(b["mm"], 1)

                def next_input(t):
                    transposes(t, hn[t % 2], b["hn"], t + 1, b["tr"], (b["hl"], t - 1) if t >= 2 else None)

                def next_product(c):
                    pe.wait_ge(wl_done, n_next + c + 1)
                    pe.wait_ge(b["up"], NT - 1 + c)
                    t_product_half(pe, j_next + c, pair(c), 0)

                for t in range(2, NT):
                    tile_t(t)
                    next_input(t - 2)
                next_input(NT - 2)
                pe.wait_ge(b["hl"], NT // 2)
                next_product(0)
                next_input(NT - 1)
                next_product(1)


            def attention_taken():
                for n in ("act", "dve"):
                    pe.wait_ge(end[n], 3)

            pe.wait_ge(at_["exp"], QPK * len(SUB))
            block_start(0, N_OUT, attention_taken)
            block_rest(0, J_Q, N_Q)
            pe.drain().then_inc(end["pe"], 1)
            for n in ("act", "dve"):
                pe.wait_ge(end[n], 4)
            for m in range(8):
                pe.wait_ge(wl_done, N_Q + m + 1)
                if m >= 2:
                    pe.wait_ge(xa["q_ev"], m - 1)
                if m >= 2:
                    t_product_half(pe, J_Q + m, pair(m % 2), 0)
                t_product_half(pe, J_Q + m, pair(m % 2), 1).then_inc(gemm, 1)
            pe.drain().then_inc(end["pe"], 1)
            for n in ("act", "dve"):
                pe.wait_ge(end[n], 5)
            pe.wait_ge(kv_in, 32)

            def x_scores(t):
                if t >= 2:
                    pe.wait_ge(xa["exp"], XH * (t - 1))
                for h in range(XH):
                    for c in range(2):
                        last = nc.tensor.matmul(pair(t % 2)[:, h * MEM:(h + 1) * MEM], xq[:, 2 * h + c, t * P:(t + 1) * P],
                                                km[:, 2 * h + c, :], start=c == 0, stop=c == 1)
                last.then_inc(xa["s"], 1)

            def x_transposes(t):
                pe.wait_ge(xa["pn"], t + 1)
                if t >= 1:
                    pe.wait_ge(xa["pt"], t)
                for m in range(MT):
                    for h in range(XH):
                        last = nc.tensor.transpose(pair(2)[:, (m * XH + h) * P:(m * XH + h + 1) * P],
                                                   xp[t % 2][:, h, m * P:(m + 1) * P], ident[:, :])
                last.then_inc(xa["tr"], 1)

            def x_values(t):
                pe.wait_ge(xa["pt"], t + 1)
                if t >= 1:
                    pe.wait_ge(xa["ol"], t)
                for c in range(KC):
                    for m in range(MT):
                        last = nc.tensor.matmul(pair(3)[:, c * P:(c + 1) * P], vm[:, m, c * P:(c + 1) * P],
                                                xpt[t % 2][:, m, c // 2, :], start=m == 0, stop=m == MT - 1)
                last.then_inc(xa["pv"], 1)

            x_scores(0)
            for t in range(NT):
                if t + 1 < NT:
                    x_scores(t + 1)
                x_transposes(t)
                if t >= 1:
                    x_values(t - 1)

            def x_end():
                x_values(NT - 1)
                pe.drain().then_inc(end["pe"], 1)

            pe.wait_ge(xa["exp"], XH * NT)
            block_start(1, N_O, x_end)
            for n in ("act", "dve"):
                pe.wait_ge(end[n], 6)
            block_rest(1, J_MLP, N_MLP)
            pe.drain().then_inc(end["pe"], 1)
            for n in ("act", "dve"):
                pe.wait_ge(end[n], 7)

            def mlp_group(g, first_done=False):
                for c in range(GROUP):
                    if not (first_done and c < 2):
                        pe.wait_ge(wl_done, g * 8 + (N_MLP + c + 1))
                        pe.wait_ge(ml["relu"], g * GROUP + (c + 1))
                        t_product_half(pe, J_MLP + c, pair(c % 2), 0)
                    t_product_half(pe, J_MLP + c, pair(c % 2), 1).then_inc(ml["up"], 1)

                def down(idx, chunks):
                    t, hf = idx // 2, idx % 2
                    ts, cs = slice(t * P, (t + 1) * P), slice(hf * HALF, (hf + 1) * HALF)
                    if chunks[0] == 0:
                        pe.wait_ge(ml["acc"], g * (2 * NT) + (idx + 1))
                    for c in chunks:
                        if idx == 0:
                            pe.wait_ge(wl_done, g * 8 + (N_MLP + GROUP + c + 1))
                            pe.wait_ge(ml["hl"], g * GROUP + (c + 3))
                        last = three_pass(pe, ps[:, 4 + idx % 4, :], hid_h[:, c, ts], hid_l[:, c, ts],
                                          w2_h[:, c, cs], w2_l[:, c, cs], c == 0, c == GROUP - 1)
                    if c == GROUP - 1:
                        last.then_inc(ml["dn"], 1)

                for idx in range(4):
                    down(idx, range(GROUP - 1))
                for idx in range(4):
                    down(idx, [GROUP - 1])
                for idx in range(4, 2 * NT):
                    down(idx, range(GROUP))

            mlp_group(0, first_done=True)
            with pe.Fori(1, NGROUP) as g:
                mlp_group(g)

        @block.scalar
        def _(act):
            def w_hi(n):
                act.wait_ge(*raw(n)[1:])
                j = t_index(n)
                if j is not None and j >= 2:
                    act.wait_ge(gemm, j - 1)
                nc.scalar.activation(w_dest(n)[0], raw(n)[0], ACT.Copy).then_inc(wh_done, 1)

            def sum_squares(src, out, scratch, done):
                nc.scalar.activation(scratch, src, ACT.Square, accum_out=out).then_inc(done, 1)

            for t in range(MT):
                act.dma_start(x_in[t][:, :], mem_t[t]).then_inc(mem_ld[t], 16)

            def mem_copy(j):
                act.wait_ge(gemm, j + 1)
                if j < 8:
                    act.activation(km0[:, j, :], pair(j % 2)[:, 0:MEM], ACT.Copy).then_inc(ev_act, 1)
                else:
                    if j >= 10:
                        act.wait_ge(tok_tr, j - 9)
                    act.activation(vmt[j % 2][:, :], pair(j % 2)[:, 0:MEM], ACT.Copy).then_inc(ev_act, 1)

            def mem_values(j):
                act.wait_ge(tok_tr, j - 7)
                act.activation(vm0[:, :, (j - 8) * P:(j - 7) * P],
                               ps[:, 2 * (j % 2) + 1, 0:MEM].rearrange("p (t c) -> p t c", t=MT), ACT.Copy).then_inc(tok_ev, 1)

            for u in range(MT + NT + 1):
                if u < MT + NT:
                    if u < MT:
                        act.wait_ge(mem_ld[u], 16)
                    else:
                        act.wait_ge(x_ld[u % 2], 16 * (u // 2))
                    if u >= 1:
                        act.wait_ge(ss_n, u)
                    sum_squares(x_in[u % 2][:, :], ss[:, u:u + 1], junk0[:, :], ss_n)
                    if u == 1:
                        w_hi(0)
                        w_hi(1)
                if u >= 1:
                    v = u - 1
                    act.wait_ge(tr_n, v + 1)
                    dst = mT_h[:, :, v * P:(v + 1) * P] if v < MT else hT_h[:, :, (v - MT) * P:(v - MT + 1) * P]
                    act.activation(dst, pair(2 + v % 2).rearrange("p (k c) -> p k c", k=KC), ACT.Copy).then_inc(hh_n, 1)
                    if v >= MT:
                        for j in (2 * (v - MT), 2 * (v - MT) + 1):
                            mem_copy(j)
                            w_hi(j + 2)
                            if j - 1 in TOK_AT:
                                mem_values(j - 1)

            def take_tokens(k):
                act.wait_ge(tok_tr, 9 + k)
                if k < 2:
                    act.activation(v_sw[:, :, k, :], pair(2 + k).rearrange("p (t c) -> p t c", t=NT), ACT.Copy).then_inc(tok_ev, 1)
                else:
                    act.activation(gates[:, :, :], pair(2)[:, 0:24 * NT].rearrange("p (t c) -> p t c", t=NT),
                                   ACT.Sigmoid).then_inc(tok_ev, 1)

            mem_values(N_IN - 1)
            act.wait_ge(const_in, 16 * 8)
            for j in range(N_IN, N_OUT):
                act.wait_ge(gemm, j + 1)
                pp = pair(j % 2)
                m = PIECES[j][1]
                if m in TOK:
                    w = 24 if m == 16 else P
                    act.activation(tokT[TOK.index(m)][0:w, :], pp[0:w, :], ACT.Copy).then_inc(ev_act, 1)
                elif m in (0, 1):
                    act.activation(pu[:, m, :], pp, ACT.Copy).then_inc(ev_act, 1)
                elif m in (2, 3):
                    act.activation(ch[:, m - 2, :], pp, ACT.Copy).then_inc(ev_act, 1)
                elif m in (4, 5):
                    if m == 5:
                        act.wait_ge(sig_step, 1)
                    act.activation(sig[:, :], pp, ACT.Sigmoid).then_inc(ev_act, 1)
                elif m in (10, 11):
                    st = c_st[m - 10]
                    act.activation(st[0:HD, 0, :], pp[0:HD, :], ACT.Copy)
                    act.activation(st[0:HD, 1, :], pp[HD:P, :], ACT.Copy).then_inc(ev_act, 1)
                elif m in (12, 14):
                    kd = (m - 12) // 2
                    if m == 12:
                        act.wait_ge(store0, 32)
                    act.activation(k_h[0:HD, kd, 0, :], pp[0:HD, :], ACT.Copy)
                    act.activation(k_h[HD:P, kd, 0, :], pp[0:HD, :], ACT.Copy)
                    act.activation(k_h[0:HD, kd, 1, :], pp[HD:P, :], ACT.Copy)
                    act.activation(k_h[HD:P, kd, 1, :], pp[HD:P, :], ACT.Copy).then_inc(ev_act, 1)
                else:
                    if m == 6:
                        act.wait_ge(sig_step, 2)
                        act.wait_ge(pool_step, POOL_STEPS)
                    h = 2 * (m - 6)
                    act.activation(q_st[0:HD, h, :], pp[0:HD, :], ACT.Copy, scale=-HD ** -0.5)
                    act.activation(q_st[HD:P, h + 1, :], pp[HD:P, :], ACT.Copy, scale=-HD ** -0.5).then_inc(ev_act, 1)
                if j + 2 < N_OUT:
                    w_hi(j + 2)
                if j - 1 in TOK_AT and j > N_IN:
                    take_tokens(TOK_AT.index(j - 1) - 8)
            act.drain().then_inc(end["act"], 1)
            act.wait_ge(end["pe"], 1)

            def pooled_hi(c):
                act.wait_ge(fb["pool"], c + 1)
                act.activation(hT_h[:, c, :], pair(1 + 2 * c), ACT.Copy, scale=smc("pool_scale", c)).then_inc(fb["pool_h"], 1)

            def by_group(x):
                return x.rearrange("p (g c) -> p g c", g=NKV)

            pooled_hi(0)
            act.wait_ge(end["dve"], 1)
            act.wait_ge(fb["tab"], 1)
            act.wait_ge(fb["cm"], 2)
            act.activation(tn[:, :, :].rearrange("p h x -> p x h"), ps[:, 4:8, :].rearrange("p a (b h) -> p (a b) h", h=NH),
                           ACT.Copy).then_inc(fb["tab_ev"], 1)
            for c in range(2):
                act.wait_ge(fb["dev"], c + 1)
                act.activation(ch[:, c, :], ca[:, c, :], ACT.Square).then_inc(fb["sq"], 1)
            act.wait_ge(fb["tab"], 2)
            act.activation(tc[:, :, :].rearrange("p h x -> p x h"),
                           pair(1)[:, 0:NH * ZC].rearrange("p (z h) -> p z h", h=NH), ACT.Copy).then_inc(fb["tab_ev"], 1)
            act.wait_ge(fb["var"], 1)
            act.activation(cln[:, :], pair(0), ACT.Sqrt, bias=smc("eps")).then_inc(fb["sd"], 1)
            for c in range(2):
                act.wait_ge(fb["z"], c + 1)
                act.activation(ca[:, c, :], ca[:, c, :], ACT.Silu, bias=smc("ln_b", c), scale=smc("ln_g", c)).then_inc(fb["silu"], 1)
            for kv in range(2):
                act.wait_ge(fb["hid"], kv + 1)
                if kv == 1:
                    act.wait_ge(fb["kc"], 1)
                act.activation(hid_c[:, :, :], ps[:, 4 + kv, 0:252].rearrange("p (t c) -> p t c", t=2),
                               ACT.Gelu_apprx_tanh).then_inc(fb["gelu"], 1)
            act.wait_ge(fb["chain"], 2)
            act.activation(by_group(kc_h[:, 0:2 * CPAD])[:, :, 0:NCMP], by_group(ps[:, 4, 256:382]), ACT.Copy).then_inc(fb["kc_h"], 1)
            act.wait_ge(fb["hid"], 1)
            act.wait_ge(fb["z"], 2)
            act.activation(v_st[:, :, 0:HD], v_sw[:, :, :, :].rearrange("p t k (g d) -> p (t k g) d", g=NKV), ACT.Copy)\
                .then_inc(at_["v_h"], 1)
            pooled_hi(1)
            act.wait_ge(fb["vc"], 1)
            act.activation(vc[0:NCMP, :, 0:HD], by_group(ps[0:NCMP, 5, 256:256 + P]), ACT.Copy).then_inc(fb["vc_ev"], 1)
            for m in range(2):
                act.wait_ge(fb["pw"], m + 1)
                act.activation(hT_h[:, 2 + m, :], pair(1 - m), ACT.Copy).then_inc(fb["pw_h"], 1)
            act.drain().then_inc(end["act"], 1)
            for n in ("pe", "dve"):
                act.wait_ge(end[n], 2)

            def exp_row(s, r):
                i, g, kind = SUB[s]
                n = s * QPK + r
                act.wait_ge(at_["max"], n + 1)
                if s >= 2 and r == 0:
                    act.wait_ge(at_["tr"], TILE0[s - 1])
                w, b0 = width(i, kind), row_at(i, kind)
                nb = nmx[:, n % 2, :]
                sc = pair(n % 2)
                if kind == 0:
                    act.activation(p_sel[:, r, 0:w], sc[:, b0:b0 + w], ACT.Exp, bias=nb[:, 0:1], scale=-1.0,
                                   accum_out=sums[:, kind, r, 1:2]).then_inc(at_["exp"], 1)
                else:
                    act.activation(p_win[:, r, 0:w], sc[:, b0:b0 + w], ACT.Exp, bias=nb[:, 0:1], scale=-1.0,
                                   accum_out=sums[:, kind, r, 2:3])
                    act.activation(p_win[:, r, 5 * P:5 * P + CPAD], sc[:, 0:CPAD], ACT.Exp,
                                   bias=nb[:, 1:2], scale=-1.0, accum_out=sums[:, kind, r, 0:1]).then_inc(at_["exp"], 1)

            def copy_tile(s, t):
                n = TILE0[s] + t
                rows = NCMP if (SUB[s][2] == 1 and t == tiles_of(s) - 1) else P
                act.wait_ge(at_["tr"], n + 1)
                if n >= 3:
                    act.wait_ge(at_["pv"], n - 2)
                act.activation(pt_h[n % 3][0:rows, :], ps[0:rows, 4 + n % 2, :], ACT.Copy).then_inc(at_["pt_h"], 1)

            def take_output(unit):
                act.wait_ge(at_["pv"], TILE0[2 * unit + 2])
                if unit >= 1:
                    act.wait_ge(at_["o_sum"], unit)
                act.activation(o_b[:, :], ps[HD:P, 6 + unit % 2, :], ACT.Copy).then_inc(at_["o_b"], 1)

            def output_hi(unit):
                i, g = unit // NKV, unit % NKV
                act.wait_ge(at_["o_sum"], unit + 1)
                act.activation(hT_h[:, 4 + 2 * g:6 + 2 * g, i * P:(i + 1) * P], o_sum[:, :, :], ACT.Copy).then_inc(at_["o_h"], 1)

            act.wait_ge(at_["v_l"], 1)
            for what, s, k in exp_order():
                if what == "row":
                    exp_row(s, k)
                else:
                    copy_tile(s, k)
                if (what, s, k) in TAKE:
                    take_output(TAKE[what, s, k])
                if (what, s, k) in FINISH:
                    output_hi(FINISH[what, s, k])
            take_output(len(SUB) // 2 - 1)
            act.wait_ge(end["pe"], 3)
            w_hi(N_OUT)
            output_hi(len(SUB) // 2 - 1)
            act.drain().then_inc(end["act"], 1)
            for n in ("pe", "dve"):
                act.wait_ge(end[n], 3)

            def block_out(s, split_next):
                b = bo[s]
                act.wait_ge(b["gain"], 32)
                for t in range(NT + 2):
                    if t < NT:
                        act.wait_ge(b["mm"], t + 1)
                        if t >= 2:
                            act.wait_ge(b["up"], t - 1)
                        if t >= 1:
                            act.wait_ge(b["ss2"], t)
                        sum_squares(pair(t % 2), ssb[:, 0, t % 2:t % 2 + 1], junk[:, :], b["ss"])
                    if t >= 2:
                        act.wait_ge(b["tr"], t - 1)
                        ts = slice((t - 2) * P, (t - 1) * P)
                        act.activation(hT_h[:, :, ts], pair(2 + t % 2).rearrange("p (k c) -> p k c", k=KC),
                                       ACT.Copy).then_inc(b["hh"], 1)
                    if t < NT:
                        act.wait_ge(b["x"], t + 1)
                        act.wait_ge(b["ss"], t + 1)
                        sum_squares(upd[t % 2][:, :], ssb[:, 1, t % 2:t % 2 + 1], junk[:, :], b["ss2"])
                        if t == NT - 2:
                            split_next()

            for k in range(1, KC):
                w_hi(N_OUT + k)
            block_out(0, lambda: (w_hi(N_Q), w_hi(N_Q + 1)))
            act.drain().then_inc(end["act"], 1)
            for n in ("pe", "dve"):
                act.wait_ge(end[n], 4)
            for m in range(8):
                act.wait_ge(gemm, J_Q + m + 1)
                if m == 0:
                    for t in range(2):
                        act.wait_ge(bo[0][f"st{t}"], 16 * (NT // 2))
                act.activation(xq[:, m, :], pair(m % 2), ACT.Copy, scale=(D // XH) ** -0.5).then_inc(xa["q_ev"], 1)
                if m + 2 < 8:
                    w_hi(N_Q + m + 2)
            act.drain().then_inc(end["act"], 1)
            for n in ("pe", "dve"):
                act.wait_ge(end[n], 5)

            for t in range(NT + 2):
                if t < NT:
                    act.wait_ge(xa["max"], t + 1)
                    if t >= 2:
                        act.wait_ge(xa["tr"], t - 1)
                    for h in range(XH):
                        act.activation(xp[t % 2][:, h, :], pair(t % 2)[:, h * MEM:(h + 1) * MEM], ACT.Exp,
                                       bias=xs[:, 0, h:h + 1], accum_out=xs[:, 1, h:h + 1]).then_inc(xa["exp"], 1)
                if 1 <= t <= NT:
                    act.wait_ge(xa["tr"], t)
                    if t >= 3:
                        act.wait_ge(xa["pv"], t - 2)
                    act.activation(xpt[(t - 1) % 2][:, :, :, :].rearrange("p m h c -> p (m h c)"), pair(2), ACT.Copy).then_inc(xa["pt"], 1)
                if t >= 2:
                    act.wait_ge(xa["pv"], t - 1)
                    ts = slice((t - 2) * P, (t - 1) * P)
                    act.activation(hT_h[:, :, ts], pair(3).rearrange("p (k c) -> p k c", k=KC), ACT.Copy).then_inc(xa["oh"], 1)
                if t < NT:
                    w_hi(N_O + t)
            act.drain().then_inc(end["act"], 1)
            for n in ("pe", "dve"):
                act.wait_ge(end[n], 6)

            def w_hi_mlp(g, c):
                n = N_MLP + c
                k, c = divmod(c, 2 * GROUP)
                act.wait_ge(raw_in[n % 2], g * (16 * 4) + raw(n)[2])
                if c < GROUP:
                    j = J_MLP + c
                    act.wait_ge(ml["up"], g * GROUP + (k * GROUP + c + 1))
                    dst = tw_h[j % 2][:, :, :].rearrange("p k n -> p (k n)")
                else:
                    act.wait_ge(ml["dn"], g * (2 * NT) + 1)
                    dst = w2_h[:, c - GROUP, :]
                act.activation(dst, wraw[n % 2][:, :], ACT.Copy).then_inc(wh_done, 1)

            act.sem_inc(ml["relu"], 2)
            act.sem_inc(ml["up"], 2)
            act.sem_inc(ml["dn"], 1)
            block_out(1, lambda: (w_hi_mlp(0, 0), w_hi_mlp(0, 1)))
            act.drain().then_inc(end["act"], 1)
            for n in ("pe", "dve"):
                act.wait_ge(end[n], 7)
            for t in range(2):
                act.wait_ge(bo[1][f"st{t}"], 16 * (NT // 2))

            def hidden(g, c):
                act.wait_ge(ml["up"], g * GROUP + (c + 3))
                act.wait_ge(ml["hl"], g * GROUP + (c + 1))
                act.activation(rl[c % 2][:, :], pair(c % 2), ACT.Relu).then_inc(ml["relu"], 1)
                act.wait_ge(ml["relu"], g * GROUP + (c + 3))
                act.activation(rl[c % 2][:, :], rl[c % 2][:, :], ACT.Square).then_inc(ml["sq"], 1)
                act.wait_ge(ml["sq"], g * GROUP + (c + 1))
                act.wait_ge(ml["dn"], g * (2 * NT) + 1)
                act.activation(hid_h[:, c, :], rl[c % 2][:, :], ACT.Copy).then_inc(ml["hh"], 1)

            def mlp_group(g, last=False):
                hidden(g, 0)
                w_hi_mlp(g, 2)
                hidden(g, 1)
                w_hi_mlp(g, 3)
                w_hi_mlp(g, 4)
                hidden(g, 2)
                w_hi_mlp(g, 5)
                w_hi_mlp(g, 6)
                hidden(g, 3)
                w_hi_mlp(g, 7)
                if not last:
                    w_hi_mlp(g, 8)
                    w_hi_mlp(g, 9)

            with act.Fori(0, NGROUP - 1) as g:
                mlp_group(g)
            mlp_group(NGROUP - 1, last=True)
            for t in range(NT):
                act.wait_ge(ml["acc"], 2 * NT * (NGROUP - 1) + 4 + 2 * (t + 1))
                if t >= 2:
                    act.wait_ge(ml["y"], t - 1)
                if t >= 1:
                    act.wait_ge(ml["ss"], t)
                sum_squares(acc[:, t, :], ssb[:, 0, t % 2:t % 2 + 1], junk_f[:, :], ml["ss"])

        @block.vector
        def _(dve):
            V = nc.vector

            def w_lo(n):
                dve.wait_ge(wh_done, n + 1)
                dst, hi = w_dest(n)[1], w_dest(n)[0]
                V.tensor_tensor(dst, raw(n)[0], hi.bitcast(F32), ALU.subtract).then_inc(wl_done, 1)

            dve.wait_ge(first_in, 32)
            for u in range(MT + NT + 1):
                if u < MT + NT:
                    dve.wait_ge(rs_n, u + 1)
                    if u == MT:
                        dve.wait_ge(gain_in, 16)
                    if u >= 2:
                        dve.wait_ge(tr_n, u - 1)
                    V.scalar_tensor_tensor(hn0[u % 2][:, :], x_in[u % 2][:, :], rstd[:, u:u + 1],
                                           (gain_m if u < MT else gain_x)[:, :], ALU.mult, ALU.mult).then_inc(hn_n, 1)
                    if u == 1:
                        w_lo(0)
                        w_lo(1)
                if u >= 1:
                    v = u - 1
                    dve.wait_ge(hh_n, v + 1)
                    hi, lo = (mT_h, mT_l) if v < MT else (hT_h, hT_l)
                    v0 = v if v < MT else v - MT
                    cs = slice(v0 * P, (v0 + 1) * P)
                    V.tensor_tensor(lo[:, :, cs], pair(2 + v % 2).rearrange("p (k c) -> p k c", k=KC),
                                    hi[:, :, cs].bitcast(F32), ALU.subtract).then_inc(hl_n, 1)
                    if v >= MT:
                        for j in (2 * (v - MT), 2 * (v - MT) + 1):
                            w_lo(j + 2)

            pstep = [0]

            def pooled(ins):
                pstep[0] += 1
                ins.then_inc(pool_step, 1)
                dve.wait_ge(pool_step, pstep[0])

            def window_sum(dst, src, d, rows):
                pooled(V.tensor_tensor(dst[rows, d:], src[rows, d:], src[rows, 0:SEQ - d], ALU.add))
                pooled(V.tensor_copy(dst[rows, 0:d], src[rows, 0:d]))

            def mean_minus(c, src, rows):
                u = pu[:, c, :]
                pooled(V.tensor_tensor(t16[rows, :], src[rows, 0:16], sm[rows, SM["inv16"][0] + 16 * c:SM["inv16"][0] + 16 * c + 16], ALU.mult))
                pooled(V.tensor_tensor(u[rows, 0:16], t16[rows, :], u[rows, 0:16], ALU.subtract))
                pooled(V.scalar_tensor_tensor(u[rows, 16:], src[rows, 16:], smc("inv_win", c, rows), u[rows, 16:], ALU.mult, ALU.subtract))

            lo_rows, hi_rows, all_rows = slice(0, HD), slice(HD, P), slice(0, P)

            def pool_tile(c):
                a_, b_ = pool_a, pool_b
                window_sum(a_, pu[:, c, :], 1, all_rows)
                if c == 0:
                    window_sum(b_, a_, 2, hi_rows)
                    mean_minus(0, a_, lo_rows)
                    mean_minus(0, b_, hi_rows)
                else:
                    window_sum(b_, a_, 2, all_rows)
                    window_sum(a_, b_, 4, all_rows)
                    window_sum(b_, a_, 8, hi_rows)
                    mean_minus(1, a_, lo_rows)
                    mean_minus(1, b_, hi_rows)

            cstep = [0]

            def conv_taps(n0, n1):
                for n in range(n0, min(n1, 2 * TAPS)):
                    c, d = n // TAPS, n % TAPS
                    w = smc("conv_w", c * TAPS + TAPS - 1 - d)
                    if d == 0:
                        ins = V.tensor_scalar(ca[:, c, :], ch[:, c, :], w, smc("conv_b", c), ALU.mult, ALU.add)
                    else:
                        ins = V.scalar_tensor_tensor(ca[:, c, d:], ch[:, c, 0:SEQ - d], w, ca[:, c, d:], ALU.mult, ALU.add)
                    ins.then_inc(conv_step, 1)
                    dve.wait_ge(conv_step, n + 1)

            def glu(c):
                V.tensor_tensor(ch[:, c, :], ch[:, c, :], sig[:, :], ALU.mult).then_inc(sig_step, 1)
                dve.wait_ge(sig_step, c + 1)

            dve.wait_ge(const_in, 16 * 8)
            fbc = [0]

            def chained(ins, s=fb["rb"]):
                fbc[0] += 1
                ins.then_inc(s, 1)
                dve.wait_ge(s, fbc[0])

            R = slice(0, 3 * NBUCKET)
            chained(V.memset(relb[96:97, :], -NEG))
            chained(V.tensor_scalar(rb[R, :], rb[R, :], -1.0, None, ALU.mult))
            chained(V.tensor_copy(rhm[R, 0, :], rb[R, :]))
            chained(V.tensor_tensor(rb1[R, :], rb[R, :], rhm[R, 0, :], ALU.subtract))
            chained(V.tensor_copy(rhm[R, 1, :], rb1[R, :]))
            chained(V.tensor_tensor(rb2[R, :], rb1[R, :], rhm[R, 1, :], ALU.subtract))
            chained(V.tensor_copy(relb[0:32, :], rhm[0:32, 0, :]))
            chained(V.tensor_copy(relb[32:64, :], rhm[32:64, 1, :]))
            V.tensor_copy(relb[64:96, :], rb2[64:96, :]).then_inc(fb["relb"], 1)
            for j in range(N_IN, N_OUT):
                m = PIECES[j][1]
                pp = pair(j % 2)
                if m in (0, 1, 4, 5) or READS[j]:
                    dve.wait_ge(ev_act, j + 1)
                if m in (4, 5):
                    glu(m - 4)
                elif m in (10, 11):
                    st = c_st[m - 10]
                    V.tensor_copy(st[HD:P, 0, 0:SEQ - 1], pp[0:HD, 1:SEQ])
                    V.tensor_copy(st[HD:P, 1, 0:SEQ - 1], pp[HD:P, 1:SEQ]).then_inc(ev_dve, 1)
                elif m in (12, 14):
                    kd = (m - 12) // 2
                    for g in range(NKV):
                        rows = slice(HD * g, HD * g + HD)
                        for e in range(2):
                            last = V.tensor_tensor(k_l[HD * e:HD * e + HD, kd, g, :], pp[rows, :],
                                                   k_h[rows, kd, g, :].bitcast(F32), ALU.subtract)
                    last.then_inc(ev_dve, 1)
                elif m in (6, 7, 8, 9):
                    h = 2 * (m - 6)
                    V.scalar_tensor_tensor(q_st[HD:P, h, :], pp[0:HD, :], -HD ** -0.5, q_st[0:HD, h, :].bitcast(F32),
                                           ALU.mult, ALU.subtract)
                    V.scalar_tensor_tensor(q_st[0:HD, h + 1, :], pp[HD:P, :], -HD ** -0.5, q_st[HD:P, h + 1, :].bitcast(F32),
                                           ALU.mult, ALU.subtract).then_inc(ev_dve, 1)
                if j + 2 < N_OUT:
                    w_lo(j + 2)
                if m in (0, 1):
                    pool_tile(m)
                elif j >= N_IN + 2:
                    n = j - N_IN - 2
                    conv_taps(CONV_PLAN[n], CONV_PLAN[n + 1])
            dve.wait_ge(tok_ev, 11)
            V.tensor_scalar(gates[:, 0, 0:24:3], gates[:, 0, 0:24:3], smc("valid"), None, ALU.mult)
            dve.drain().then_inc(end["dve"], 1)
            for n in ("pe", "act"):
                dve.wait_ge(end[n], 1)

            def pooled_lo(c):
                dve.wait_ge(fb["pool_h"], c + 1)
                V.scalar_tensor_tensor(hT_l[:, c, :], pair(1 + 2 * c), smc("pool_scale", c), hT_h[:, c, :].bitcast(F32),
                                       ALU.mult, ALU.subtract).then_inc(fb["pool_l"], 1)

            def by_group(x):
                return x.rearrange("p (g c) -> p g c", g=NKV)

            pooled_lo(0)
            for kv in range(2):
                for j in range(16):
                    last = V.tensor_scalar(cm[kv][:, j, :, :], c_st[kv][:, :, 2 * j:2 * j + CMP_STRIDE * (NCMP - 1) + 1:CMP_STRIDE],
                                           smc(("pos_k", "pos_v")[kv], j), None, ALU.add)
                last.then_inc(fb["cm"], 1)
            dve.wait_ge(fb["mean"], 1)
            for c in range(2):
                V.tensor_tensor(ca[:, c, :], ca[:, c, :], pair(0), ALU.subtract).then_inc(fb["dev"], 1)
            dve.wait_ge(fb["sd"], 1)
            V.reciprocal(ctmp[:, :], cln[:, :]).then_inc(fb["rec"], 1)
            dve.wait_ge(fb["rec"], 1)
            for c in range(2):
                V.tensor_tensor(ca[:, c, :], ca[:, c, :], ctmp[:, :], ALU.mult).then_inc(fb["z"], 1)
            dve.wait_ge(fb["hid"], 2)
            V.memset(kc_h[:, :].bitcast(F32), 0.0).then_inc(fb["chain"], 1)
            V.memset(kc_l[:, :].bitcast(F32), 0.0).then_inc(fb["chain"], 1)
            dve.wait_ge(fb["chain"], 2)
            dve.wait_ge(fb["kc_h"], 1)
            V.tensor_tensor(by_group(kc_l[:, 0:2 * CPAD])[:, :, 0:NCMP], by_group(ps[:, 4, 256:382]),
                            by_group(kc_h[:, 0:2 * CPAD])[:, :, 0:NCMP].bitcast(F32), ALU.subtract)
            dve.wait_ge(at_["v_h"], 1)
            V.tensor_tensor(v_st[:, :, HD:P], v_sw[:, :, :, :].rearrange("p t k (g d) -> p (t k g) d", g=NKV),
                            v_st[:, :, 0:HD].bitcast(F32), ALU.subtract).then_inc(at_["v_l"], 1)
            pooled_lo(1)
            dve.wait_ge(fb["vc_ev"], 1)
            V.tensor_tensor(vc[0:NCMP, :, HD:P], by_group(ps[0:NCMP, 5, 256:256 + P]), vc[0:NCMP, :, 0:HD].bitcast(F32),
                            ALU.subtract)
            for m in range(2):
                dve.wait_ge(fb["pw_h"], m + 1)
                V.tensor_tensor(hT_l[:, 2 + m, :], pair(1 - m), hT_h[:, 2 + m, :].bitcast(F32), ALU.subtract)
            dve.drain().then_inc(end["dve"], 1)
            for n in ("pe", "act"):
                dve.wait_ge(end[n], 2)

            step = [0]

            def link(ins):
                step[0] += 1
                ins.then_inc(at_["chain"], 1)
                dve.wait_ge(at_["chain"], step[0])

            def row_max(s, r):
                i, g, kind = SUB[s]
                n = s * QPK + r
                h = QPK * g + r
                w, b0 = width(i, kind), row_at(i, kind)
                sc = pair(n % 2)[:, b0:b0 + w]
                near = min(w, NEAR)
                far = w - near
                dve.wait_ge(at_["qk"], n + 1)
                if n >= 2:
                    dve.wait_ge(at_["exp"], n - 1)
                part, top = mx[:, n % 2:n % 2 + 1], nmx[:, n % 2, :]
                init = 3.0e38
                if kind == 1 and w == 5 * P:
                    link(V.tensor_tensor_reduce(sc[:, 0:far], sc[:, 0:far], wm[:, :], 1.0, init, ALU.add, ALU.min, part))
                    init = part
                elif far:
                    link(V.tensor_reduce(part, sc[:, 0:far], AX.X, ALU.min))
                    init = part
                last = V.tensor_tensor_reduce(sc[:, far:w], sc[:, far:w], tn[:, h, NEAR - near:NEAR], 1.0, init, ALU.add,
                                              ALU.min, top[:, 0:1])
                if kind == 1:
                    cc = pair(n % 2)[:, 0:CPAD]
                    z0 = 56 - 8 * i
                    last = V.tensor_tensor_reduce(cc, cc, tc[:, h, z0:z0 + CPAD], 1.0, 3.0e38, ALU.add, ALU.min, top[:, 1:2])
                last.then_inc(at_["max"], 1)

            def copy_lo(s, t):
                n = TILE0[s] + t
                rows = NCMP if (SUB[s][2] == 1 and t == tiles_of(s) - 1) else P
                dve.wait_ge(at_["pt_h"], n + 1)
                V.tensor_tensor(pt_l[n % 3][0:rows, :], ps[0:rows, 4 + n % 2, :], pt_h[n % 3][0:rows, :].bitcast(F32),
                                ALU.subtract).then_inc(at_["pt_l"], 1)

            def output_sum(unit):
                dve.wait_ge(at_["o_b"], unit + 1)
                if unit >= 1:
                    dve.wait_ge(at_["o_l"], unit)
                for e in range(2):
                    parts = (x.rearrange("p (c e q) -> p c e q", e=2, q=P)[:, :, e, :] for x in (o_b[:, :], ps[0:HD, 6 + unit % 2, :]))
                    last = V.tensor_tensor(o_sum[HD * e:HD * e + HD, :, :], *parts, ALU.add)
                last.then_inc(at_["o_sum"], 1)

            def output_lo(unit):
                i, g = unit // NKV, unit % NKV
                dve.wait_ge(at_["o_h"], unit + 1)
                dst = (slice(0, P), slice(4 + 2 * g, 6 + 2 * g), slice(i * P, (i + 1) * P))
                V.tensor_tensor(hT_l[dst], o_sum[:, :, :], hT_h[dst].bitcast(F32), ALU.subtract).then_inc(at_["o_l"], 1)

            dve.wait_ge(wm_in, 16)
            for what, s, k in ORDER:
                if what == "row":
                    row_max(s, k)
                else:
                    copy_lo(s, k)
                if (what, s, k) in TAKE:
                    output_sum(TAKE[what, s, k])
                if (what, s, k) in FINISH:
                    output_lo(FINISH[what, s, k])
            output_sum(len(SUB) // 2 - 1)
            dve.wait_ge(end["pe"], 3)
            w_lo(N_OUT)
            output_lo(len(SUB) // 2 - 1)
            dve.drain().then_inc(end["dve"], 1)
            for n in ("pe", "act"):
                dve.wait_ge(end[n], 3)

            def block_out(s, split_next):
                b = bo[s]
                dve.wait_ge(b["gain"], 32)
                for t in range(NT + 2):
                    if t < NT:
                        u = upd[t % 2][:, :]
                        dve.wait_ge(b["rs"], t + 1)
                        if t >= 2:
                            dve.wait_ge(b[f"st{t % 2}"], 16 * (t // 2))
                        V.scalar_tensor_tensor(u, pair(t % 2), rsb[:, 0, t % 2:t % 2 + 1], gain_post[:, :],
                                               ALU.mult, ALU.mult).then_inc(b["up"], 1)
                        dve.wait_ge(b["up"], t + 1)
                        dve.wait_ge(b[f"res{t % 2}"], 16 * (t // 2 + 1))
                        V.tensor_tensor(u, u, res[t % 2][:, :], ALU.add).then_inc(b["x"], 1)
                    if t >= 2:
                        dve.wait_ge(b["hh"], t - 1)
                        ts = slice((t - 2) * P, (t - 1) * P)
                        V.tensor_tensor(hT_l[:, :, ts], pair(2 + t % 2).rearrange("p (k c) -> p k c", k=KC),
                                        hT_h[:, :, ts].bitcast(F32), ALU.subtract).then_inc(b["hl"], 1)
                    if t < NT:
                        dve.wait_ge(b["rs2"], t + 1)
                        if t >= 2:
                            dve.wait_ge(b["tr"], t - 1)
                        V.scalar_tensor_tensor(hn[t % 2][:, :], upd[t % 2][:, :], rsb[:, 1, t % 2:t % 2 + 1], gain_pre[:, :],
                                               ALU.mult, ALU.mult).then_inc(b["hn"], 1)
                        if t == NT - 2:
                            split_next()

            for k in range(1, KC):
                w_lo(N_OUT + k)
            block_out(0, lambda: (w_lo(N_Q), w_lo(N_Q + 1)))
            dve.drain().then_inc(end["dve"], 1)
            for n in ("pe", "act"):
                dve.wait_ge(end[n], 4)
            for m in range(2, 8):
                w_lo(N_Q + m)
            dve.drain().then_inc(end["dve"], 1)
            for n in ("pe", "act"):
                dve.wait_ge(end[n], 5)

            xstep = [0]

            def x_link(ins):
                xstep[0] += 1
                ins.then_inc(xa["chain"], 1)
                dve.wait_ge(xa["chain"], xstep[0])

            for t in range(NT + 2):
                if t < NT:
                    dve.wait_ge(xa["s"], t + 1)
                    V.tensor_reduce(xs[:, 0, :], pair(t % 2).rearrange("p (h m) -> p h m", h=XH), AX.X, ALU.max,
                                    negate=True).then_inc(xa["max"], 1)
                    dve.wait_ge(xa["exp"], XH * (t + 1))
                    x_link(V.reciprocal(xs[:, 2, :], xs[:, 1, :]))
                    for h in range(XH):
                        last = V.tensor_scalar(xp[t % 2][:, h, :], xp[t % 2][:, h, :], xs[:, 2, h:h + 1], None, ALU.mult)
                    last.then_inc(xa["pn"], 1)
                if t >= 2:
                    dve.wait_ge(xa["oh"], t - 1)
                    ts = slice((t - 2) * P, (t - 1) * P)
                    V.tensor_tensor(hT_l[:, :, ts], pair(3).rearrange("p (k c) -> p k c", k=KC), hT_h[:, :, ts].bitcast(F32),
                                    ALU.subtract).then_inc(xa["ol"], 1)
                if t < NT:
                    w_lo(N_O + t)
            dve.drain().then_inc(end["dve"], 1)
            for n in ("pe", "act"):
                dve.wait_ge(end[n], 6)

            def w_lo_mlp(g, c):
                n = N_MLP + c
                dve.wait_ge(wh_done, g * 8 + (n + 1))
                c %= 2 * GROUP
                if c < GROUP:
                    j = J_MLP + c
                    hi, lo = (w[j % 2][:, :, :].rearrange("p k n -> p (k n)") for w in (tw_h, tw_l))
                else:
                    hi, lo = w2_h[:, c - GROUP, :], w2_l[:, c - GROUP, :]
                V.tensor_tensor(lo, wraw[n % 2][:, :], hi.bitcast(F32), ALU.subtract).then_inc(wl_done, 1)

            dve.sem_inc(ml["acc"], 4)
            dve.sem_inc(ml["hl"], 2)
            block_out(1, lambda: (w_lo_mlp(0, 0), w_lo_mlp(0, 1)))
            dve.drain().then_inc(end["dve"], 1)
            for n in ("pe", "act"):
                dve.wait_ge(end[n], 7)

            def hidden_lo(g, c):
                dve.wait_ge(ml["hh"], g * GROUP + (c + 1))
                V.tensor_tensor(hid_l[:, c, :], rl[c % 2][:, :], hid_h[:, c, :].bitcast(F32), ALU.subtract).then_inc(ml["hl"], 1)

            def split_group(g):
                hidden_lo(g, 0)
                w_lo_mlp(g, 2)
                hidden_lo(g, 1)
                w_lo_mlp(g, 3)
                w_lo_mlp(g, 4)
                hidden_lo(g, 2)
                w_lo_mlp(g, 5)
                w_lo_mlp(g, 6)
                hidden_lo(g, 3)
                w_lo_mlp(g, 7)

            def add(g, idx, first=False):
                t, hf = idx // 2, idx % 2
                o = acc[:, t, hf * HALF:(hf + 1) * HALF]
                dve.wait_ge(ml["dn"], g * (2 * NT) + (idx + 2))
                if first:
                    V.tensor_copy(o, ps[:, 4 + idx % 4, :]).then_inc(ml["acc"], 1)
                else:
                    V.tensor_tensor(o, o, ps[:, 4 + idx % 4, :], ALU.add).then_inc(ml["acc"], 1)

            def mlp_group(g, first=False):
                split_group(g)
                for idx in range(2 * NT):
                    add(g, idx, first)
                    if idx in (3, 5):
                        w_lo_mlp(g, 8 + (idx - 3) // 2)

            def output_tile(t):
                u = upd_f[t % 2][:, :]
                dve.wait_ge(ml["rs"], t + 1)
                if t >= 2:
                    dve.wait_ge(ml[f"st{t % 2}"], 16 * (t // 2))
                V.scalar_tensor_tensor(u, acc[:, t, :], rsb[:, 0, t % 2:t % 2 + 1], gain_f[:, :], ALU.mult,
                                       ALU.mult).then_inc(ml["y"], 1)
                dve.wait_ge(ml["y"], t + 1)
                dve.wait_ge(ml[f"res{t % 2}"], 16 * (t // 2 + 1))
                V.tensor_tensor(u, u, res_f[t % 2][:, :], ALU.add).then_inc(ml["fin"], 1)

            mlp_group(0, first=True)
            with dve.Fori(1, NGROUP - 1) as g:
                mlp_group(g)
            split_group(NGROUP - 1)
            dve.wait_ge(ml["gain"], 16)
            dve.wait_ge(ml["hl"], GROUP * NGROUP + 2)
            for t in range(NT):
                add(NGROUP - 1, 2 * t)
                add(NGROUP - 1, 2 * t + 1)
                if t >= 1:
                    output_tile(t - 1)
            output_tile(NT - 1)


def kernel(**inputs):
    import concourse.bacc as _bacc
    from concourse.bass_utils import run_bass_kernel_spmd as _run

    c = np.ascontiguousarray
    v = {n: np.asarray(x) for n, x in inputs.items()}

    def chunks(w):
        return c(w.reshape(KC, P, -1, P).transpose(2, 1, 0, 3))

    def cols(w):
        return w.reshape(2, P).T

    w_in = v["w_in"][0]
    small = np.zeros((P, SMW), np.float32)

    def put(name, x):
        small[:, SM[name][0]:SM[name][1]] = x

    put("conv_w", v["conv_w"][0].T.reshape(2, P, TAPS).transpose(1, 0, 2).reshape(P, 2 * TAPS))
    put("conv_b", cols(v["conv_b"][0]))
    put("ln_g", cols(v["conv_ln_g"][0]))
    put("ln_b", cols(v["conv_ln_b"][0]))
    put("pool_scale", cols(v["pool_scale"][0]))
    put("pos_k", v["cmp_k_pos"][0].reshape(16, P).T)
    put("pos_v", v["cmp_v_pos"][0].reshape(16, P).T)
    win = np.repeat(np.array([[2, 8], [4, 16]], np.float32), HD, axis=0)
    put("inv_win", 1 / win)
    put("inv16", (1 / np.minimum(np.arange(1, 17, dtype=np.float32), win[:, :, None])).reshape(P, 32))
    put("valid", (np.arange(P)[:, None] >= CMP_LEN - 1).astype(np.float32))
    put("eps", EPS)
    pool_w = np.zeros((P, 2, P), np.float32)
    for g in range(4):
        r = slice(HD * (g % 2), HD * (g % 2) + HD)
        pool_w[r, g // 2, r] = v["pool_w"][0, g]
    d = np.arange(ND) + DMIN
    n = np.maximum(d, 1).astype(np.float32)
    large = MAX_EXACT + (np.log(n / MAX_EXACT) / math.log(MAX_DIST / MAX_EXACT) * (NBUCKET - MAX_EXACT)).astype(np.int32)
    bucket = np.where(d < MAX_EXACT, np.maximum(d, 0), np.minimum(large, NBUCKET - 1))
    hot = (np.arange(NBUCKET)[:, None] == bucket).astype(np.float32)
    hot[NBUCKET - 1] -= 1.0
    hot *= d >= 0
    onehot = np.concatenate([hot, hot, hot, (d < 0)[None].astype(np.float32)])
    q, x = np.arange(P)[:, None], np.arange(3 * P)[None, :]
    arrays = {
        "x": c(v["x"][0]), "mem": c(v["mem"][0]), "rel_bias": v["rel_bias"],
        "in": chunks(np.concatenate([w_in, np.zeros((D, P - 24), np.float32)], axis=1)),
        "wout": v["w_out"][0], "wq": chunks(v["xa_wq"][0]), "wk": chunks(v["xa_wk"][0]), "wv": chunks(v["xa_wv"][0]),
        "wo": v["xa_wo"][0], "w1": chunks(v["mlp_w1"][0]), "w2": c(v["mlp_w2"][0].reshape(FF // P, P, D)),
        "pool_w": pool_w, "small": small, "conv_pw": v["conv_pw"][0],
        "cmp_k_w1": v["cmp_k_w1"][0], "cmp_k_w2": v["cmp_k_w2"][0], "cmp_v_w1": v["cmp_v_w1"][0], "cmp_v_w2": v["cmp_v_w2"][0],
        "onehot": onehot, "ident": np.eye(P, dtype=np.float32),
        "winmask": np.where((x < P) & (x <= q), np.float32(-NEG), np.float32(0)),
    }
    for g in ("mix_pre_g", "mix_post_g", "xa_pre_g", "xa_post_g", "mem_g", "mlp_pre_g", "mlp_post_g"):
        arrays[g] = c(v[g][0])
    nc = _bacc.Bacc("TRN2", target_bir_lowering=False, num_devices=1)
    aps = {k: nc.dram_tensor("in_" + k, w.shape, mybir.dt.from_np(w.dtype), kind="ExternalInput").ap() for k, w in arrays.items()}
    for k, shape in (("x1", (SEQ, D)), ("x2", (SEQ, D)), ("kmd", (P, KC, MEM)), ("vmd", (P, MT, D))):
        aps[k] = nc.dram_tensor(k, shape, F32, kind="Internal").ap()
    aps["out"] = nc.dram_tensor("out", (SEQ, D), F32, kind="ExternalOutput").ap()
    hybrid_layer(nc, aps)
    r = _run(nc, [{"in_" + k: w for k, w in arrays.items()}], core_ids=[0])
    return r.results[0]["out"].reshape(1, SEQ, D)
```
